# Optimizing a Trainium2 kernel written in Bass

```python
import jax, jax.numpy as jnp
from jax import lax
import numpy as np

D_MODEL = 1024
BATCH = 1
SEQ = 1024
DEPTH = 2

GRID_W = 64
HEAD_DIM = 64
N_HEADS = 12
N_KV_HEADS = 4
Q_GROUP = N_HEADS // N_KV_HEADS
N_FOURIER_GROUPS = 4
FOURIER_GROUP_W = 64
Q_W = N_HEADS * HEAD_DIM
KV_W = N_KV_HEADS * HEAD_DIM
F_W = N_FOURIER_GROUPS * FOURIER_GROUP_W
N_BRANCHES = 2
GATE_W = N_BRANCHES * D_MODEL
IN_W = Q_W + 2 * KV_W + F_W + GATE_W
D_FF = 4 * D_MODEL
Q_BLOCK = 128
ROPE_THETA = 10000.0
ROPE_PAIRS_PER_AXIS = HEAD_DIM // 4
EPS = 1e-6

kernel_name = "hybrid_gqa_axial_rope_fnet_gated_encoder"

def rmsnorm(x, g):
    xf = x.astype(jnp.float32)
    y = xf * lax.rsqrt(jnp.mean(xf * xf, axis=-1, keepdims=True) + EPS)
    return (y * g.astype(jnp.float32)).astype(x.dtype)

def axial_rope_tables(seq_len):
    n_rows = seq_len // GRID_W
    rows = jnp.repeat(jnp.arange(n_rows, dtype=jnp.float32), GRID_W)
    cols = jnp.tile(jnp.arange(GRID_W, dtype=jnp.float32), n_rows)
    inv_freq = ROPE_THETA ** (-jnp.arange(ROPE_PAIRS_PER_AXIS, dtype=jnp.float32) / ROPE_PAIRS_PER_AXIS)
    ang = jnp.concatenate([rows[:, None] * inv_freq[None, :],
                           cols[:, None] * inv_freq[None, :]], axis=-1)
    return jnp.cos(ang), jnp.sin(ang)

def apply_rope(x, cos, sin):
    xp = x.reshape(*x.shape[:-1], HEAD_DIM // 2, 2)
    x0, x1 = xp[..., 0], xp[..., 1]
    c = cos[None, :, None, :].astype(x.dtype)
    s = sin[None, :, None, :].astype(x.dtype)
    return jnp.stack([x0 * c - x1 * s, x0 * s + x1 * c], axis=-1).reshape(x.shape)

def blocked_gqa(q, k, v):
    B, S, _, _ = q.shape
    n_blk = S // Q_BLOCK
    scale = HEAD_DIM ** -0.5
    qg = q.reshape(B, n_blk, Q_BLOCK, N_KV_HEADS, Q_GROUP, HEAD_DIM)
    qg = jnp.transpose(qg, (1, 0, 3, 4, 2, 5))
    kt = jnp.transpose(k, (0, 2, 1, 3))
    vt = jnp.transpose(v, (0, 2, 1, 3))

    def one_block(qb):
        s = jnp.einsum('bkgqd,bksd->bkgqs', qb, kt, preferred_element_type=jnp.float32) * scale
        p = jax.nn.softmax(s, axis=-1)
        return jnp.einsum('bkgqs,bksd->bkgqd', p.astype(vt.dtype), vt)

    o = lax.map(one_block, qg)
    o = jnp.transpose(o, (1, 0, 4, 2, 3, 5))
    return o.reshape(B, S, Q_W)

def fourier_mix(f):
    B, S, _ = f.shape
    fg = f.reshape(B, S, N_FOURIER_GROUPS, FOURIER_GROUP_W).astype(jnp.float32)
    out = jnp.fft.fft2(fg, axes=(1, 3), norm="ortho").real
    return out.reshape(B, S, F_W).astype(f.dtype)

def mixer_block(h, w_in, b_gate, q_gain, k_gain, w_attn_branch, w_fourier_branch, w_out, cos, sin):
    B, S, _ = h.shape
    proj = h @ w_in
    q, k, v, f, gate_logits = jnp.split(
        proj, [Q_W, Q_W + KV_W, Q_W + 2 * KV_W, Q_W + 2 * KV_W + F_W], axis=-1)
    q = apply_rope(rmsnorm(q.reshape(B, S, N_HEADS, HEAD_DIM), q_gain), cos, sin)
    k = apply_rope(rmsnorm(k.reshape(B, S, N_KV_HEADS, HEAD_DIM), k_gain), cos, sin)
    v = v.reshape(B, S, N_KV_HEADS, HEAD_DIM)
    attn = blocked_gqa(q, k, v)
    four = fourier_mix(f)
    gates = jax.nn.sigmoid((gate_logits + b_gate).astype(jnp.float32)).astype(h.dtype)
    g_attn, g_four = jnp.split(gates, N_BRANCHES, axis=-1)
    merged = g_attn * (attn @ w_attn_branch) + g_four * (four @ w_fourier_branch)
    return merged @ w_out

def squared_relu_mlp(h, w_up, w_down):
    u = jax.nn.relu(h @ w_up)
    return (u * u) @ w_down

def setup_inputs(seed: int = 0) -> dict:
    key = jax.random.key(seed)
    ks = jax.random.split(key, 13)
    f32 = jnp.float32

    def nrm(k, shape, fan_in):
        return jax.random.normal(k, shape, f32) * (fan_in ** -0.5)

    def gain(k, shape):
        return 1.0 + 0.02 * jax.random.normal(k, shape, f32)

    return {
        "x": jax.random.normal(ks[0], (BATCH, SEQ, D_MODEL), f32),
        "norm_mix": gain(ks[1], (DEPTH, D_MODEL)),
        "w_in": nrm(ks[2], (DEPTH, D_MODEL, IN_W), D_MODEL),
        "b_gate": 0.01 * jax.random.normal(ks[3], (DEPTH, GATE_W), f32),
        "q_gain": gain(ks[4], (DEPTH, HEAD_DIM)),
        "k_gain": gain(ks[5], (DEPTH, HEAD_DIM)),
        "w_attn_branch": nrm(ks[6], (DEPTH, Q_W, D_MODEL), Q_W),
        "w_fourier_branch": nrm(ks[7], (DEPTH, F_W, D_MODEL), F_W),
        "w_out": nrm(ks[8], (DEPTH, D_MODEL, D_MODEL), D_MODEL),
        "norm_mlp": gain(ks[9], (DEPTH, D_MODEL)),
        "w_up": nrm(ks[10], (DEPTH, D_MODEL, D_FF), D_MODEL),
        "w_down": nrm(ks[11], (DEPTH, D_FF, D_MODEL), D_FF),
        "norm_final": gain(ks[12], (D_MODEL,)),
    }

def reference(x, norm_mix, w_in, b_gate, q_gain, k_gain, w_attn_branch, w_fourier_branch,
              w_out, norm_mlp, w_up, w_down, norm_final):
    cos, sin = axial_rope_tables(x.shape[1])
    for l in range(DEPTH):
        h = rmsnorm(x, norm_mix[l])
        x = x + mixer_block(h, w_in[l], b_gate[l], q_gain[l], k_gain[l], w_attn_branch[l],
                            w_fourier_branch[l], w_out[l], cos, sin)
        h = rmsnorm(x, norm_mlp[l])
        x = x + squared_relu_mlp(h, w_up[l], w_down[l])
    return rmsnorm(x, norm_final)


_drawn_inputs = setup_inputs


def setup_inputs(seed=0):
    import zlib

    import numpy as np

    out = dict(_drawn_inputs(seed))
    spreads = {}
    factors = {'norm_mix': 5.231, 'b_gate': 8.0, 'q_gain': 8.0, 'k_gain': 8.0, 'norm_final': 2.889}
    for name, (base, spread) in spreads.items():
        noise = np.random.default_rng([zlib.crc32(name.encode()), seed]).standard_normal(out[name].shape)
        drawn = base * np.exp(spread * noise) if base else spread * noise
        out[name] = __import__('jax').numpy.asarray(drawn.astype(out[name].dtype))
    for name, factor in factors.items():
        out[name] = (out[name] * factor).astype(out[name].dtype)
    return out
```

```python
from contextlib import ExitStack

import numpy as np

import concourse.bass as bass
from concourse import mybir

F32 = mybir.dt.float32
F32R = mybir.dt.float32r
ACT = mybir.ActivationFunctionType
ALU = mybir.AluOpType
AX = mybir.AxisListType

P = 128
D, SEQ, DEPTH = 1024, 1024, 2
HD, NH, NKV = 64, 12, 4
GROUP = NH // NKV
QW, KVW = NH * HD, NKV * HD
FW = 256
DFF = 4 * D
EPS = 1e-6
KB = D // P
TB = SEQ // P
NT = 512
UNIT = 2048
CHUNK = UNIT // KB
N_PROJ, N_GATE = 6, 2 * D // CHUNK
N_MERGE, N_MLP = D // CHUNK, DFF // CHUNK
U_GATE = N_PROJ
U_DFT = U_GATE + N_GATE
U_MERGE = U_DFT + 2
U_MLP = U_MERGE + 2 * N_MERGE
UNITS = U_MLP + 2 * N_MLP
HALF = SEQ // 2
QB = 256
N_TILES = NH * SEQ // QB
N_ROWS = 2 * N_TILES


def up_unit(g):
    return 2 * g - 1 if g else 0


def down_unit(g, n):
    return 2 * g + 2 if g < n - 1 else 2 * n - 1


def build(nc, t, out):
    ctx = ExitStack()
    with ctx:
        def sem(name):
            return ctx.enter_context(nc.semaphore(name))

        base = (nc.sbuf_base + 31) // 32 * 32
        plan = {}
        off = base
        for name, size in (("x", 32768), ("raw", 16384), ("w", 32768), ("a", 65536), ("b", 32768),
                           ("vf", 16384), ("tmp", 10240), ("rope", 2048), ("ident", 512),
                           ("gain", 1024), ("bgate", 128), ("small", 1536)):
            plan[name] = off
            off += size

        def at(name, shape, dt, region, byte=0):
            return nc.alloc_sbuf_tensor_at(name, [P] + shape, dt, offset=plan[region] + byte)

        x = at("x", [TB, D], F32, "x")
        raw = at("raw", [2, UNIT], F32, "raw")
        w_hi = at("w_hi", [2, UNIT], F32R, "w")
        w_lo = at("w_lo", [2, UNIT], F32R, "w", 16384)
        ht_hi = at("ht_hi", [KB, SEQ], F32R, "a")
        ht_lo = at("ht_lo", [KB, SEQ], F32R, "a", 32768)
        q_t = at("q_t", [NH, SEQ], F32R, "a")
        v_hl = at("v_hl", [TB, NKV, P], F32R, "a", 49152)
        four = at("four", [2, 2, SEQ], F32R, "a", 49152)
        k_hi = at("k_hi", [NKV, SEQ], F32R, "w")
        k_lo = at("k_lo", [NKV, SEQ], F32R, "w", 16384)
        prob = at("prob", [4, SEQ], F32, "raw")
        qs = at("qs", [2, NH, P], F32, "raw")
        ks = at("ks", [2, NKV, P], F32, "raw", 12288)
        qk = at("qk", [TB, D], F32, "b")
        vf = at("vf", [TB, NT], F32, "vf")
        pt_hi = at("pt_hi", [2, KB, QB], F32R, "b")
        pt_lo = at("pt_lo", [2, KB, QB], F32R, "b", 16384)
        u_hi = at("u_hi", [4, SEQ], F32R, "b")
        u_lo = at("u_lo", [4, SEQ], F32R, "b", 16384)
        h_row = at("h_row", [2, D], F32, "b")
        g_row = at("g_row", [D], F32, "b", 16384)
        junk = at("junk", [D], F32, "b", 20480)
        f_t = at("f_t", [2, SEQ], F32, "tmp")
        fold = at("fold", [2, 2, HALF + 2], F32, "b")
        fold_hi = at("fold_hi", [2, 2, HALF + 2], F32R, "b", 8224)
        fold_lo = at("fold_lo", [2, 2, HALF + 2], F32R, "b", 16448)
        dft64 = at("dft64", [2, P], F32, "b", 24672)
        dft64_hi = at("dft64_hi", [2, P], F32R, "b", 25696)
        dft64_lo = at("dft64_lo", [2, P], F32R, "b", 26720)
        alt_row = at("alt_row", [NT], F32, "b", 27744)
        alt_col = at("alt_col", [2], F32, "b", 29792)
        alt_col_r = at("alt_col_r", [2], F32R, "b", 29824)
        last_row = at("last_row", [2, P], F32, "b", 29856)
        gh_hi = at("gh_hi", [4, 2, 2, P], F32R, "vf")
        gh_lo = at("gh_lo", [4, 2, 2, P], F32R, "vf", 8192)
        sine = at("sine", [2, NT], F32, "b")
        gate_in = at("gate_in", [4, 2, NT], F32, "vf")
        gate_out = at("gate_out", [2, NT], F32, "tmp")
        relu = at("relu", [2, NT], F32, "tmp")
        rope_tmp = at("rope_tmp", [3, NT], F32, "tmp", 4096)
        squares = at("squares", [2, NT], F32, "tmp", 4096)
        qk_stat = at("qk_stat", [3, TB * 16], F32, "tmp", 4096 + 2048)
        v_low = at("v_low", [2, QB], F32, "tmp", 4096)
        o_sum = at("o_sum", [2, QB], F32, "tmp", 4096 + 2048)
        rope = at("rope", [TB, 2, 32], F32, "rope")
        ident = at("ident", [P], F32, "ident")
        qk_gain = at("qk_gain", [DEPTH, 2, HD], F32, "gain")
        b_gate = at("b_gate", [DEPTH, 16], F32, "bgate")
        rstd = at("rstd", [4, TB], F32, "small")
        qk_rstd = at("qk_rstd", [TB, 16], F32, "small", 128)
        top = at("top", [3, 4], F32, "small", 640)
        eps = at("eps", [1], F32, "small", 704)
        bias = at("bias", [4], F32, "small", 736)

        ps = ctx.enter_context(nc.psum_tensor("ps", [P, 8, NT], F32))
        gates = nc.dram_tensor("gates", [2, KB, P, SEQ], F32, kind="Internal").ap()

        x_loaded = [sem(f"x_loaded{i}") for i in range(TB)]
        consts_loaded = sem("consts_loaded")
        raw_loaded = [sem("raw_loaded0"), sem("raw_loaded1")]
        g_loaded = sem("g_loaded")
        dft_loaded = sem("dft_loaded")
        gate_loaded = [sem(f"gate_loaded{i}") for i in range(4)]
        gate_stored = [sem("gate_stored0"), sem("gate_stored1")]
        y_stored = [sem("y_stored0"), sem("y_stored1")]
        eps_set = sem("eps_set")
        hi_split = sem("hi_split")
        lo_split = sem("lo_split")
        first_half = sem("first_half")
        sq_summed = sem("sq_summed")
        sd_ready = sem("sd_ready")
        chain = sem("chain")
        h_ready = sem("h_ready")
        h_turned = sem("h_turned")
        ht_hi_set = sem("ht_hi_set")
        ht_lo_set = sem("ht_lo_set")
        proj_done = sem("proj_done")
        proj_kept = sem("proj_kept")
        qk_summed = sem("qk_summed")
        qk_sd = sem("qk_sd")
        qk_ready = sem("qk_ready")
        gate_done = sem("gate_done")
        gate_made = sem("gate_made")
        bias_set = sem("bias_set")
        qs_hi = sem("qs_hi")
        qs_lo = sem("qs_lo")
        turned = sem("turned")
        turn_act = sem("turn_act")
        turn_dve = sem("turn_dve")
        v_hi_set = sem("v_hi_set")
        v_lo_set = sem("v_lo_set")
        scored = sem("scored")
        topped = sem("topped")
        exped = sem("exped")
        inverted = sem("inverted")
        normed = sem("normed")
        p_turned = sem("p_turned")
        pt_hi_set = sem("pt_hi_set")
        pt_lo_set = sem("pt_lo_set")
        valued = sem("valued")
        v_low_set = sem("v_low_set")
        o_summed = sem("o_summed")
        o_hi_set = sem("o_hi_set")
        o_split = sem("o_split")
        f_turned = sem("f_turned")
        f_kept = sem("f_kept")
        dft_hi = sem("dft_hi")
        folded = sem("folded")
        fold_hi_set = sem("fold_hi_set")
        fold_lo_set = sem("fold_lo_set")
        rows_done = sem("rows_done")
        gh_hi_set = sem("gh_hi_set")
        gh_lo_set = sem("gh_lo_set")
        freq_done = sem("freq_done")
        sine_kept = sem("sine_kept")
        f_out = sem("f_out")
        four_hi_set = sem("four_hi_set")
        four_lo_set = sem("four_lo_set")
        branch_done = sem("branch_done")
        branch_used = sem("branch_used")
        gated = sem("gated")
        up_done = sem("up_done")
        relu_set = sem("relu_set")
        squared = sem("squared")
        u_hi_set = sem("u_hi_set")
        u_lo_set = sem("u_lo_set")
        down_done = sem("down_done")
        added = sem("added")

        block = ctx.enter_context(nc.Block())

        def f32(ap):
            return ap.bitcast(F32)

        TILES_UP = 4 * (N_MERGE + N_MLP)
        TILES_DOWN = 16 * (N_MERGE + N_MLP)

        def used(n):
            l, u = divmod(n, UNITS)
            if u < U_GATE:
                return (proj_done, TB * (3 * l + u // 2 + 1)) if u % 2 else (first_half, 3 * l + u // 2 + 1)
            if u < U_DFT:
                return gate_done, 4 * (N_GATE * l + u - U_GATE + 1)
            if u < U_MERGE:
                return freq_done, 5 * l + (4, 2)[u - U_DFT]
            merge = u < U_MLP
            n_steps, first = (N_MERGE, U_MERGE) if merge else (N_MLP, U_MLP)
            for g in range(n_steps):
                if u - first == up_unit(g):
                    return (branch_done, 4 * (N_MERGE * l + g + 1)) if merge else (up_done, 4 * (N_MLP * l + g + 1))
                if u - first == down_unit(g, n_steps):
                    return down_done, l * TILES_DOWN + 16 * ((0 if merge else N_MERGE) + g + 1)

        @block.sync
        def _(sp):
            for tb in range(TB):
                sp.dma_start(x[:, tb, :], t["x"][0, tb * P:(tb + 1) * P, :]).then_inc(x_loaded[tb], 16)
                if tb == 1:
                    sp.dma_start(g_row[:], t["norm_mix"][0:1, :].to_broadcast([P, D])).then_inc(g_loaded, 16)
                    sp.dma_start(ident[:], t["c_ident"]).then_inc(consts_loaded, 16)
            sp.dma_start(rope[:], t["c_rope"].rearrange("(b p) c f -> p b c f", p=P)).then_inc(consts_loaded, 16)
            for i, name in enumerate(("q_gain", "k_gain")):
                for l in range(DEPTH):
                    sp.dma_start(qk_gain[:, l, i, :], t[name][l:l + 1, :].to_broadcast([P, HD])).then_inc(consts_loaded, 16)
            for l in range(DEPTH):
                with nc.allow_non_contiguous_dma(reason="small"):
                    sp.dma_start(b_gate[:, l, :], t["b_gate"][l].rearrange("(f p) -> p f", p=P)).then_inc(consts_loaded, 16)

            def load(n, src, slot):
                sp.dma_start(raw[:, slot, :].rearrange("p (a c) -> p a c", a=src.shape[1]), src).then_inc(raw_loaded[slot], 16)

            for l in range(DEPTH):
                n0 = l * UNITS
                w_in = t["w_in"][l].rearrange("(k p) n -> p k n", p=P)
                for u in range(N_PROJ):
                    c, half = u // 2, u % 2
                    col = (QW + KVW, 0, NT)[c]
                    n = n0 + u
                    if n >= 2:
                        sp.wait_ge(lo_split, n - 1)
                    load(n, w_in[:, half * 4:half * 4 + 4, col:col + NT], u % 2)
                with sp.Fori(0, N_GATE // 2) as i:
                    for s in range(2):
                        sp.wait_ge(lo_split, i * 2 + (n0 + U_GATE + s - 1))
                        load(None, w_in[:, :, bass.ds(i * (2 * CHUNK) + (QW + 2 * KVW + FW + s * CHUNK), CHUNK)], s)
                sp.wait_ge(p_turned, 2 * N_ROWS * (l + 1))
                for s, name in enumerate(("c_cos", "c_sin")):
                    load(None, t[name].rearrange("(k p) n -> p k n", p=P), s)
                sp.wait_ge(valued, N_TILES * (l + 1))
                sp.dma_start(dft64[:], t["c_dft64"].rearrange("p (a c) -> p a c", a=2)).then_inc(dft_loaded, 16)
                sp.dma_start(alt_row[0:1, :], t["c_alt"][0:1, 0:NT]).then_inc(dft_loaded, 16)
                sp.dma_start(alt_col[:], t["c_altcol"]).then_inc(dft_loaded, 16)

                w_br = [t["w_attn_branch"][l].rearrange("(k p) n -> p k n", p=P),
                        t["w_fourier_branch"][l].rearrange("(k p) n -> p k n", p=P)]
                w_out = t["w_out"][l].rearrange("(k p) n -> p k n", p=P)
                gates_in = gates.rearrange("a f p n -> p a f n")
                order = [("up", 0)]
                for g in range(1, N_MERGE):
                    order += [("up", g), ("down", g - 1)]
                order += [("down", N_MERGE - 1)]
                for u, (kind, g) in enumerate(order):
                    n = n0 + U_MERGE + u
                    sp.wait_ge(lo_split, n - 1)
                    s = u % 2
                    if kind == "up":
                        sp.dma_start(raw[:, s, 0:6 * CHUNK].rearrange("p (a c) -> p a c", a=6),
                                     w_br[0][:, :, g * CHUNK:(g + 1) * CHUNK]).then_inc(raw_loaded[s], 16)
                        sp.dma_start(raw[:, s, 6 * CHUNK:].rearrange("p (a c) -> p a c", a=2),
                                     w_br[1][:, :, g * CHUNK:(g + 1) * CHUNK]).then_inc(raw_loaded[s], 16)
                        for i in range(4):
                            k = l * 4 * N_MERGE + 4 * g + i
                            if g == 0:
                                if i == 0:
                                    sp.wait_ge(freq_done, 5 * (l + 1))
                                    for z in range(2):
                                        sp.wait_ge(gate_stored[z], 16 * 2 * N_GATE * (l + 1))
                            else:
                                sp.wait_ge(u_lo_set, l * TILES_UP + 4 * (g - 1) + i + 1)
                            sp.dma_start(gate_in[:, i, :, :],
                                         gates_in[:, :, 2 * g + i // 2, (i % 2) * NT:(i % 2 + 1) * NT]).then_inc(gate_loaded[i], 16)
                    else:
                        load(n, w_out[:, 2 * g:2 * g + 2, :], s)
                sp.wait_ge(*used(n0 + U_MLP - 2))
                sp.dma_start(g_row[:], t["norm_mlp"][l:l + 1, :].to_broadcast([P, D])).then_inc(g_loaded, 16)

                w_up = t["w_up"][l].rearrange("(k p) n -> p k n", p=P)
                w_down = t["w_down"][l].rearrange("(k p) n -> p k n", p=P)
                m0 = n0 + U_MLP
                sp.wait_ge(lo_split, m0 - 1)
                load(m0, w_up[:, :, 0:CHUNK], 0)
                with sp.Fori(0, N_MLP // 2 - 1) as i:
                    for j, (kind, g) in enumerate((("up", 1), ("down", 0), ("up", 2), ("down", 1))):
                        sp.wait_ge(lo_split, i * 4 + (m0 + 1 + j - 1))
                        if kind == "up":
                            src = w_up[:, :, bass.ds(i * (2 * CHUNK) + g * CHUNK, CHUNK)]
                        else:
                            src = t["w_down"][l][bass.ds(i * (4 * P) + g * 2 * P, 2 * P), :].rearrange("(k p) n -> p k n", p=P)
                        load(None, src, (1 + j) % 2)
                g = N_MLP - 1
                for j, src in enumerate((w_up[:, :, g * CHUNK:(g + 1) * CHUNK], w_down[:, 2 * g - 2:2 * g, :],
                                         w_down[:, 2 * g:2 * g + 2, :])):
                    n = m0 + 2 * N_MLP - 3 + j
                    sp.wait_ge(lo_split, n - 1)
                    load(n, src, n % 2)
                sp.wait_ge(*used(n0 + UNITS - 2))
                last_gain = t["norm_mix"][l + 1:l + 2, :] if l + 1 < DEPTH else t["norm_final"].rearrange("(a d) -> a d", a=1)
                sp.dma_start(g_row[:], last_gain.to_broadcast([P, D])).then_inc(g_loaded, 16)
            for tb in range(TB):
                sp.wait_ge(h_ready, 2 * DEPTH * TB + tb + 1)
                sp.dma_start(out[0, tb * P:(tb + 1) * P, :], h_row[:, tb % 2, :]).then_inc(y_stored[tb % 2], 16)
            for z in range(2):
                sp.wait_ge(y_stored[z], 16 * TB // 2)
                sp.wait_ge(gate_stored[z], 16 * 2 * N_GATE * DEPTH)

        @block.tensor
        def _(pe):
            def three(o, stat, mov, start, stop):
                nc.tensor.matmul(o, stat[0], mov[0], start=start, stop=False)
                nc.tensor.matmul(o, stat[0], mov[1], start=False, stop=False)
                return nc.tensor.matmul(o, stat[1], mov[0], start=False, stop=stop)

            def turn_h(k, tb):
                pe.wait_ge(h_ready, TB * k + tb + 1)
                if k == 0 and tb == 0:
                    pe.wait_ge(consts_loaded, 16 * 8)
                for i in range(2):
                    if tb >= 2:
                        pe.wait_ge(ht_lo_set, 2 * (TB * k + tb - 2) + i + 1)
                    for j in range(4):
                        b = 4 * i + j
                        mm = nc.tensor.transpose(ps[:, 2 * (tb % 2) + i, j * P:(j + 1) * P],
                                                 h_row[:, tb % 2, b * P:(b + 1) * P], ident[:])
                    mm.then_inc(h_turned, 1)

            def project(l):
                for c in range(3):
                    for half in range(2):
                        n = l * UNITS + 2 * c + half
                        pe.wait_ge(lo_split, n + 1)
                        for tb in range(TB):
                            if half == 0 and c == 0:
                                if tb == 0:
                                    pe.wait_ge(ht_lo_set, 2 * TB * (2 * l + 1))
                            elif half == 0:
                                pe.wait_ge(proj_kept, TB * (3 * l + c - 1) + tb + 1)
                            for i in range(4):
                                kb = 4 * half + i
                                tok = slice(tb * P, (tb + 1) * P)
                                mm = three(ps[:, tb, :], (ht_hi[:, kb, tok], ht_lo[:, kb, tok]),
                                           (w_hi[:, half, i * NT:(i + 1) * NT], w_lo[:, half, i * NT:(i + 1) * NT]),
                                           kb == 0, kb == KB - 1)
                            if half == 1:
                                mm.then_inc(proj_done, 1)
                        if half == 0:
                            mm.then_inc(first_half, 1)

            def gate_tiles(slot, waits):
                for i in range(4):
                    fb, th = i // 2, i % 2
                    waits(i)
                    for kb in range(KB):
                        w = slice(kb * CHUNK + fb * P, kb * CHUNK + (fb + 1) * P)
                        tok = slice(th * NT, (th + 1) * NT)
                        mm = three(ps[:, i, :], (w_hi[:, slot, w], w_lo[:, slot, w]),
                                   (ht_hi[:, kb, tok], ht_lo[:, kb, tok]), kb == 0, kb == KB - 1)
                    yield mm

            def gate_stage(l):
                g0, n0 = l * 4 * N_GATE, l * UNITS + U_GATE
                pe.wait_ge(proj_kept, TB * 3 * (l + 1))
                for s in range(2):
                    pe.wait_ge(lo_split, n0 + s + 1)
                    for mm in gate_tiles(s, lambda i: s and pe.wait_ge(gate_made, g0 + i + 1)):
                        mm.then_inc(gate_done, 1)
                with pe.Fori(1, N_GATE // 2) as it:
                    for s in range(2):
                        pe.wait_ge(lo_split, it * 2 + (n0 + s + 1))
                        for mm in gate_tiles(s, lambda i: pe.wait_ge(gate_made, it * 8 + (g0 + 4 * s - 4 + i + 1))):
                            mm.then_inc(gate_done, 1)

            def turn_heads(l):
                for tb in range(TB):
                    pe.wait_ge(qs_lo, 2 * (TB * l + tb) + 2)
                    for bank in range(5):
                        if tb == 0 and bank == 0:
                            pe.wait_ge(gate_made, 4 * N_GATE * (l + 1))
                        elif tb > 0 and bank in (0, 2, 4):
                            pe.wait_ge(turn_act, 3 * (TB * l + tb - 1) + bank // 2 + 1)
                        elif tb > 0:
                            pe.wait_ge(turn_dve, 2 * (TB * l + tb - 1) + bank // 2 + 1)
                        for j in range(4):
                            src = ks[:, bank, j, :] if bank < 2 else qs[:, tb % 2, 4 * (bank - 2) + j, :]
                            mm = nc.tensor.transpose(ps[:, bank, j * P:(j + 1) * P], src, ident[:])
                        mm.then_inc(turned, 1)

            def score(l, n):
                tile, qb = n // 2, n % 2
                pair, quarter, odd = tile // 8, tile // 2 % 4, tile % 2
                head = 2 * pair + odd
                tok = quarter * QB + qb * P
                if n >= 2:
                    pe.wait_ge(exped, N_ROWS * l + n - 1)
                for kh in range(2):
                    o = ps[:, 2 * (n % 2) + kh, :]
                    keys = slice(kh * NT, (kh + 1) * NT)
                    nc.tensor.matmul(o, q_t[:, head, tok:tok + P], k_hi[:, head // GROUP, keys], start=True, stop=False)
                    mm = nc.tensor.matmul(o, q_t[:, head, tok:tok + P], k_lo[:, head // GROUP, keys], start=False, stop=True)
                mm.then_inc(scored, 1)

            def turn_probs(l, n):
                pe.wait_ge(normed, N_ROWS * l + n + 1)
                for i in range(2):
                    k = 2 * n + i
                    if k >= 3:
                        pe.wait_ge(pt_lo_set, 2 * N_ROWS * l + k - 2)
                    for j in range(4):
                        kb = 4 * i + j
                        mm = nc.tensor.transpose(ps[:, 4 + k % 3, j * P:(j + 1) * P],
                                                 prob[:, n % 4, kb * P:(kb + 1) * P], ident[:])
                    mm.then_inc(p_turned, 1)

            def value(l, tile):
                head = 2 * (tile // 8) + tile % 2
                pe.wait_ge(pt_lo_set, 2 * N_ROWS * l + 4 * (tile + 1))
                if tile == 0:
                    pe.wait_ge(v_lo_set, l + 1)
                else:
                    pe.wait_ge(o_summed, N_TILES * l + tile)
                for kb in range(KB):
                    v = v_hl[:, kb, head // GROUP, :]
                    nc.tensor.matmul(ps[:, 7, 0:QB], v, pt_hi[:, tile % 2, kb, :], start=(kb == 0), stop=False)
                    mm = nc.tensor.matmul(ps[:, 7, 0:QB], v, pt_lo[:, tile % 2, kb, :], start=False, stop=(kb == KB - 1))
                mm.then_inc(valued, 1)

            def attend(l):
                pe.wait_ge(turn_act, 3 * TB * (l + 1))
                pe.wait_ge(turn_dve, 2 * TB * (l + 1))
                score(l, 0)
                score(l, 1)
                for n in range(N_ROWS + 1):
                    if n + 2 < N_ROWS:
                        score(l, n + 2)
                    if n >= 1:
                        turn_probs(l, n - 1)
                        if n % 2 == 0 and n >= 4:
                            value(l, n // 2 - 2)
                value(l, N_TILES - 1)

            def fourier(l):
                for cb in range(2):
                    for i in range(2):
                        for j in range(4):
                            tb = 4 * i + j
                            mm = nc.tensor.transpose(ps[:, 2 * cb + i, j * P:(j + 1) * P],
                                                     vf[:, tb, FW + cb * P:FW + (cb + 1) * P], ident[:])
                        mm.then_inc(f_turned, 1)
                pe.wait_ge(dft_loaded, 48 * (l + 1))
                pe.wait_ge(folded, l + 1)
                for cb in range(2):
                    mm = nc.tensor.matmul(ps[0:1, 0, cb * P:(cb + 1) * P], fold[:, 0, cb, HALF:HALF + 1],
                                          dft64[:, 0, :], start=True, stop=True)
                mm.then_inc(rows_done, 1)
                pe.wait_ge(fold_lo_set, l + 1)
                pe.wait_ge(o_summed, N_TILES * (l + 1))
                for sb in range(4):
                    for cs in range(2):
                        for cb in range(2):
                            pos = slice(sb * P, (sb + 1) * P)
                            c0 = (2 * cs + cb) * P
                            mm = three(ps[:, 4 + sb, c0:c0 + P], (fold_hi[:, cs, cb, pos], fold_lo[:, cs, cb, pos]),
                                       (dft64_hi[:, cs, :], dft64_lo[:, cs, :]), True, True)
                    mm.then_inc(rows_done, 1)
                n0 = l * UNITS + U_DFT
                for cs in (1, 0):
                    pe.wait_ge(lo_split, n0 + cs + 1)
                    pe.wait_ge(gh_lo_set, 4 * (l + 1))
                    for cb in range(2):
                        o = ps[:, 2 * cs + cb, :]
                        for sb in range(4):
                            tab = slice(sb * NT, (sb + 1) * NT)
                            mm = three(o, (gh_hi[:, sb, cs, cb, :], gh_lo[:, sb, cs, cb, :]),
                                       (w_hi[:, cs, tab], w_lo[:, cs, tab]), sb == 0, cs == 1 and sb == 3)
                        if cs == 0:
                            mm = nc.tensor.matmul(o, last_row[0:1, cb, :], alt_row[0:1, :], start=False, stop=True)
                        mm.then_inc(freq_done, 1)
                for cb in range(2):
                    o = ps[:, 4, 2 * cb:2 * cb + 2]
                    for sb in range(4):
                        nc.tensor.matmul(o, gh_hi[:, sb, 0, cb, :], alt_col_r[:], start=(sb == 0), stop=False)
                        nc.tensor.matmul(o, gh_lo[:, sb, 0, cb, :], alt_col_r[:], start=False, stop=False)
                    mm = nc.tensor.matmul(o, last_row[0:1, cb, :], alt_col[0:1, :], start=False, stop=True)
                mm.then_inc(freq_done, 1)

            def branch(l, g):
                n = l * UNITS + U_MERGE + up_unit(g)
                s = n % 2
                pe.wait_ge(lo_split, n + 1)
                for i in range(4):
                    fb, th = i // 2, i % 2
                    k = l * 4 * N_MERGE + 4 * g + i
                    tok = slice(th * NT, (th + 1) * NT)
                    if g or i >= 2:
                        pe.wait_ge(branch_used, k - 1)
                    for kb in range(8):
                        w = slice(kb * CHUNK + fb * P, kb * CHUNK + (fb + 1) * P)
                        if kb < 6:
                            mov = (q_t[:, 2 * kb, tok], q_t[:, 2 * kb + 1, tok])
                        else:
                            mov = (four[:, 0, kb - 6, tok], four[:, 1, kb - 6, tok])
                        mm = three(ps[:, i % 2 + 2 * (kb >= 6), :], (w_hi[:, s, w], w_lo[:, s, w]), mov,
                                   kb in (0, 6), kb in (5, 7))
                    mm.then_inc(branch_done, 1)

            def up(slot, waits):
                for i in range(4):
                    fb, th = i // 2, i % 2
                    waits(i)
                    for kb in range(KB):
                        w = slice(kb * CHUNK + fb * P, kb * CHUNK + (fb + 1) * P)
                        tok = slice(th * NT, (th + 1) * NT)
                        mm = three(ps[:, i, :], (w_hi[:, slot, w], w_lo[:, slot, w]),
                                   (ht_hi[:, kb, tok], ht_lo[:, kb, tok]), kb == 0, kb == KB - 1)
                    mm.then_inc(up_done, 1)

            def down(slot, par, first, waits, after=None):
                for tb in range(TB):
                    for nh in range(2):
                        i = 2 * tb + nh
                        waits(i)
                        for j in range(2):
                            tok = slice(tb * P, (tb + 1) * P)
                            w = slice(j * D + nh * NT, j * D + (nh + 1) * NT)
                            mm = three(ps[:, 4 + i % 4, :], (u_hi[:, 2 * par + j, tok], u_lo[:, 2 * par + j, tok]),
                                       (w_hi[:, slot, w], w_lo[:, slot, w]), j == 0, j == 1)
                        mm.then_inc(down_done, 1)
                    if after:
                        after(tb)

            def norm_turns(k):
                def after(tb):
                    if tb >= 2:
                        turn_h(k, tb - 2)
                    if tb == TB - 1:
                        turn_h(k, TB - 2)
                        turn_h(k, TB - 1)
                return after

            for tb in range(TB):
                turn_h(0, tb)
            for l in range(DEPTH):
                project(l)
                gate_stage(l)
                turn_heads(l)
                attend(l)
                fourier(l)
                n0 = l * UNITS + U_MERGE
                d0 = l * TILES_DOWN
                u0 = l * TILES_UP
                pe.wait_ge(four_lo_set, l + 1)
                pe.wait_ge(o_split, N_TILES // 2 * (l + 1))

                def merge_down(g, after=None):
                    n = n0 + down_unit(g, N_MERGE)
                    pe.wait_ge(lo_split, n + 1)
                    pe.wait_ge(u_lo_set, u0 + 4 * (g + 1))
                    down(n % 2, g % 2, g == 0,
                         lambda i: (g or i >= 4) and pe.wait_ge(added, d0 + 16 * g + i - 3), after)

                branch(l, 0)
                for g in range(1, N_MERGE):
                    branch(l, g)
                    merge_down(g - 1)
                merge_down(N_MERGE - 1, norm_turns(2 * l + 1))
                n0 = l * UNITS + U_MLP
                d0 += 16 * N_MERGE
                u0 += 4 * N_MERGE
                r0 = l * 4 * N_MLP
                pe.wait_ge(ht_lo_set, 2 * TB * (2 * l + 2))

                def mlp_up(g):
                    n = n0 + up_unit(g)
                    pe.wait_ge(lo_split, n + 1)
                    up(n % 2, lambda i: g and pe.wait_ge(relu_set, r0 + 4 * (g - 1) + i + 1))

                def mlp_down(g, after=None):
                    n = n0 + down_unit(g, N_MLP)
                    pe.wait_ge(lo_split, n + 1)
                    pe.wait_ge(u_lo_set, u0 + 4 * (g + 1))
                    down(n % 2, g % 2, g == 0, lambda i: pe.wait_ge(added, d0 + 16 * g + i - 3), after)

                mlp_up(0)
                with pe.Fori(0, N_MLP // 2 - 1) as it:
                    for j in range(2):
                        pe.wait_ge(lo_split, it * 4 + (n0 + 2 * j + 2))
                        up(1, lambda i: pe.wait_ge(relu_set, it * 8 + (r0 + 4 * j + i + 1)))
                        pe.wait_ge(lo_split, it * 4 + (n0 + 2 * j + 3))
                        pe.wait_ge(u_lo_set, it * 8 + (u0 + 4 * j + 4))
                        down(0, j, False, lambda i: pe.wait_ge(added, it * 32 + (d0 + 16 * j + i - 3)))
                mlp_up(N_MLP - 1)
                mlp_down(N_MLP - 2)
                mlp_down(N_MLP - 1, norm_turns(2 * l + 2) if l + 1 < DEPTH else None)

        @block.scalar
        def _(act):
            def split_hi(n, slot):
                nc.scalar.activation(w_hi[:, slot, :], raw[:, slot, :], ACT.Copy).then_inc(hi_split, 1)

            def split(n):
                extra = sum(1 for m in merge_loads if m <= n and (m - n) % 2 == 0)
                act.wait_ge(raw_loaded[n % 2], 16 * (n // 2 + 1 + extra))
                if n % UNITS in (U_DFT, U_DFT + 1):
                    act.wait_ge(valued, N_TILES * (n // UNITS + 1))
                elif n >= 2:
                    act.wait_ge(*used(n - 2))
                split_hi(n, n % 2)

            merge_loads = [l * UNITS + U_MERGE + up_unit(g) for l in range(DEPTH) for g in range(N_MERGE)]

            def loads_before(n):
                return n // 2 + 1 + sum(1 for m in merge_loads if m <= n and (m - n) % 2 == 0)

            def norm_sums(k, tb):
                if k == 0:
                    act.wait_ge(x_loaded[tb], 16)
                else:
                    act.wait_ge(added, (k - 1) // 2 * TILES_DOWN + 16 * (N_MERGE if k % 2 else N_MERGE + N_MLP) - 14 + 2 * tb)
                if tb == 0:
                    act.wait_ge(g_loaded, 16 * (k + 1))
                if k >= 1:
                    act.wait_ge(h_ready, TB * (k - 1) + tb + 1)
                nc.scalar.activation(junk[:], x[:, tb, :], ACT.Square,
                                     accum_out=rstd[:, 0, tb:tb + 1]).then_inc(sq_summed, 1)
                act.wait_ge(sq_summed, TB * k + tb + 1)
                nc.scalar.activation(rstd[:, 1, tb:tb + 1], rstd[:, 0, tb:tb + 1], ACT.Sqrt,
                                     bias=eps[:], scale=1.0 / D).then_inc(sd_ready, 1)

            def keep_hi(k, tb):
                for i in range(2):
                    act.wait_ge(h_turned, 2 * (TB * k + tb) + i + 1)
                    nc.scalar.activation(ht_hi[:, 4 * i:4 * i + 4, tb * P:(tb + 1) * P],
                                         ps[:, 2 * (tb % 2) + i, :].rearrange("p (a c) -> p a c", a=4),
                                         ACT.Copy).then_inc(ht_hi_set, 1)

            def norm(k):
                for tb in range(TB):
                    norm_sums(k, tb)
                    if tb >= 3 and k < 2 * DEPTH:
                        keep_hi(k, tb - 3)
                if k < 2 * DEPTH:
                    for tb in range(TB - 3, TB):
                        keep_hi(k, tb)

            act.wait_ge(eps_set, 1)
            norm(0)
            split(0)
            split(1)
            for l in range(DEPTH):
                n0 = l * UNITS
                for c in range(3):
                    split(n0 + 2 * c + 2)
                    for tb in range(TB):
                        act.wait_ge(proj_done, TB * (3 * l + c) + tb + 1)
                        dst = vf[:, tb, :] if c == 0 else qk[:, tb, (c - 1) * NT:c * NT]
                        nc.scalar.activation(dst, ps[:, tb, :], ACT.Copy).then_inc(proj_kept, 1)
                    split(n0 + 2 * c + 3)
                act.wait_ge(qk_summed, 2 * TB * (l + 1))
                nc.scalar.activation(qk_stat[:, 1, :], qk_stat[:, 0, :], ACT.Sqrt, bias=eps[:],
                                     scale=1.0 / HD).then_inc(qk_sd, 1)

                def gate_unit(slot, done0, stored, bias):
                    for i in range(4):
                        act.wait_ge(gate_done, done0(i))
                        stored(i)
                        nc.scalar.activation(gate_out[:, i % 2, :], ps[:, i, :], ACT.Sigmoid,
                                             bias=bias(i)).then_inc(gate_made, 1)
                        act.wait_ge(gate_made, done0(i))
                        yield i

                gates_out = gates.rearrange("a f p n -> p (a f) n")
                g0 = l * 4 * N_GATE
                s0 = l * 2 * N_GATE
                act.wait_ge(consts_loaded, 16 * 8)
                with act.Fori(0, N_GATE // 2 - 1) as it:
                    nc.scalar.activation(bias[:], b_gate[:, l, bass.ds(it * 4, 4)], ACT.Copy).then_inc(bias_set, 1)
                    act.wait_ge(bias_set, it + (l * (N_GATE // 2 - 1) + 1))
                    for s in range(2):
                        def stored(i):
                            act.wait_ge(gate_stored[i % 2], it * 64 + 16 * (s0 + 2 * s + i // 2))
                        for i in gate_unit(s, lambda i: it * 8 + (g0 + 4 * s + i + 1), stored,
                                           lambda i: bias[:, 2 * s + i // 2:2 * s + i // 2 + 1]):
                            act.dma_start(gates_out[:, bass.ds(it * 4 + (2 * s + i // 2), 1), (i % 2) * NT:(i % 2 + 1) * NT],
                                          gate_out[:, i % 2:i % 2 + 1, :]).then_inc(gate_stored[i % 2], 16)
                        act.wait_ge(raw_loaded[s], it * 16 + 16 * loads_before(n0 + U_GATE + 2 + s))
                        act.wait_ge(gate_done, it * 8 + (g0 + 4 * s + 4))
                        split_hi(None, s)
                for s in range(2):
                    u = N_GATE - 2 + s
                    for i in gate_unit(s, lambda i: g0 + 4 * u + i + 1,
                                       lambda i: act.wait_ge(gate_stored[i % 2], 16 * (s0 + 2 * u + i // 2)),
                                       lambda i: b_gate[:, l, 2 * u + i // 2:2 * u + i // 2 + 1]):
                        fb = 2 * u + i // 2
                        act.dma_start(gates_out[:, fb:fb + 1, (i % 2) * NT:(i % 2 + 1) * NT],
                                      gate_out[:, i % 2:i % 2 + 1, :]).then_inc(gate_stored[i % 2], 16)

                def head_hi(tb):
                    act.wait_ge(qk_ready, TB * l + tb + 1)
                    if tb == 0:
                        act.wait_ge(lo_split, n0 + U_DFT)
                    if tb >= 1:
                        act.wait_ge(turned, 5 * (TB * l + tb - 1) + 2)
                    nc.scalar.activation(ks[:, 0, :, :].rearrange("p k (d c) -> p k d c", d=2).bitcast(F32R),
                                         qk[:, tb, QW:].rearrange("p (k c) -> p k c", k=NKV).unsqueeze(2).to_broadcast([P, NKV, 2, HD]),
                                         ACT.Copy).then_inc(qs_hi, 1)
                    if tb >= 2:
                        act.wait_ge(turned, 5 * (TB * l + tb - 1))
                    nc.scalar.activation(qs[:, tb % 2, :, 0:HD].bitcast(F32R),
                                         qk[:, tb, 0:QW].rearrange("p (k c) -> p k c", k=NH),
                                         ACT.Copy).then_inc(qs_hi, 1)

                head_hi(0)
                for tb in range(TB):
                    if tb + 1 < TB:
                        head_hi(tb + 1)
                    if tb == 0:
                        act.wait_ge(*used(n0 + U_DFT - 1))
                    for bank in (0, 2, 4):
                        act.wait_ge(turned, 5 * (TB * l + tb) + bank + 1)
                        dst = k_hi[:, :, tb * P:(tb + 1) * P] if bank == 0 else q_t[:, 4 * bank - 8:4 * bank - 4, tb * P:(tb + 1) * P]
                        nc.scalar.activation(dst, ps[:, bank, :].rearrange("p (a c) -> p a c", a=4),
                                             ACT.Copy).then_inc(turn_act, 1)
                nc.scalar.activation(v_hl[:, :, :, 0:HD], vf[:, :, 0:KVW].rearrange("p b (k c) -> p b k c", k=NKV),
                                     ACT.Copy).then_inc(v_hi_set, 1)

                def exp(n):
                    act.wait_ge(topped, N_ROWS * l + n + 1)
                    if n >= 4:
                        act.wait_ge(p_turned, 2 * (N_ROWS * l + n - 3))
                    nc.scalar.activation(prob[:, n % 4, :], ps[:, 2 * (n % 2):2 * (n % 2) + 2, :].rearrange("p a c -> p (a c)"),
                                         ACT.Exp, bias=top[:, 0, n % 4:n % 4 + 1],
                                         accum_out=top[:, 1, n % 4:n % 4 + 1]).then_inc(exped, 1)

                exp(0)
                for n in range(N_ROWS + 1):
                    if n + 1 < N_ROWS:
                        exp(n + 1)
                    if n >= 1:
                        m = n - 1
                        tile, qb = m // 2, m % 2
                        if tile >= 2 and qb == 0:
                            act.wait_ge(valued, N_TILES * l + tile - 1)
                        for i in range(2):
                            k = 2 * m + i
                            act.wait_ge(p_turned, 2 * N_ROWS * l + k + 1)
                            nc.scalar.activation(pt_hi[:, tile % 2, 4 * i:4 * i + 4, qb * P:(qb + 1) * P],
                                                 ps[:, 4 + k % 3, :].rearrange("p (a c) -> p a c", a=4),
                                                 ACT.Copy).then_inc(pt_hi_set, 1)
                        if n % 2 == 0 and n >= 4:
                            tile = n // 2 - 2
                            act.wait_ge(valued, N_TILES * l + tile + 1)
                            if tile >= 2:
                                act.wait_ge(o_summed, N_TILES * l + tile - 1)
                            nc.scalar.activation(v_low[0:HD, tile % 2, :], ps[HD:P, 7, 0:QB], ACT.Copy).then_inc(v_low_set, 1)
                tile = N_TILES - 1
                act.wait_ge(valued, N_TILES * l + tile + 1)
                act.wait_ge(o_summed, N_TILES * l + tile - 1)
                nc.scalar.activation(v_low[0:HD, tile % 2, :], ps[HD:P, 7, 0:QB], ACT.Copy).then_inc(v_low_set, 1)

                for cb in range(2):
                    for i in range(2):
                        act.wait_ge(f_turned, 4 * l + 2 * cb + i + 1)
                        if cb == 0 and i == 0:
                            act.wait_ge(o_split, N_TILES // 2 * (l + 1))
                            for z in range(2):
                                act.wait_ge(gate_stored[z], 16 * 2 * N_GATE * (l + 1))
                        nc.scalar.activation(f_t[:, cb, i * NT:(i + 1) * NT], ps[:, 2 * cb + i, :],
                                             ACT.Copy).then_inc(f_kept, 1)
                act.wait_ge(dft_loaded, 48 * (l + 1))
                nc.scalar.activation(dft64_hi[:], dft64[:], ACT.Copy).then_inc(dft_hi, 1)
                nc.scalar.activation(alt_col_r[:], alt_col[:], ACT.Copy).then_inc(dft_hi, 1)
                act.wait_ge(folded, l + 1)
                nc.scalar.activation(fold_hi[:], fold[:], ACT.Copy).then_inc(fold_hi_set, 1)
                split(n0 + U_DFT)
                split(n0 + U_DFT + 1)
                act.wait_ge(rows_done, 5 * l + 1)
                nc.scalar.activation(last_row[0:1, :, :], ps[0:1, 0, 0:2 * P].rearrange("p (a c) -> p a c", a=2),
                                     ACT.Copy).then_inc(gh_hi_set, 1)
                for sb in range(4):
                    act.wait_ge(rows_done, 5 * l + sb + 2)
                    nc.scalar.activation(gh_hi[:, sb].rearrange("p a b c -> p (a b c)"), ps[:, 4 + sb, :], ACT.Copy).then_inc(gh_hi_set, 1)
                for cb in range(2):
                    act.wait_ge(freq_done, 5 * l + cb + 1)
                    nc.scalar.activation(sine[:, cb, :], ps[:, 2 + cb, :], ACT.Copy).then_inc(sine_kept, 1)
                act.wait_ge(freq_done, 5 * (l + 1))
                for cb in range(2):
                    nc.scalar.activation(f_t[:, cb, HALF:HALF + 1], ps[:, 4, 2 * cb:2 * cb + 1], ACT.Copy).then_inc(sine_kept, 1)
                act.wait_ge(f_out, l + 1)
                act.wait_ge(sine_kept, 4 * (l + 1))
                nc.scalar.activation(four[:, 0], f_t[:], ACT.Copy).then_inc(four_hi_set, 1)
                split(n0 + U_MERGE)
                split(n0 + U_MERGE + 1)

                u0 = l * TILES_UP

                def merge_hi(g):
                    for i in range(4):
                        k = l * 4 * N_MERGE + 4 * g + i
                        act.wait_ge(gated, k + 1)
                        if g >= 2 and i == 0:
                            act.wait_ge(*used(n0 + U_MERGE + down_unit(g - 2, N_MERGE)))
                        nc.scalar.activation(u_hi[:, 2 * (g % 2) + i // 2, (i % 2) * NT:(i % 2 + 1) * NT],
                                             gate_in[:, i, 0, :], ACT.Copy).then_inc(u_hi_set, 1)

                merge_hi(0)
                split(n0 + U_MERGE + 2)
                for g in range(1, N_MERGE):
                    merge_hi(g)
                    split(n0 + U_MERGE + up_unit(g) + 2)
                    split(n0 + U_MERGE + up_unit(g) + 3)
                norm(2 * l + 1)
                split(n0 + U_MLP + 1)

                m0 = n0 + U_MLP
                r0 = l * 4 * N_MLP
                d0 = l * TILES_DOWN + 16 * N_MERGE

                def relu_tiles(par, val, fresh, used):
                    def hi(i):
                        act.wait_ge(squared, val(i))
                        if i == 0:
                            used()
                        nc.scalar.activation(u_hi[:, 2 * par + i // 2, (i % 2) * NT:(i % 2 + 1) * NT],
                                             squares[:, i % 2, :], ACT.Copy).then_inc(u_hi_set, 1)
                    for i in range(4):
                        act.wait_ge(up_done, val(i))
                        if not fresh or i >= 2:
                            act.wait_ge(squared, val(i - 2))
                        nc.scalar.activation(relu[:, i % 2, :], ps[:, i, :], ACT.Relu).then_inc(relu_set, 1)
                        if i:
                            hi(i - 1)
                    hi(3)

                relu_tiles(0, lambda i: r0 + i + 1, True, lambda: None)
                split(m0 + 2)
                with act.Fori(0, N_MLP // 2 - 1) as it:
                    for j in range(2):
                        relu_tiles((1 + j) % 2, lambda i: it * 8 + (r0 + 4 * (j + 1) + i + 1), False,
                                   lambda: act.wait_ge(down_done, it * 32 + (d0 + 16 * j)))
                        for s in (1, 0):
                            q = 2 * j + (3 if s else 4)
                            act.wait_ge(raw_loaded[s], it * 32 + 16 * loads_before(m0 + q))
                            if s:
                                act.wait_ge(up_done, it * 8 + (r0 + 4 * j + 8))
                            else:
                                act.wait_ge(down_done, it * 32 + (d0 + 16 * j + 16))
                            split_hi(None, s)
                g = N_MLP - 1
                relu_tiles(1, lambda i: r0 + 4 * g + i + 1, False,
                           lambda: act.wait_ge(*used(m0 + down_unit(g - 2, N_MLP))))
                split(m0 + 2 * N_MLP - 1)
                if l + 1 < DEPTH:
                    split(m0 + 2 * N_MLP)
                norm(2 * l + 2)
                if l + 1 < DEPTH:
                    split(m0 + 2 * N_MLP + 1)

        @block.vector
        def _(dve):
            step = [0]

            def link(ins):
                step[0] += 1
                ins.then_inc(chain, 1)
                dve.wait_ge(chain, step[0])

            def newton(r, sd, sq, scale, tmp):
                link(nc.vector.tensor_scalar(tmp, sq, scale, EPS, ALU.mult, ALU.add))
                link(nc.vector.reciprocal(r, sd))
                link(nc.vector.tensor_tensor(tmp, tmp, r, ALU.mult))
                link(nc.vector.tensor_tensor(tmp, tmp, r, ALU.mult))
                link(nc.vector.tensor_scalar(tmp, tmp, -0.5, 1.5, ALU.mult, ALU.add))
                link(nc.vector.tensor_tensor(r, r, tmp, ALU.mult))

            def norm_row(k, tb):
                dve.wait_ge(sd_ready, TB * k + tb + 1)
                if tb == 0:
                    dve.wait_ge(g_loaded, 16 * (k + 1))
                newton(rstd[:, 2, tb:tb + 1], rstd[:, 1, tb:tb + 1], rstd[:, 0, tb:tb + 1], 1.0 / D, rstd[:, 3, tb:tb + 1])
                if tb >= 2:
                    if k < 2 * DEPTH:
                        dve.wait_ge(h_turned, 2 * (TB * k + tb - 1))
                    else:
                        dve.wait_ge(y_stored[tb % 2], 16 * (tb // 2))
                nc.vector.scalar_tensor_tensor(out=h_row[:, tb % 2, :], in0=x[:, tb, :], scalar=rstd[:, 2, tb:tb + 1],
                                               in1=g_row[:], op0=ALU.mult, op1=ALU.mult).then_inc(h_ready, 1)

            def keep_lo(k, tb):
                for i in range(2):
                    dve.wait_ge(ht_hi_set, 2 * (TB * k + tb) + i + 1)
                    hi = ht_hi[:, 4 * i:4 * i + 4, tb * P:(tb + 1) * P]
                    nc.vector.tensor_tensor(ht_lo[:, 4 * i:4 * i + 4, tb * P:(tb + 1) * P],
                                            ps[:, 2 * (tb % 2) + i, :].rearrange("p (a c) -> p a c", a=4),
                                            f32(hi), ALU.subtract).then_inc(ht_lo_set, 1)

            def norm(k, adds):
                for tb in range(TB):
                    adds(tb)
                    if tb >= 1:
                        norm_row(k, tb - 1)
                    if tb >= 3 and k < 2 * DEPTH:
                        keep_lo(k, tb - 3)
                norm_row(k, TB - 1)
                if k < 2 * DEPTH:
                    for tb in range(TB - 3, TB):
                        keep_lo(k, tb)

            def add_tile(i, val):
                dve.wait_ge(down_done, val)
                xt = x[:, i // 2, (i % 2) * NT:(i % 2 + 1) * NT]
                nc.vector.tensor_tensor(xt, ps[:, 4 + i % 4, :], xt, ALU.add).then_inc(added, 1)

            nc.vector.memset(eps[:], EPS).then_inc(eps_set, 1)
            norm(0, lambda tb: None)
            dve.wait_ge(consts_loaded, 16 * 8)
            for l in range(DEPTH):
                link(nc.vector.tensor_scalar(qk_gain[:, l, 0, :], qk_gain[:, l, 0, :], HD ** -0.5, None, ALU.mult))
            for l in range(DEPTH):
                n0 = l * UNITS
                for c in (1, 2):
                    for tb in range(TB):
                        dve.wait_ge(proj_kept, TB * (3 * l + c) + tb + 1)
                        src = qk[:, tb, (c - 1) * NT:c * NT]
                        done = TB * (2 * l + c - 1) + tb
                        sq = rope_tmp[:, 2 * (tb % 2), :]
                        if done >= 2:
                            dve.wait_ge(qk_summed, done - 1)
                        link(nc.vector.tensor_tensor(sq, src, src, ALU.mult))
                        nc.vector.tensor_reduce(qk_stat[:, 0, tb * 16 + 8 * (c - 1):tb * 16 + 8 * c],
                                                sq.rearrange("p (h c) -> p h c", h=8), AX.X,
                                                ALU.add).then_inc(qk_summed, 1)
                dve.wait_ge(qk_sd, l + 1)
                r_all = qk_rstd[:].rearrange("p b h -> p (b h)")
                newton(r_all, qk_stat[:, 1, :], qk_stat[:, 0, :], 1.0 / HD, qk_stat[:, 2, :])
                t0, t1, t2 = (rope_tmp[:, i, :].rearrange("p (h c) -> p h c", h=16) for i in range(3))
                for tb in range(TB):
                    row = qk[:, tb, :].rearrange("p (h c) -> p h c", h=16)
                    link(nc.vector.tensor_tensor(row, row, qk_rstd[:, tb, :].unsqueeze(2).to_broadcast([P, 16, HD]), ALU.mult))
                    for i, hs in enumerate((slice(0, NH), slice(NH, 16))):
                        g = qk_gain[:, l, i, :].unsqueeze(1).to_broadcast([P, hs.stop - hs.start, HD])
                        link(nc.vector.tensor_tensor(row[:, hs, :], row[:, hs, :], g, ALU.mult))
                    if tb:
                        dve.wait_ge(qk_ready, TB * l + tb)
                    x0, x1 = row[:, :, 0:HD:2], row[:, :, 1:HD:2]
                    c, s = (rope[:, tb, i, :].unsqueeze(1).to_broadcast([P, 16, 32]) for i in range(2))
                    nc.vector.tensor_tensor(t0, x0, c, ALU.mult)
                    nc.vector.tensor_tensor(t1, x1, s, ALU.mult)
                    link(nc.vector.tensor_tensor(t2, x0, s, ALU.mult))
                    link(nc.vector.tensor_tensor(x0, t0, t1, ALU.subtract))
                    link(nc.vector.tensor_tensor(t0, x1, c, ALU.mult))
                    nc.vector.tensor_tensor(x1, t2, t0, ALU.add).then_inc(qk_ready, 1)

                def head_lo(tb):
                    dve.wait_ge(qs_hi, 2 * (TB * l + tb) + 1)
                    nc.vector.tensor_tensor(ks[:, 1].rearrange("p k (d c) -> p k d c", d=2),
                                            qk[:, tb, QW:].rearrange("p (k c) -> p k c", k=NKV).unsqueeze(2).to_broadcast([P, NKV, 2, HD]),
                                            ks[:, 0].rearrange("p k (d c) -> p k d c", d=2),
                                            ALU.subtract).then_inc(qs_lo, 1)
                    dve.wait_ge(qs_hi, 2 * (TB * l + tb) + 2)
                    nc.vector.tensor_tensor(qs[:, tb % 2, :, HD:P],
                                            qk[:, tb, 0:QW].rearrange("p (k c) -> p k c", k=NH),
                                            qs[:, tb % 2, :, 0:HD], ALU.subtract).then_inc(qs_lo, 1)

                head_lo(0)
                for tb in range(TB):
                    if tb + 1 < TB:
                        head_lo(tb + 1)
                    if tb == 0:
                        dve.wait_ge(*used(n0 + U_DFT - 1))
                    for bank in (1, 3):
                        dve.wait_ge(turned, 5 * (TB * l + tb) + bank + 1)
                        dst = k_lo[:, :, tb * P:(tb + 1) * P] if bank == 1 else q_t[:, 4:8, tb * P:(tb + 1) * P]
                        nc.vector.tensor_copy(dst, ps[:, bank, :].rearrange("p (a c) -> p a c", a=4)).then_inc(turn_dve, 1)
                dve.wait_ge(v_hi_set, l + 1)
                for tb in range(TB):
                    ins = nc.vector.tensor_tensor(v_hl[:, tb, :, HD:P], vf[:, tb, 0:KVW].rearrange("p (k c) -> p k c", k=NKV),
                                                  f32(v_hl[:, tb, :, 0:HD]), ALU.subtract)
                ins.then_inc(v_lo_set, 1)

                def top_of(n):
                    dve.wait_ge(scored, N_ROWS * l + n + 1)
                    nc.vector.tensor_reduce(top[:, 0, n % 4:n % 4 + 1], ps[:, 2 * (n % 2):2 * (n % 2) + 2, :].rearrange("p a c -> p (a c)"),
                                            AX.X, ALU.max, negate=True).then_inc(topped, 1)

                def invert(n):
                    dve.wait_ge(exped, N_ROWS * l + n + 1)
                    nc.vector.reciprocal(top[:, 2, n % 4:n % 4 + 1], top[:, 1, n % 4:n % 4 + 1]).then_inc(inverted, 1)

                def add_low(tile):
                    odd = tile % 2
                    dve.wait_ge(v_low_set, N_TILES * l + tile + 1)
                    if tile >= 4:
                        dve.wait_ge(o_split, N_TILES // 2 * l + tile // 2 - 1)
                    nc.vector.tensor_tensor(o_sum[HD * odd:HD * odd + HD, tile // 2 % 2, :], ps[0:HD, 7, 0:QB],
                                            v_low[0:HD, tile % 2, :], ALU.add).then_inc(o_summed, 1)

                top_of(0)
                top_of(1)
                invert(0)
                for n in range(N_ROWS + 1):
                    if n + 2 < N_ROWS:
                        top_of(n + 2)
                    if n + 1 < N_ROWS:
                        invert(n + 1)
                    if n >= 1:
                        m = n - 1
                        tile, qb = m // 2, m % 2
                        for i in range(2):
                            k = 2 * m + i
                            dve.wait_ge(pt_hi_set, 2 * N_ROWS * l + k + 1)
                            sl = (slice(None), tile % 2, slice(4 * i, 4 * i + 4), slice(qb * P, (qb + 1) * P))
                            nc.vector.tensor_tensor(pt_lo[sl], ps[:, 4 + k % 3, :].rearrange("p (a c) -> p a c", a=4),
                                                    f32(pt_hi[sl]), ALU.subtract).then_inc(pt_lo_set, 1)
                        if n % 2 == 0 and n >= 4:
                            add_low(n // 2 - 2)
                add_low(N_TILES - 1)

                dve.wait_ge(f_kept, 4 * (l + 1))
                dve.wait_ge(valued, N_TILES * (l + 1))
                fwd, rev = f_t[:, :, 1:HALF], f_t[:, :, SEQ - 1:HALF:-1]
                nc.vector.tensor_tensor(fold[:, 0, :, 1:HALF], fwd, rev, ALU.add)
                nc.vector.tensor_tensor(fold[:, 1, :, 1:HALF], fwd, rev, ALU.subtract)
                nc.vector.tensor_copy(fold[:, 0, :, 0:1], f_t[:, :, 0:1])
                nc.vector.tensor_copy(fold[:, 0, :, HALF:HALF + 1], f_t[:, :, HALF:HALF + 1])
                nc.vector.memset(fold[:, 0, :, HALF + 1:HALF + 2], 0.0)
                nc.vector.memset(fold[:, 1, :, 0:1], 0.0)
                nc.vector.memset(fold[:, 1, :, HALF:HALF + 2], 0.0).then_inc(folded, 1)
                dve.wait_ge(dft_hi, 2 * l + 1)
                link(nc.vector.tensor_tensor(dft64_lo[:], dft64[:], f32(dft64_hi[:]), ALU.subtract))
                dve.wait_ge(fold_hi_set, l + 1)
                nc.vector.tensor_tensor(fold_lo[:], fold[:], f32(fold_hi[:]), ALU.subtract).then_inc(fold_lo_set, 1)
                dve.wait_ge(f_turned, 4 * (l + 1))
                for sb in range(4):
                    dve.wait_ge(gh_hi_set, 5 * l + sb + 2)
                    nc.vector.tensor_tensor(gh_lo[:, sb].rearrange("p a b c -> p (a b c)"), ps[:, 4 + sb, :],
                                            f32(gh_hi[:, sb].rearrange("p a b c -> p (a b c)")), ALU.subtract).then_inc(gh_lo_set, 1)
                dve.wait_ge(sine_kept, 4 * l + 2)
                for cb in range(2):
                    dve.wait_ge(freq_done, 5 * l + 3 + cb)
                    nc.vector.tensor_tensor(f_t[:, cb, 0:HALF], ps[:, cb, :], sine[:, cb, :], ALU.subtract)
                    ins = nc.vector.tensor_tensor(f_t[:, cb, SEQ - 1:HALF:-1], ps[:, cb, 1:HALF], sine[:, cb, 1:HALF], ALU.add)
                ins.then_inc(f_out, 1)
                dve.wait_ge(four_hi_set, l + 1)
                nc.vector.tensor_tensor(four[:, 1], f_t[:], f32(four[:, 0]), ALU.subtract).then_inc(four_lo_set, 1)

                k0 = l * 4 * N_MERGE
                d0 = l * TILES_DOWN

                def merge_tiles(g):
                    def lo(i):
                        dve.wait_ge(u_hi_set, l * TILES_UP + 4 * g + i + 1)
                        sl = (slice(None), 2 * (g % 2) + i // 2, slice((i % 2) * NT, (i % 2 + 1) * NT))
                        nc.vector.tensor_tensor(u_lo[sl], gate_in[:, i, 0, :], f32(u_hi[sl]), ALU.subtract).then_inc(u_lo_set, 1)
                    for i in range(4):
                        k = k0 + 4 * g + i
                        dve.wait_ge(branch_done, k + 1)
                        dve.wait_ge(gate_loaded[i], 16 * (l * N_MERGE + g + 1))
                        nc.vector.tensor_tensor(gate_in[:, i, 0, :], ps[:, i % 2, :], gate_in[:, i, 0, :], ALU.mult)
                        ins = nc.vector.tensor_tensor(gate_in[:, i, 1, :], ps[:, 2 + i % 2, :], gate_in[:, i, 1, :], ALU.mult)
                        ins.then_inc(branch_used, 1)
                        dve.wait_ge(branch_used, k + 1)
                        nc.vector.tensor_tensor(gate_in[:, i, 0, :], gate_in[:, i, 0, :], gate_in[:, i, 1, :], ALU.add).then_inc(gated, 1)
                        if i:
                            lo(i - 1)
                    lo(3)

                merge_tiles(0)
                for g in range(1, N_MERGE):
                    merge_tiles(g)
                    for i in range(16):
                        add_tile(i, d0 + 16 * (g - 1) + i + 1)

                def last_adds(base):
                    def adds(tb):
                        add_tile(2 * tb, base + 2 * tb + 1)
                        add_tile(2 * tb + 1, base + 2 * tb + 2)
                    return adds

                norm(2 * l + 1, last_adds(d0 + 16 * (N_MERGE - 1)))

                d0 += 16 * N_MERGE
                u0 = l * TILES_UP + 4 * N_MERGE
                r0 = l * 4 * N_MLP

                def square_tiles(par, r, u):
                    def lo(i):
                        dve.wait_ge(u_hi_set, u(i))
                        sl = (slice(None), 2 * par + i // 2, slice((i % 2) * NT, (i % 2 + 1) * NT))
                        nc.vector.tensor_tensor(u_lo[sl], squares[:, i % 2, :], f32(u_hi[sl]), ALU.subtract).then_inc(u_lo_set, 1)
                    for i in range(4):
                        dve.wait_ge(relu_set, r(i))
                        dve.wait_ge(u_lo_set, u(i) - 2)
                        nc.vector.tensor_tensor(squares[:, i % 2, :], relu[:, i % 2, :], relu[:, i % 2, :], ALU.mult).then_inc(squared, 1)
                        if i:
                            lo(i - 1)
                    lo(3)

                square_tiles(0, lambda i: r0 + i + 1, lambda i: u0 + i + 1)
                with dve.Fori(0, N_MLP // 2 - 1) as it:
                    for j in range(2):
                        square_tiles((1 + j) % 2, lambda i: it * 8 + (r0 + 4 * (j + 1) + i + 1),
                                     lambda i: it * 8 + (u0 + 4 * (j + 1) + i + 1))
                        for i in range(16):
                            add_tile(i, it * 32 + (d0 + 16 * j + i + 1))
                g = N_MLP - 1
                square_tiles(1, lambda i: r0 + 4 * g + i + 1, lambda i: u0 + 4 * g + i + 1)
                for i in range(16):
                    add_tile(i, d0 + 16 * (g - 1) + i + 1)
                norm(2 * l + 2, last_adds(d0 + 16 * g))

        @block.gpsimd
        def _(pool):
            def split_lo(slot):
                nc.gpsimd.tensor_tensor(w_lo[:, slot, :], raw[:, slot, :], f32(w_hi[:, slot, :]),
                                        ALU.subtract).then_inc(lo_split, 1)

            for l in range(DEPTH):
                n0 = l * UNITS
                with pool.Fori(0, U_DFT // 2) as it:
                    for s in range(2):
                        pool.wait_ge(hi_split, it * 2 + (n0 + s + 1))
                        split_lo(s)

                def split_out(both):
                    pair, quarter = both // 4, both % 4
                    tok = slice(quarter * QB, (quarter + 1) * QB)
                    done = N_TILES // 2 * l + both + 1
                    pool.wait_ge(o_summed, 2 * done)
                    nc.gpsimd.tensor_copy(q_t[:, 2 * pair, tok], o_sum[:, both % 2, :]).then_inc(o_hi_set, 1)
                    pool.wait_ge(o_hi_set, done)
                    nc.gpsimd.tensor_tensor(q_t[:, 2 * pair + 1, tok], o_sum[:, both % 2, :],
                                            f32(q_t[:, 2 * pair, tok]), ALU.subtract).then_inc(o_split, 1)

                for n in range(N_ROWS):
                    pool.wait_ge(inverted, N_ROWS * l + n + 1)
                    nc.gpsimd.tensor_scalar(prob[:, n % 4, :], prob[:, n % 4, :], top[:, 2, n % 4:n % 4 + 1], 1.0,
                                            ALU.mult, ALU.mult).then_inc(normed, 1)
                    if n % 4 == 3 and n >= 7:
                        split_out(n // 4 - 1)
                split_out(N_TILES // 2 - 1)
                with pool.Fori(0, (UNITS - U_DFT) // 2) as it:
                    for s in range(2):
                        pool.wait_ge(hi_split, it * 2 + (n0 + U_DFT + s + 1))
                        split_lo(s)


def tables():
    pairs = HD // 4
    inv = np.float32(10000.0) ** (-np.arange(pairs, dtype=np.float32) / np.float32(pairs))
    pos = np.arange(SEQ)
    ang = np.concatenate([(pos // 64).astype(np.float32)[:, None] * inv, (pos % 64).astype(np.float32)[:, None] * inv], -1)
    rope = np.stack([np.cos(ang), np.sin(ang)], 1).astype(np.float32)
    scale = 1.0 / np.sqrt(SEQ * 64.0)
    sk = np.outer(np.arange(HALF), np.arange(HALF)) % SEQ * (2 * np.pi / SEQ)
    cc = np.outer(np.arange(64), np.arange(64)) % 64 * (2 * np.pi / 64)
    two = np.eye(2)
    return {
        "c_ident": np.eye(P, dtype=np.float32),
        "c_rope": rope,
        "c_cos": (np.cos(sk) * scale).astype(np.float32),
        "c_sin": (np.sin(sk) * scale).astype(np.float32),
        "c_dft64": np.concatenate([np.kron(two, np.cos(cc)), np.kron(two, np.sin(cc))], 1).astype(np.float32),
        "c_alt": (scale * (1.0 - 2.0 * (np.arange(NT) % 2)))[None].astype(np.float32),
        "c_altcol": (scale * (1.0 - 2.0 * (np.arange(P) % 2)))[:, None].repeat(2, 1).astype(np.float32),
    }


def kernel(**inputs):
    import concourse.bacc as bacc
    from concourse.bass_utils import run_bass_kernel_spmd

    nc = bacc.Bacc("TRN2", target_bir_lowering=False, num_devices=1)
    arrays, args = {}, {}
    for name, a in {**inputs, **tables()}.items():
        a = np.ascontiguousarray(a)
        arrays[f"in_{name}"] = a
        args[name] = nc.dram_tensor(f"in_{name}", a.shape, mybir.dt.from_np(a.dtype), kind="ExternalInput").ap()
    out = nc.dram_tensor("out_0", (1, SEQ, D), F32, kind="ExternalOutput").ap()
    build(nc, args, out)
    r = run_bass_kernel_spmd(nc, [arrays], core_ids=[0])
    return r.results[0]["out_0"]
```

```python
from contextlib import ExitStack

import numpy as np

import concourse.bass as bass
from concourse import mybir

F32 = mybir.dt.float32
F32R = mybir.dt.float32r
ACT = mybir.ActivationFunctionType
ALU = mybir.AluOpType
AX = mybir.AxisListType

P = 128
D, SEQ, DEPTH = 1024, 1024, 2
HD, NH, NKV = 64, 12, 4
GROUP = NH // NKV
QW, KVW = NH * HD, NKV * HD
FW = 256
DFF = 4 * D
EPS = 1e-6
KB = D // P
TB = SEQ // P
NT = 512
UNIT = 2048
CHUNK = UNIT // KB
N_PROJ, N_GATE = 6, 2 * D // CHUNK
N_MERGE, N_MLP = D // CHUNK, DFF // CHUNK
U_GATE = N_PROJ
U_DFT = U_GATE + N_GATE // 2
U_MERGE = U_GATE + N_GATE + 2
U_MLP = U_MERGE + 2 * N_MERGE
UNITS = U_MLP + 2 * N_MLP
HALF = SEQ // 2
QB = 256
N_TILES = NH * SEQ // QB
N_ROWS = 2 * N_TILES
FOUR_STEPS = (9, 13, 17, 21)


def gate_unit(j):
    return U_GATE + j + (2 if j >= N_GATE // 2 else 0)


def up_unit(g):
    return 2 * g - 1 if g else 0


def down_unit(g, n):
    return 2 * g + 2 if g < n - 1 else 2 * n - 1


def build(nc, t, out):
    ctx = ExitStack()
    with ctx:
        def sem(name):
            return ctx.enter_context(nc.semaphore(name))

        base = (nc.sbuf_base + 31) // 32 * 32
        plan = {}
        off = base
        for name, size in (("x", 32768), ("raw", 16384), ("w", 32768), ("a", 65536), ("b", 32768),
                           ("vf", 16384), ("tmp", 8192), ("rope", 2048), ("dft64", 2048),
                           ("ident", 512), ("gain", 1024), ("bgate", 128), ("small", 1024)):
            plan[name] = off
            off += size

        def at(name, shape, dt, region, byte=0):
            return nc.alloc_sbuf_tensor_at(name, [P] + shape, dt, offset=plan[region] + byte)

        x = at("x", [TB, D], F32, "x")
        raw = at("raw", [2, UNIT], F32, "raw")
        w_hi = at("w_hi", [2, UNIT], F32R, "w")
        w_lo = at("w_lo", [2, UNIT], F32R, "w", 16384)
        ht_hi = at("ht_hi", [KB, SEQ], F32R, "a")
        ht_lo = at("ht_lo", [KB, SEQ], F32R, "a", 32768)
        q_t = at("q_t", [NH, SEQ], F32R, "a")
        v_hl = at("v_hl", [TB, NKV, P], F32R, "a", 49152)
        four = at("four", [2, 2, SEQ], F32R, "vf")
        k_hi = at("k_hi", [NKV, SEQ], F32R, "w")
        k_lo = at("k_lo", [NKV, SEQ], F32R, "w", 16384)
        prob = at("prob", [4, SEQ], F32, "x", 16384)
        k_twice = at("k_twice", [4, NKV, P], F32, "x", 24576)
        qk = at("qk", [TB, D], F32, "b")
        vf = at("vf", [TB, NT], F32, "vf")
        pt_hi = at("pt_hi", [2, KB, QB], F32R, "b")
        pt_lo = at("pt_lo", [2, KB, QB], F32R, "b", 16384)
        u_hi = at("u_hi", [4, SEQ], F32R, "b")
        u_lo = at("u_lo", [4, SEQ], F32R, "b", 16384)
        h_row = at("h_row", [2, D], F32, "b")
        g_row = at("g_row", [D], F32, "b", 16384)
        junk = at("junk", [D], F32, "b", 20480)
        f_t = at("f_t", [2, SEQ], F32, "x")
        fold = at("fold", [2, 2, HALF], F32, "x", 8192)
        fold_hi = at("fold_hi", [2, 2, HALF], F32R, "x", 16384)
        fold_lo = at("fold_lo", [2, 2, HALF], F32R, "x", 24576)
        gh_hi = at("gh_hi", [4, 2, 2, P], F32R, "x")
        gh_lo = at("gh_lo", [4, 2, 2, P], F32R, "x", 8192)
        cosine = at("cosine", [2, NT], F32, "x", 16384)
        f_out = at("f_out", [2, SEQ], F32, "x")
        dft64 = at("dft64", [2, P], F32, "b", 24576)
        dft64_hi = at("dft64_hi", [2, P], F32R, "dft64")
        dft64_lo = at("dft64_lo", [2, P], F32R, "dft64", 1024)
        alt_row = vf[0:1, 0:2, FW:]
        last_row = vf[0:1, 2, FW:]
        gate_in = at("gate_in", [4, 2, NT], F32, "a", 49152)
        gate_out = at("gate_out", [2, NT], F32, "tmp")
        relu = at("relu", [2, NT], F32, "tmp")
        rope_tmp = at("rope_tmp", [2, NT], F32, "tmp", 4096)
        squares = at("squares", [2, NT], F32, "tmp", 4096)
        qk_stat = at("qk_stat", [3, TB * 16], F32, "tmp", 6144)
        v_low = at("v_low", [2, QB], F32, "tmp", 4096)
        o_sum = at("o_sum", [2, QB], F32, "tmp", 6144)
        rope = at("rope", [TB, 2, 32], F32, "rope")
        ident = at("ident", [P], F32, "ident")
        qk_gain = at("qk_gain", [DEPTH, 2, HD], F32, "gain")
        b_gate = at("b_gate", [DEPTH, 16], F32, "bgate")
        rstd = at("rstd", [4, TB], F32, "small")
        qk_rstd = at("qk_rstd", [TB, 16], F32, "small", 128)
        top = at("top", [3, 4], F32, "small", 640)
        eps = at("eps", [1], F32, "small", 704)
        alt_col = at("alt_col", [2], F32, "small", 736)
        alt_col_r = at("alt_col_r", [2], F32R, "small", 768)
        mid = at("mid", [2], F32, "small", 800)
        mid_out = at("mid_out", [2], F32, "small", 832)

        ps = ctx.enter_context(nc.psum_tensor("ps", [P, 8, NT], F32))
        x_park = nc.dram_tensor("x_park", [SEQ, D], F32, kind="Internal").ap()
        gates = nc.dram_tensor("gates", [2, KB, P, SEQ], F32, kind="Internal").ap()

        x_loaded = [sem(f"x_loaded{i}") for i in range(TB)]
        x_parked = sem("x_parked")
        ident_loaded = sem("ident_loaded")
        consts_loaded = sem("consts_loaded")
        raw_loaded = [sem("raw_loaded0"), sem("raw_loaded1")]
        g_loaded = sem("g_loaded")
        dft_loaded = sem("dft_loaded")
        gate_loaded = [sem(f"gate_loaded{i}") for i in range(4)]
        gate_stored = [sem("gate_stored0"), sem("gate_stored1")]
        y_stored = [sem("y_stored0"), sem("y_stored1")]
        eps_set = sem("eps_set")
        hi_split = sem("hi_split")
        lo_split = sem("lo_split")
        first_half = sem("first_half")
        sq_summed = sem("sq_summed")
        sd_ready = sem("sd_ready")
        inv_ready = sem("inv_ready")
        newton_step = sem("newton_step")
        rstd_ready = sem("rstd_ready")
        chain = sem("chain")
        h_ready = sem("h_ready")
        h_turned = sem("h_turned")
        ht_hi_set = sem("ht_hi_set")
        ht_lo_set = sem("ht_lo_set")
        proj_done = sem("proj_done")
        proj_kept = sem("proj_kept")
        qk_summed = sem("qk_summed")
        qk_sd = sem("qk_sd")
        qk_ready = sem("qk_ready")
        gate_done = sem("gate_done")
        gate_made = sem("gate_made")
        k_doubled = sem("k_doubled")
        turned = sem("turned")
        turn_act = sem("turn_act")
        turn_dve = sem("turn_dve")
        v_hi_set = sem("v_hi_set")
        v_lo_set = sem("v_lo_set")
        scored = sem("scored")
        topped = sem("topped")
        exped = sem("exped")
        inverted = sem("inverted")
        normed = sem("normed")
        p_turned = sem("p_turned")
        pt_hi_set = sem("pt_hi_set")
        pt_lo_set = sem("pt_lo_set")
        valued = sem("valued")
        v_low_set = sem("v_low_set")
        o_summed = sem("o_summed")
        o_hi_set = sem("o_hi_set")
        o_split = sem("o_split")
        f_turned = sem("f_turned")
        f_kept = sem("f_kept")
        dft_hi = sem("dft_hi")
        dft_lo = sem("dft_lo")
        folded = sem("folded")
        fold_hi_set = sem("fold_hi_set")
        fold_lo_set = sem("fold_lo_set")
        rows_done = sem("rows_done")
        gh_hi_set = sem("gh_hi_set")
        gh_lo_set = sem("gh_lo_set")
        freq_done = sem("freq_done")
        cosine_kept = sem("cosine_kept")
        f_made = sem("f_made")
        four_hi_set = sem("four_hi_set")
        four_set = sem("four_set")
        branch_done = sem("branch_done")
        branch_used = sem("branch_used")
        gated = sem("gated")
        up_done = sem("up_done")
        relu_set = sem("relu_set")
        squared = sem("squared")
        u_hi_set = sem("u_hi_set")
        u_lo_set = sem("u_lo_set")
        down_done = sem("down_done")
        added = sem("added")

        block = ctx.enter_context(nc.Block())

        def f32(ap):
            return ap.bitcast(F32)

        def turn_parts(tb, part):
            tok = slice(tb * P, (tb + 1) * P)
            if part == 0:
                return (k_hi[:, :, tok], k_lo[:, :, tok]), ps[:, 4 * (tb % 2), :].rearrange("p (a c) -> p a c", a=NKV)
            here, other = (slice(0, HD), slice(HD, P))[::3 - 2 * part]
            pairs = ps[here, 4 * (tb % 2) + 1:4 * (tb % 2) + 3, :].rearrange("p b (a c) -> p (b a) c", a=4)
            return (q_t[here, part - 1::2, tok], q_t[other, part - 1::2, tok]), pairs[:, 0:NH // 2, :]

        TILES_UP = 4 * (N_MERGE + N_MLP)
        TILES_DOWN = 16 * (N_MERGE + N_MLP)

        def used(n):
            l, u = divmod(n, UNITS)
            if u < U_GATE:
                return (proj_done, TB * (3 * l + u // 2 + 1)) if u % 2 else (first_half, 3 * l + u // 2 + 1)
            if u in (U_DFT, U_DFT + 1):
                return freq_done, 5 * l + (3, 5)[u - U_DFT]
            if u < U_MERGE:
                return gate_done, 4 * (N_GATE * l + u - U_GATE + 1 - (2 if u > U_DFT else 0))
            merge = u < U_MLP
            n_steps, first = (N_MERGE, U_MERGE) if merge else (N_MLP, U_MLP)
            for g in range(n_steps):
                if u - first == up_unit(g):
                    return (branch_done, 4 * (N_MERGE * l + g + 1)) if merge else (up_done, 4 * (N_MLP * l + g + 1))
                if u - first == down_unit(g, n_steps):
                    return down_done, l * TILES_DOWN + 16 * ((0 if merge else N_MERGE) + g + 1)

        @block.sync
        def _(sp):
            def load(n, src, slot):
                sp.dma_start(raw[:, slot, :].rearrange("p (a c) -> p a c", a=src.shape[1]), src).then_inc(raw_loaded[slot], 16)

            def w_proj(l, u):
                c, half = u // 2, u % 2
                col = (QW + KVW, 0, NT)[c]
                return t["w_in"][l].rearrange("(k p) n -> p k n", p=P)[:, half * 4:half * 4 + 4, col:col + NT]

            for tb in range(TB):
                sp.dma_start(x[:, tb, :], t["x"][0, tb * P:(tb + 1) * P, :]).then_inc(x_loaded[tb], 16)
                if tb == 0:
                    sp.dma_start(g_row[:], t["norm_mix"][0:1, :].to_broadcast([P, D])).then_inc(g_loaded, 16)
                    sp.dma_start(ident[:], t["c_ident"]).then_inc(ident_loaded, 16)
                if tb in (1, 5):
                    load(tb // 4, w_proj(0, tb // 4), tb // 4)
            sp.dma_start(dft64[:], t["c_dft64"].rearrange("p (a c) -> p a c", a=2)).then_inc(dft_loaded, 16)
            sp.dma_start(alt_col[:], t["c_altcol"]).then_inc(dft_loaded, 16)
            sp.dma_start(rope[:], t["c_rope"].rearrange("(b p) c f -> p b c f", p=P)).then_inc(consts_loaded, 16)
            for i, name in enumerate(("q_gain", "k_gain")):
                for l in range(DEPTH):
                    sp.dma_start(qk_gain[:, l, i, :], t[name][l:l + 1, :].to_broadcast([P, HD])).then_inc(consts_loaded, 16)
            for l in range(DEPTH):
                with nc.allow_non_contiguous_dma(reason="small"):
                    sp.dma_start(b_gate[:, l, :], t["b_gate"][l].rearrange("(f p) -> p f", p=P)).then_inc(consts_loaded, 16)

            for l in range(DEPTH):
                n0 = l * UNITS
                w_in = t["w_in"][l].rearrange("(k p) n -> p k n", p=P)
                for u in range(N_PROJ):
                    n = n0 + u
                    if u == 2 and l:
                        for tb in range(TB):
                            sp.wait_ge(added, l * TILES_DOWN - 14 + 2 * tb)
                            sp.dma_start(x_park[tb * P:(tb + 1) * P, :], x[:, tb, :]).then_inc(x_parked, 16)
                    if n >= 2:
                        sp.wait_ge(lo_split, n - 1)
                        load(n, w_proj(l, u), u % 2)
                for half in range(2):
                    with sp.Fori(0, N_GATE // 4) as i:
                        for s in range(2):
                            sp.wait_ge(lo_split, i * 2 + (n0 + gate_unit(half * (N_GATE // 2)) + s - 1))
                            load(None, w_in[:, :, bass.ds(i * (2 * CHUNK) + (QW + 2 * KVW + FW + (half * (N_GATE // 2) + s) * CHUNK), CHUNK)], s)
                    if half == 0:
                        sp.wait_ge(f_turned, 4 * (l + 1))
                        sp.dma_start(alt_row, t["c_alt"].rearrange("a (b c) -> a b c", b=2)).then_inc(dft_loaded, 16)
                        for s, name in enumerate(("c_cos", "c_sin")):
                            sp.wait_ge(lo_split, n0 + U_DFT + s - 1)
                            load(None, t[name].rearrange("(k p) n -> p k n", p=P), s)

                w_br = [t["w_attn_branch"][l].rearrange("(k p) n -> p k n", p=P),
                        t["w_fourier_branch"][l].rearrange("(k p) n -> p k n", p=P)]
                w_out = t["w_out"][l].rearrange("(k p) n -> p k n", p=P)
                gates_in = gates.rearrange("a f p n -> p a f n")
                order = [("up", 0)]
                for g in range(1, N_MERGE):
                    order += [("up", g), ("down", g - 1)]
                order += [("down", N_MERGE - 1)]
                for u, (kind, g) in enumerate(order):
                    n = n0 + U_MERGE + u
                    sp.wait_ge(lo_split, n - 1)
                    s = u % 2
                    if kind == "up":
                        sp.dma_start(raw[:, s, 0:6 * CHUNK].rearrange("p (a c) -> p a c", a=6),
                                     w_br[0][:, :, g * CHUNK:(g + 1) * CHUNK]).then_inc(raw_loaded[s], 16)
                        sp.dma_start(raw[:, s, 6 * CHUNK:].rearrange("p (a c) -> p a c", a=2),
                                     w_br[1][:, :, g * CHUNK:(g + 1) * CHUNK]).then_inc(raw_loaded[s], 16)
                        for i in range(4):
                            k = l * 4 * N_MERGE + 4 * g + i
                            if g == 0:
                                if i == 0:
                                    sp.wait_ge(valued, N_TILES * (l + 1))
                                    for z in range(2):
                                        sp.wait_ge(gate_stored[z], 16 * 2 * N_GATE * (l + 1))
                            else:
                                sp.wait_ge(u_lo_set, l * TILES_UP + 4 * (g - 1) + i + 1)
                            sp.dma_start(gate_in[:, i, :, :],
                                         gates_in[:, :, 2 * g + i // 2, (i % 2) * NT:(i % 2 + 1) * NT]).then_inc(gate_loaded[i], 16)
                    else:
                        load(n, w_out[:, 2 * g:2 * g + 2, :], s)
                    if u == 2:
                        sp.wait_ge(p_turned, 2 * N_ROWS * (l + 1))
                        sp.wait_ge(four_set, 4 * (l + 1))
                        for tb in range(TB):
                            src = t["x"][0, tb * P:(tb + 1) * P, :] if l == 0 else x_park[tb * P:(tb + 1) * P, :]
                            sp.dma_start(x[:, tb, :], src).then_inc(x_loaded[tb], 16)
                sp.wait_ge(*used(n0 + U_MLP - 2))
                sp.dma_start(g_row[:], t["norm_mlp"][l:l + 1, :].to_broadcast([P, D])).then_inc(g_loaded, 16)

                w_up = t["w_up"][l].rearrange("(k p) n -> p k n", p=P)
                w_down = t["w_down"][l].rearrange("(k p) n -> p k n", p=P)
                m0 = n0 + U_MLP
                sp.wait_ge(lo_split, m0 - 1)
                load(m0, w_up[:, :, 0:CHUNK], 0)
                with sp.Fori(0, N_MLP // 2 - 1) as i:
                    for j, (kind, g) in enumerate((("up", 1), ("down", 0), ("up", 2), ("down", 1))):
                        sp.wait_ge(lo_split, i * 4 + (m0 + 1 + j - 1))
                        if kind == "up":
                            src = w_up[:, :, bass.ds(i * (2 * CHUNK) + g * CHUNK, CHUNK)]
                        else:
                            src = t["w_down"][l][bass.ds(i * (4 * P) + g * 2 * P, 2 * P), :].rearrange("(k p) n -> p k n", p=P)
                        load(None, src, (1 + j) % 2)
                g = N_MLP - 1
                for j, src in enumerate((w_up[:, :, g * CHUNK:(g + 1) * CHUNK], w_down[:, 2 * g - 2:2 * g, :],
                                         w_down[:, 2 * g:2 * g + 2, :])):
                    n = m0 + 2 * N_MLP - 3 + j
                    sp.wait_ge(lo_split, n - 1)
                    load(n, src, n % 2)
                sp.wait_ge(*used(n0 + UNITS - 2))
                last_gain = t["norm_mix"][l + 1:l + 2, :] if l + 1 < DEPTH else t["norm_final"].rearrange("(a d) -> a d", a=1)
                sp.dma_start(g_row[:], last_gain.to_broadcast([P, D])).then_inc(g_loaded, 16)
            for tb in range(TB):
                sp.wait_ge(h_ready, 2 * DEPTH * TB + tb + 1)
                sp.dma_start(out[0, tb * P:(tb + 1) * P, :], h_row[:, tb % 2, :]).then_inc(y_stored[tb % 2], 16)
            for z in range(2):
                sp.wait_ge(y_stored[z], 16 * TB // 2)
                sp.wait_ge(gate_stored[z], 16 * 2 * N_GATE * DEPTH)

        @block.tensor
        def _(pe):
            def three(o, stat, mov, start, stop):
                nc.tensor.matmul(o, stat[0], mov[0], start=start, stop=False)
                nc.tensor.matmul(o, stat[0], mov[1], start=False, stop=False)
                return nc.tensor.matmul(o, stat[1], mov[0], start=False, stop=stop)

            def turn_h(k, tb):
                pe.wait_ge(h_ready, TB * k + tb + 1)
                if k == 0 and tb == 0:
                    pe.wait_ge(ident_loaded, 16)
                for i in range(2):
                    if tb >= 2:
                        pe.wait_ge(ht_lo_set, 2 * (TB * k + tb - 2) + i + 1)
                    for j in range(4):
                        b = 4 * i + j
                        mm = nc.tensor.transpose(ps[:, 2 * (tb % 2) + i, j * P:(j + 1) * P],
                                                 h_row[:, tb % 2, b * P:(b + 1) * P], ident[:])
                    mm.then_inc(h_turned, 1)

            def project_tile(l, c, half, tb):
                bank = (tb + 4) % TB
                if half == 0 and c == 0:
                    if l and tb < 4:
                        pe.wait_ge(added, l * TILES_DOWN - 3 + tb)
                    pe.wait_ge(ht_lo_set, 2 * (2 * TB * l + tb + 1))
                    if tb == 4:
                        pe.wait_ge(ht_lo_set, 2 * TB * (2 * l + 1))
                elif half == 0:
                    pe.wait_ge(proj_kept, TB * (3 * l + c - 1) + tb + 1)
                for i in range(4):
                    kb = 4 * half + i
                    tok = slice(tb * P, (tb + 1) * P)
                    mm = three(ps[:, bank, :], (ht_hi[:, kb, tok], ht_lo[:, kb, tok]),
                               (w_hi[:, half, i * NT:(i + 1) * NT], w_lo[:, half, i * NT:(i + 1) * NT]),
                               kb == 0, kb == KB - 1)
                if half == 1:
                    mm.then_inc(proj_done, 1)
                elif tb == TB - 1:
                    mm.then_inc(first_half, 1)

            def project(l):
                for c in range(3):
                    for half in range(2):
                        if (c, half) != (0, 0):
                            pe.wait_ge(lo_split, l * UNITS + 2 * c + half + 1)
                        for tb in range(0 if (c, half) != (0, 0) else 4, TB):
                            project_tile(l, c, half, tb)

            def gate_tiles(slot, waits):
                for i in range(4):
                    fb, th = i // 2, i % 2
                    waits(i)
                    for kb in range(KB):
                        w = slice(kb * CHUNK + fb * P, kb * CHUNK + (fb + 1) * P)
                        tok = slice(th * NT, (th + 1) * NT)
                        mm = three(ps[:, i, :], (w_hi[:, slot, w], w_lo[:, slot, w]),
                                   (ht_hi[:, kb, tok], ht_lo[:, kb, tok]), kb == 0, kb == KB - 1)
                    yield mm

            def gate_pair(l, pair, waits):
                for s in range(2):
                    n = l * UNITS + U_GATE + s + 1 + (2 if not isinstance(pair, int) or pair >= 2 else 0)
                    pe.wait_ge(lo_split, pair * 2 + n)
                    for mm in gate_tiles(s, lambda i: waits(s, i)):
                        mm.then_inc(gate_done, 1)

            def gate_stage(l):
                g0 = l * 4 * N_GATE
                k0 = TB * (3 * l + 2)

                def bank_read(s, i):
                    if s == 0:
                        pe.wait_ge(proj_kept, k0 + 4 + i + 1)
                    else:
                        pe.wait_ge(gate_made, g0 + i + 1)

                fourier_turn(l)
                gate_pair(l, 0, bank_read)
                fourier_rows(l)
                gate_pair(l, 1, lambda s, i: pe.wait_ge(gate_made, g0 + 8 + 4 * s - 4 + i + 1))
                fourier_freq(l)
                with pe.Fori(2, N_GATE // 2) as pair:
                    gate_pair(l, pair, lambda s, i: pe.wait_ge(gate_made, pair * 8 + (g0 + 4 * s - 4 + i + 1)))

            def turn_heads(l):
                for tb in range(TB):
                    pe.wait_ge(k_doubled, TB * l + tb + 1)
                    if tb == 0:
                        pe.wait_ge(gate_made, 4 * N_GATE * (l + 1))
                    elif tb == 1:
                        pe.wait_ge(f_made, l + 1)
                    else:
                        pe.wait_ge(turn_dve, 3 * (TB * l + tb - 1))
                    for j in range(4 + NH // 2):
                        if j < 4:
                            src = k_twice[:, tb % 4, j, :]
                        else:
                            src = qk[:, tb, (j - 4) * P:(j - 3) * P]
                        mm = nc.tensor.transpose(ps[:, 4 * (tb % 2) + j // 4, j % 4 * P:(j % 4 + 1) * P], src, ident[:])
                        if j in (3, 9):
                            mm.then_inc(turned, 1)

            def score(l, n):
                tile, qb = n // 2, n % 2
                pair, quarter, odd = tile // 8, tile // 2 % 4, tile % 2
                head = 2 * pair + odd
                tok = quarter * QB + qb * P
                if n >= 2:
                    pe.wait_ge(exped, N_ROWS * l + n - 1)
                for kh in range(2):
                    o = ps[:, 2 * (n % 2) + kh, :]
                    keys = slice(kh * NT, (kh + 1) * NT)
                    nc.tensor.matmul(o, q_t[:, head, tok:tok + P], k_hi[:, head // GROUP, keys], start=True, stop=False)
                    mm = nc.tensor.matmul(o, q_t[:, head, tok:tok + P], k_lo[:, head // GROUP, keys], start=False, stop=True)
                mm.then_inc(scored, 1)

            def turn_probs(l, n):
                pe.wait_ge(normed, N_ROWS * l + n + 1)
                for i in range(2):
                    k = 2 * n + i
                    if k >= 3:
                        pe.wait_ge(pt_lo_set, 2 * N_ROWS * l + k - 2)
                    for j in range(4):
                        kb = 4 * i + j
                        mm = nc.tensor.transpose(ps[:, 4 + k % 3, j * P:(j + 1) * P],
                                                 prob[:, n % 4, kb * P:(kb + 1) * P], ident[:])
                    mm.then_inc(p_turned, 1)

            def value(l, tile):
                head = 2 * (tile // 8) + tile % 2
                pe.wait_ge(pt_lo_set, 2 * N_ROWS * l + 4 * (tile + 1))
                if tile == 0:
                    pe.wait_ge(v_lo_set, TB * (l + 1))
                else:
                    pe.wait_ge(o_summed, N_TILES * l + tile)
                for kb in range(KB):
                    v = v_hl[:, kb, head // GROUP, :]
                    nc.tensor.matmul(ps[:, 7, 0:QB], v, pt_hi[:, tile % 2, kb, :], start=(kb == 0), stop=False)
                    mm = nc.tensor.matmul(ps[:, 7, 0:QB], v, pt_lo[:, tile % 2, kb, :], start=False, stop=(kb == KB - 1))
                mm.then_inc(valued, 1)

            def attend(l):
                pe.wait_ge(turn_dve, 3 * TB * (l + 1))
                score(l, 0)
                score(l, 1)
                for n in range(N_ROWS + 1):
                    if n + 2 < N_ROWS:
                        score(l, n + 2)
                    if n >= 1:
                        turn_probs(l, n - 1)
                        if n % 2 == 0 and n >= 4:
                            value(l, n // 2 - 2)
                value(l, N_TILES - 1)

            def fourier_turn(l):
                pe.wait_ge(proj_kept, TB * (3 * l + 2) + 4)
                for cb in range(2):
                    for i in range(2):
                        for j in range(4):
                            tb = 4 * i + j
                            mm = nc.tensor.transpose(ps[:, 4 + 2 * cb + i, j * P:(j + 1) * P],
                                                     vf[:, tb, FW + cb * P:FW + (cb + 1) * P], ident[:])
                        mm.then_inc(f_turned, 1)

            def fourier_rows(l):
                pe.wait_ge(dft_lo, 1)
                pe.wait_ge(fold_lo_set, l + 1)
                for cb in range(2):
                    o = ps[0:1, 7, cb * P:(cb + 1) * P]
                    nc.tensor.matmul(o, mid[:, cb:cb + 1], f32(dft64_hi[:, 0, :]), start=True, stop=False)
                    mm = nc.tensor.matmul(o, mid[:, cb:cb + 1], f32(dft64_lo[:, 0, :]), start=False, stop=True)
                mm.then_inc(rows_done, 1)
                for sb in range(4):
                    if sb == 3:
                        pe.wait_ge(gh_hi_set, 5 * l + 1)
                    for cs in range(2):
                        for cb in range(2):
                            pos = slice(sb * P, (sb + 1) * P)
                            c0 = (2 * cs + cb) * P
                            mm = three(ps[:, 4 + sb, c0:c0 + P], (fold_hi[:, cs, cb, pos], fold_lo[:, cs, cb, pos]),
                                       (dft64_hi[:, cs, :], dft64_lo[:, cs, :]), True, True)
                    mm.then_inc(rows_done, 1)

            def fourier_freq(l):
                n0 = l * UNITS + U_DFT
                pe.wait_ge(gh_lo_set, 4 * (l + 1))
                pe.wait_ge(dft_loaded, 32 + 16 * (l + 1))
                for cb in range(2):
                    o = ps[:, 6, 2 * cb:2 * cb + 2]
                    for sb in range(4):
                        nc.tensor.matmul(o, gh_hi[:, sb, 0, cb, :], alt_col_r[:], start=(sb == 0), stop=False)
                        nc.tensor.matmul(o, gh_lo[:, sb, 0, cb, :], alt_col_r[:], start=False, stop=False)
                    mm = nc.tensor.matmul(o, last_row[:, cb * P:(cb + 1) * P], alt_col[0:1, :], start=False, stop=True)
                mm.then_inc(freq_done, 1)
                for cs in range(2):
                    pe.wait_ge(lo_split, n0 + cs + 1)
                    if cs == 1:
                        pe.wait_ge(cosine_kept, 3 * l + 1)
                    for cb in range(2):
                        o = ps[:, 4 + 2 * cs + cb, :]
                        for sb in range(4):
                            tab = slice(sb * NT, (sb + 1) * NT)
                            mm = three(o, (gh_hi[:, sb, cs, cb, :], gh_lo[:, sb, cs, cb, :]),
                                       (w_hi[:, cs, tab], w_lo[:, cs, tab]), sb == 0, cs == 1 and sb == 3)
                        if cs == 0:
                            mm = nc.tensor.matmul(o.rearrange("p (b c) -> p b c", b=2), last_row[:, cb * P:(cb + 1) * P],
                                                  alt_row, start=False, stop=True)
                        mm.then_inc(freq_done, 1)

            def branch(l, g):
                n = l * UNITS + U_MERGE + up_unit(g)
                s = n % 2
                pe.wait_ge(lo_split, n + 1)
                for i in range(4):
                    fb, th = i // 2, i % 2
                    k = l * 4 * N_MERGE + 4 * g + i
                    tok = slice(th * NT, (th + 1) * NT)
                    if g or i >= 2:
                        pe.wait_ge(branch_used, k - 1)
                    for kb in (6, 7, 0, 1, 2, 3, 4, 5):
                        if g == 0 and i == 0 and kb == 5:
                            pe.wait_ge(o_split, N_TILES // 2 * (l + 1))
                        w = slice(kb * CHUNK + fb * P, kb * CHUNK + (fb + 1) * P)
                        if kb < 6:
                            mov = (q_t[:, 2 * kb, tok], q_t[:, 2 * kb + 1, tok])
                        else:
                            mov = (four[:, 0, kb - 6, tok], four[:, 1, kb - 6, tok])
                        mm = three(ps[:, i % 2 + 2 * (kb >= 6), :], (w_hi[:, s, w], w_lo[:, s, w]), mov,
                                   kb in (0, 6), kb in (5, 7))
                    mm.then_inc(branch_done, 1)

            def up(slot, waits):
                for i in range(4):
                    fb, th = i // 2, i % 2
                    waits(i)
                    for kb in range(KB):
                        w = slice(kb * CHUNK + fb * P, kb * CHUNK + (fb + 1) * P)
                        tok = slice(th * NT, (th + 1) * NT)
                        mm = three(ps[:, i, :], (w_hi[:, slot, w], w_lo[:, slot, w]),
                                   (ht_hi[:, kb, tok], ht_lo[:, kb, tok]), kb == 0, kb == KB - 1)
                    mm.then_inc(up_done, 1)

            def down(slot, par, first, waits, after=None):
                for tb in range(TB):
                    for nh in range(2):
                        i = 2 * tb + nh
                        waits(i)
                        for j in range(2):
                            tok = slice(tb * P, (tb + 1) * P)
                            w = slice(j * D + nh * NT, j * D + (nh + 1) * NT)
                            mm = three(ps[:, 4 + i % 4, :], (u_hi[:, 2 * par + j, tok], u_lo[:, 2 * par + j, tok]),
                                       (w_hi[:, slot, w], w_lo[:, slot, w]), j == 0, j == 1)
                        mm.then_inc(down_done, 1)
                    if after:
                        after(tb)

            def norm_turns(k):
                def after(tb):
                    if tb >= 3:
                        turn_h(k, tb - 3)
                return after

            for tb in range(4):
                turn_h(0, tb)
            for l in range(DEPTH):
                for tb in range(4):
                    if tb or l == 0:
                        turn_h(2 * l, 4 + tb)
                    if tb == 0:
                        pe.wait_ge(lo_split, l * UNITS + 1)
                    project_tile(l, 0, 0, tb)
                project(l)
                gate_stage(l)
                turn_heads(l)
                attend(l)
                n0 = l * UNITS + U_MERGE
                d0 = l * TILES_DOWN
                u0 = l * TILES_UP
                pe.wait_ge(four_set, 4 * (l + 1))
                pe.wait_ge(o_split, N_TILES // 2 * (l + 1) - 4)
                pe.wait_ge(exped, N_ROWS * (l + 1))

                def merge_down(g, after=None):
                    n = n0 + down_unit(g, N_MERGE)
                    pe.wait_ge(lo_split, n + 1)
                    pe.wait_ge(u_lo_set, u0 + 4 * (g + 1))
                    down(n % 2, g % 2, g == 0,
                         lambda i: (g or i >= 4) and pe.wait_ge(added, d0 + 16 * g + i - 3), after)

                pe.wait_ge(pt_lo_set, 2 * N_ROWS * (l + 1))
                branch(l, 0)
                for g in range(1, N_MERGE):
                    branch(l, g)
                    merge_down(g - 1)
                merge_down(N_MERGE - 1, norm_turns(2 * l + 1))
                n0 = l * UNITS + U_MLP
                d0 += 16 * N_MERGE
                u0 += 4 * N_MERGE
                r0 = l * 4 * N_MLP
                def mlp_up(g):
                    n = n0 + up_unit(g)
                    pe.wait_ge(lo_split, n + 1)
                    up(n % 2, lambda i: g and pe.wait_ge(relu_set, r0 + 4 * (g - 1) + i + 1))

                def mlp_down(g, after=None):
                    n = n0 + down_unit(g, N_MLP)
                    pe.wait_ge(lo_split, n + 1)
                    pe.wait_ge(u_lo_set, u0 + 4 * (g + 1))
                    down(n % 2, g % 2, g == 0, lambda i: pe.wait_ge(added, d0 + 16 * g + i - 3), after)

                turn_h(2 * l + 1, 5)
                pe.wait_ge(lo_split, n0 + 1)
                for i in range(4):
                    th, fb = i // 2, i % 2
                    if i == 1:
                        turn_h(2 * l + 1, 6)
                        turn_h(2 * l + 1, 7)
                    if i == 0:
                        pe.wait_ge(ht_lo_set, 2 * TB * (2 * l + 1) + 8)
                    if i == 2:
                        pe.wait_ge(ht_lo_set, 2 * TB * (2 * l + 2))
                    pe.wait_ge(added, d0 - 4 + i + 1)
                    for kb in range(KB):
                        w = slice(kb * CHUNK + fb * P, kb * CHUNK + (fb + 1) * P)
                        tok = slice(th * NT, (th + 1) * NT)
                        mm = three(ps[:, 4 + i, :], (w_hi[:, 0, w], w_lo[:, 0, w]),
                                   (ht_hi[:, kb, tok], ht_lo[:, kb, tok]), kb == 0, kb == KB - 1)
                    mm.then_inc(up_done, 1)
                with pe.Fori(0, N_MLP // 2 - 1) as it:
                    for j in range(2):
                        pe.wait_ge(lo_split, it * 4 + (n0 + 2 * j + 2))
                        up(1, lambda i: pe.wait_ge(relu_set, it * 8 + (r0 + 4 * j + i + 1)))
                        pe.wait_ge(lo_split, it * 4 + (n0 + 2 * j + 3))
                        pe.wait_ge(u_lo_set, it * 8 + (u0 + 4 * j + 4))
                        down(0, j, False, lambda i: pe.wait_ge(added, it * 32 + (d0 + 16 * j + i - 3)))
                mlp_up(N_MLP - 1)
                mlp_down(N_MLP - 2)
                mlp_down(N_MLP - 1, norm_turns(2 * l + 2) if l + 1 < DEPTH else None)

        @block.scalar
        def _(act):
            def split_hi(n, slot):
                nc.scalar.activation(w_hi[:, slot, :], raw[:, slot, :], ACT.Copy).then_inc(hi_split, 1)

            def split(n):
                extra = sum(1 for m in merge_loads if m <= n and (m - n) % 2 == 0)
                act.wait_ge(raw_loaded[n % 2], 16 * (n // 2 + 1 + extra))
                if n % UNITS in (U_MERGE, U_MERGE + 1):
                    act.wait_ge(scored, N_ROWS * (n // UNITS + 1))
                elif n >= 2:
                    act.wait_ge(*used(n - 2))
                split_hi(n, n % 2)

            merge_loads = [l * UNITS + U_MERGE + up_unit(g) for l in range(DEPTH) for g in range(N_MERGE)]

            def loads_before(n):
                return n // 2 + 1 + sum(1 for m in merge_loads if m <= n and (m - n) % 2 == 0)

            def norm_sums(k, tb):
                if k == 0:
                    act.wait_ge(x_loaded[tb], 16)
                else:
                    act.wait_ge(added, (k - 1) // 2 * TILES_DOWN + 16 * (N_MERGE if k % 2 else N_MERGE + N_MLP) - 14 + 2 * tb)
                if tb == 0:
                    act.wait_ge(g_loaded, 16 * (k + 1))
                if k >= 1:
                    act.wait_ge(h_ready, TB * (k - 1) + tb + 1)
                nc.scalar.activation(junk[:], x[:, tb, :], ACT.Square,
                                     accum_out=rstd[:, 0, tb:tb + 1]).then_inc(sq_summed, 1)
                act.wait_ge(sq_summed, TB * k + tb + 1)
                nc.scalar.activation(rstd[:, 1, tb:tb + 1], rstd[:, 0, tb:tb + 1], ACT.Sqrt,
                                     bias=eps[:], scale=1.0 / D).then_inc(sd_ready, 1)

            def keep_hi(k, tb):
                for i in range(2):
                    act.wait_ge(h_turned, 2 * (TB * k + tb) + i + 1)
                    nc.scalar.activation(ht_hi[:, 4 * i:4 * i + 4, tb * P:(tb + 1) * P],
                                         ps[:, 2 * (tb % 2) + i, :].rearrange("p (a c) -> p a c", a=4),
                                         ACT.Copy).then_inc(ht_hi_set, 1)

            def norm(k, units):
                for s in range(TB + 4):
                    if s < TB:
                        norm_sums(k, s)
                    if s >= 4 and k < 2 * DEPTH:
                        keep_hi(k, s - 4)
                    if s in units:
                        split(units[s])

            act.wait_ge(eps_set, 1)
            norm(0, {2: 0, 5: 1})
            for l in range(DEPTH):
                n0 = l * UNITS
                for c in range(3):
                    split(n0 + 2 * c + 2)
                    if c == 1 and l == 0:
                        act.wait_ge(dft_loaded, 32)
                        nc.scalar.activation(dft64_hi[:], dft64[:], ACT.Copy).then_inc(dft_hi, 1)
                        nc.scalar.activation(alt_col_r[:], alt_col[:], ACT.Copy).then_inc(dft_hi, 1)
                        act.wait_ge(dft_lo, 1)
                        act.wait_ge(consts_loaded, 16 * 7)
                    for tb in range(TB):
                        act.wait_ge(proj_done, TB * (3 * l + c) + tb + 1)
                        dst = vf[:, tb, :] if c == 0 else qk[:, tb, (c - 1) * NT:c * NT]
                        nc.scalar.activation(dst, ps[:, (tb + 4) % TB, :], ACT.Copy).then_inc(proj_kept, 1)
                    split(n0 + 2 * c + 3)
                act.wait_ge(qk_summed, 2 * TB * (l + 1))
                nc.scalar.activation(qk_stat[:, 1, :], qk_stat[:, 0, :], ACT.Sqrt, bias=eps[:],
                                     scale=1.0 / HD).then_inc(qk_sd, 1)

                if l:
                    act.wait_ge(x_parked, 16 * TB * l)
                for i in range(4):
                    act.wait_ge(f_turned, 4 * l + i + 1)
                    nc.scalar.activation(f_t[:, i // 2, (i % 2) * NT:(i % 2 + 1) * NT], ps[:, 4 + i, :],
                                         ACT.Copy).then_inc(f_kept, 1)
                act.wait_ge(folded, l + 1)
                nc.scalar.activation(fold_hi[:], fold[:], ACT.Copy).then_inc(fold_hi_set, 1)

                gates_out = gates.rearrange("a f p n -> p (a f) n")
                for j in range(N_GATE):
                    for i in range(4):
                        k = 4 * (N_GATE * l + j) + i
                        fb = 2 * j + i // 2
                        act.wait_ge(gate_done, k + 1)
                        if k >= 2:
                            act.wait_ge(gate_stored[i % 2], 16 * (k // 2))
                        nc.scalar.activation(gate_out[:, i % 2, :], ps[:, i, :], ACT.Sigmoid,
                                             bias=b_gate[:, l, fb:fb + 1]).then_inc(gate_made, 1)
                        act.wait_ge(gate_made, k + 1)
                        act.dma_start(gates_out[:, fb:fb + 1, (i % 2) * NT:(i % 2 + 1) * NT],
                                      gate_out[:, i % 2:i % 2 + 1, :]).then_inc(gate_stored[i % 2], 16)
                    if j < N_GATE - 2:
                        split(n0 + gate_unit(j) + 2)
                    if j == 1:
                        act.wait_ge(rows_done, 5 * l + 1)
                        nc.scalar.activation(last_row, ps[0:1, 7, 0:2 * P], ACT.Copy).then_inc(gh_hi_set, 1)
                        for sb in range(4):
                            act.wait_ge(rows_done, 5 * l + sb + 2)
                            nc.scalar.activation(gh_hi[:, sb].rearrange("p a b c -> p (a b c)"), ps[:, 4 + sb, :],
                                                 ACT.Copy).then_inc(gh_hi_set, 1)
                    if j == 3:
                        act.wait_ge(freq_done, 5 * l + 1)
                        nc.scalar.activation(mid_out[:], ps[:, 6, 0:4:2], ACT.Copy).then_inc(cosine_kept, 1)
                        for cb in range(2):
                            act.wait_ge(freq_done, 5 * l + cb + 2)
                            nc.scalar.activation(cosine[:, cb, :], ps[:, 4 + cb, :], ACT.Copy).then_inc(cosine_kept, 1)
                        split(n0 + U_DFT + 2)
                        split(n0 + U_DFT + 3)

                act.wait_ge(*used(n0 + U_MERGE - 1))
                for tb in range(TB):
                    for part in range(3):
                        act.wait_ge(turned, 2 * (TB * l + tb) + (1, 2, 2)[part])
                        dst, src = turn_parts(tb, part)
                        nc.scalar.activation(dst[0], src, ACT.Copy).then_inc(turn_act, 1)

                def exp(n):
                    act.wait_ge(topped, N_ROWS * l + n + 1)
                    if n >= 4:
                        act.wait_ge(p_turned, 2 * (N_ROWS * l + n - 3))
                    nc.scalar.activation(prob[:, n % 4, :], ps[:, 2 * (n % 2):2 * (n % 2) + 2, :].rearrange("p a c -> p (a c)"),
                                         ACT.Exp, bias=top[:, 0, n % 4:n % 4 + 1],
                                         accum_out=top[:, 1, n % 4:n % 4 + 1]).then_inc(exped, 1)

                act.wait_ge(f_made, l + 1)
                exp(0)
                for n in range(N_ROWS + 1):
                    if n + 1 < N_ROWS:
                        exp(n + 1)
                    if n == N_ROWS - 1:
                        split(n0 + U_MERGE)
                    if n >= 1:
                        m = n - 1
                        tile, qb = m // 2, m % 2
                        if tile >= 2 and qb == 0:
                            act.wait_ge(valued, N_TILES * l + tile - 1)
                        for i in range(2):
                            k = 2 * m + i
                            act.wait_ge(p_turned, 2 * N_ROWS * l + k + 1)
                            nc.scalar.activation(pt_hi[:, tile % 2, 4 * i:4 * i + 4, qb * P:(qb + 1) * P],
                                                 ps[:, 4 + k % 3, :].rearrange("p (a c) -> p a c", a=4),
                                                 ACT.Copy).then_inc(pt_hi_set, 1)
                        if n % 2 == 0 and n >= 4:
                            tile = n // 2 - 2
                            act.wait_ge(valued, N_TILES * l + tile + 1)
                            if tile >= 2:
                                act.wait_ge(o_summed, N_TILES * l + tile - 1)
                            nc.scalar.activation(v_low[0:HD, tile % 2, :], ps[HD:P, 7, 0:QB], ACT.Copy).then_inc(v_low_set, 1)
                tile = N_TILES - 1
                act.wait_ge(valued, N_TILES * l + tile + 1)
                act.wait_ge(o_summed, N_TILES * l + tile - 1)
                nc.scalar.activation(v_low[0:HD, tile % 2, :], ps[HD:P, 7, 0:QB], ACT.Copy).then_inc(v_low_set, 1)

                split(n0 + U_MERGE + 1)

                u0 = l * TILES_UP

                def merge_hi(g):
                    for i in range(4):
                        k = l * 4 * N_MERGE + 4 * g + i
                        act.wait_ge(gated, k + 1)
                        if g >= 2 and i == 0:
                            act.wait_ge(*used(n0 + U_MERGE + down_unit(g - 2, N_MERGE)))
                        nc.scalar.activation(u_hi[:, 2 * (g % 2) + i // 2, (i % 2) * NT:(i % 2 + 1) * NT],
                                             gate_in[:, i, 0, :], ACT.Copy).then_inc(u_hi_set, 1)

                merge_hi(0)
                split(n0 + U_MERGE + 2)
                for g in range(1, N_MERGE):
                    merge_hi(g)
                    split(n0 + U_MERGE + up_unit(g) + 2)
                    if g < N_MERGE - 1:
                        split(n0 + U_MERGE + up_unit(g) + 3)
                norm(2 * l + 1, {2: n0 + U_MLP})
                split(n0 + U_MLP + 1)

                m0 = n0 + U_MLP
                r0 = l * 4 * N_MLP
                d0 = l * TILES_DOWN + 16 * N_MERGE

                def relu_tiles(par, val, fresh, used):
                    def hi(i):
                        act.wait_ge(squared, val(i))
                        if i == 0:
                            used()
                        fb, th = (i % 2, i // 2) if fresh else (i // 2, i % 2)
                        nc.scalar.activation(u_hi[:, 2 * par + fb, th * NT:(th + 1) * NT],
                                             squares[:, i % 2, :], ACT.Copy).then_inc(u_hi_set, 1)
                    for i in range(4):
                        act.wait_ge(up_done, val(i))
                        if not fresh or i >= 2:
                            act.wait_ge(squared, val(i - 2))
                        nc.scalar.activation(relu[:, i % 2, :], ps[:, 4 * fresh + i, :], ACT.Relu).then_inc(relu_set, 1)
                        if i:
                            hi(i - 1)
                    hi(3)

                relu_tiles(0, lambda i: r0 + i + 1, True, lambda: None)
                split(m0 + 2)
                with act.Fori(0, N_MLP // 2 - 1) as it:
                    for j in range(2):
                        relu_tiles((1 + j) % 2, lambda i: it * 8 + (r0 + 4 * (j + 1) + i + 1), False,
                                   lambda: act.wait_ge(down_done, it * 32 + (d0 + 16 * j)))
                        for s in (1, 0):
                            q = 2 * j + (3 if s else 4)
                            act.wait_ge(raw_loaded[s], it * 32 + 16 * loads_before(m0 + q))
                            if s:
                                act.wait_ge(up_done, it * 8 + (r0 + 4 * j + 8))
                            else:
                                act.wait_ge(down_done, it * 32 + (d0 + 16 * j + 16))
                            split_hi(None, s)
                g = N_MLP - 1
                relu_tiles(1, lambda i: r0 + 4 * g + i + 1, False,
                           lambda: act.wait_ge(*used(m0 + down_unit(g - 2, N_MLP))))
                split(m0 + 2 * N_MLP - 1)
                norm(2 * l + 2, {2: n0 + UNITS} if l + 1 < DEPTH else {})
                if l + 1 < DEPTH:
                    split(m0 + 2 * N_MLP + 1)

        @block.vector
        def _(dve):
            step = [0]

            def link(ins):
                step[0] += 1
                ins.then_inc(chain, 1)
                dve.wait_ge(chain, step[0])

            def newton(r, sd, sq, scale, tmp):
                link(nc.vector.tensor_scalar(tmp, sq, scale, EPS, ALU.mult, ALU.add))
                link(nc.vector.reciprocal(r, sd))
                link(nc.vector.tensor_tensor(tmp, tmp, r, ALU.mult))
                link(nc.vector.tensor_tensor(tmp, tmp, r, ALU.mult))
                link(nc.vector.tensor_scalar(tmp, tmp, -0.5, 1.5, ALU.mult, ALU.add))
                link(nc.vector.tensor_tensor(r, r, tmp, ALU.mult))

            def norm_inv(k, tb):
                dve.wait_ge(sd_ready, TB * k + tb + 1)
                nc.vector.reciprocal(rstd[:, 2, tb:tb + 1], rstd[:, 1, tb:tb + 1]).then_inc(inv_ready, 1)

            def norm_row(k, tb):
                dve.wait_ge(rstd_ready, TB * k + tb + 1)
                if tb == 0:
                    dve.wait_ge(g_loaded, 16 * (k + 1))
                if tb >= 2:
                    if k < 2 * DEPTH:
                        dve.wait_ge(h_turned, 2 * (TB * k + tb - 1))
                    else:
                        dve.wait_ge(y_stored[tb % 2], 16 * (tb // 2))
                nc.vector.scalar_tensor_tensor(out=h_row[:, tb % 2, :], in0=x[:, tb, :], scalar=rstd[:, 2, tb:tb + 1],
                                               in1=g_row[:], op0=ALU.mult, op1=ALU.mult).then_inc(h_ready, 1)

            def keep_lo(k, tb):
                for i in range(2):
                    dve.wait_ge(ht_hi_set, 2 * (TB * k + tb) + i + 1)
                    hi = ht_hi[:, 4 * i:4 * i + 4, tb * P:(tb + 1) * P]
                    nc.vector.tensor_tensor(ht_lo[:, 4 * i:4 * i + 4, tb * P:(tb + 1) * P],
                                            ps[:, 2 * (tb % 2) + i, :].rearrange("p (a c) -> p a c", a=4),
                                            f32(hi), ALU.subtract).then_inc(ht_lo_set, 1)

            def norm(k, adds):
                for s in range(TB + 4):
                    if s < TB:
                        adds(s)
                    if 1 <= s <= TB:
                        norm_inv(k, s - 1)
                    if 2 <= s < TB + 2:
                        norm_row(k, s - 2)
                    if k == 0 and s == 4:
                        dve.wait_ge(hi_split, 1)
                        nc.vector.tensor_tensor(w_lo[:, 0, :], raw[:, 0, :], f32(w_hi[:, 0, :]),
                                                ALU.subtract).then_inc(lo_split, 1)
                    if s >= 4 and k < 2 * DEPTH:
                        keep_lo(k, s - 4)

            def add_tile(i, val, back=None):
                dve.wait_ge(down_done, val)
                if back:
                    dve.wait_ge(x_loaded[i // 2], back)
                xt = x[:, i // 2, (i % 2) * NT:(i % 2 + 1) * NT]
                nc.vector.tensor_tensor(xt, ps[:, 4 + i % 4, :], xt, ALU.add).then_inc(added, 1)

            nc.vector.memset(eps[:], EPS).then_inc(eps_set, 1)
            norm(0, lambda tb: None)
            dve.wait_ge(dft_hi, 1)
            nc.vector.tensor_tensor(dft64_lo[:], dft64[:], f32(dft64_hi[:]), ALU.subtract).then_inc(dft_lo, 1)
            dve.wait_ge(consts_loaded, 16 * 7)
            for l in range(DEPTH):
                link(nc.vector.tensor_scalar(qk_gain[:, l, 0, :], qk_gain[:, l, 0, :], HD ** -0.5, None, ALU.mult))
            for l in range(DEPTH):
                n0 = l * UNITS
                for c in (1, 2):
                    for tb in range(TB):
                        dve.wait_ge(proj_kept, TB * (3 * l + c) + tb + 1)
                        src = qk[:, tb, (c - 1) * NT:c * NT]
                        done = TB * (2 * l + c - 1) + tb
                        sq = rope_tmp[:, 0, :]
                        if done:
                            dve.wait_ge(qk_summed, done)
                        link(nc.vector.tensor_tensor(sq, src, src, ALU.mult))
                        nc.vector.tensor_reduce(qk_stat[:, 0, tb * 16 + 8 * (c - 1):tb * 16 + 8 * c],
                                                sq.rearrange("p (h c) -> p h c", h=8), AX.X,
                                                ALU.add).then_inc(qk_summed, 1)
                dve.wait_ge(f_kept, 4 * (l + 1))
                fwd, rev = f_t[:, :, 1:HALF], f_t[:, :, SEQ - 1:HALF:-1]
                nc.vector.tensor_tensor(fold[:, 0, :, 1:], fwd, rev, ALU.add)
                nc.vector.tensor_tensor(fold[:, 1, :, 1:], fwd, rev, ALU.subtract)
                nc.vector.tensor_copy(fold[:, 0, :, 0:1], f_t[:, :, 0:1])
                nc.vector.tensor_copy(mid[:].unsqueeze(2), f_t[:, :, HALF:HALF + 1])
                nc.vector.memset(fold[:, 1, :, 0:1], 0.0).then_inc(folded, 1)
                dve.wait_ge(fold_hi_set, l + 1)
                nc.vector.tensor_tensor(fold_lo[:], fold[:], f32(fold_hi[:]), ALU.subtract).then_inc(fold_lo_set, 1)

                dve.wait_ge(qk_sd, l + 1)
                r_all = qk_rstd[:].rearrange("p b h -> p (b h)")
                newton(r_all, qk_stat[:, 1, :], qk_stat[:, 0, :], 1.0 / HD, qk_stat[:, 2, :])
                t0, t1 = (rope_tmp[:, i, :].rearrange("p (h c) -> p h c", h=16) for i in range(2))
                for tb in range(TB):
                    row = qk[:, tb, :].rearrange("p (h c) -> p h c", h=16)
                    link(nc.vector.tensor_tensor(row, row, qk_rstd[:, tb, :].unsqueeze(2).to_broadcast([P, 16, HD]), ALU.mult))
                    for i, hs in enumerate((slice(0, NH), slice(NH, 16))):
                        g = qk_gain[:, l, i, :].unsqueeze(1).to_broadcast([P, hs.stop - hs.start, HD])
                        link(nc.vector.tensor_tensor(row[:, hs, :], row[:, hs, :], g, ALU.mult))
                    if tb:
                        dve.wait_ge(qk_ready, TB * l + tb)
                    x0, x1 = row[:, :, 0:HD:2], row[:, :, 1:HD:2]
                    c, s = (rope[:, tb, i, :].unsqueeze(1).to_broadcast([P, 16, 32]) for i in range(2))
                    nc.vector.tensor_tensor(t0, x0, s, ALU.mult)
                    link(nc.vector.tensor_tensor(t1, x1, s, ALU.mult))
                    link(nc.vector.tensor_tensor(x0, x0, c, ALU.mult))
                    link(nc.vector.tensor_tensor(x1, x1, c, ALU.mult))
                    nc.vector.tensor_tensor(x0, x0, t1, ALU.subtract)
                    nc.vector.tensor_tensor(x1, x1, t0, ALU.add).then_inc(qk_ready, 1)
                    if tb == 5:
                        for sb in range(4):
                            dve.wait_ge(gh_hi_set, 5 * l + sb + 2)
                            nc.vector.tensor_tensor(gh_lo[:, sb].rearrange("p a b c -> p (a b c)"), ps[:, 4 + sb, :],
                                                    f32(gh_hi[:, sb].rearrange("p a b c -> p (a b c)")),
                                                    ALU.subtract).then_inc(gh_lo_set, 1)
                dve.wait_ge(cosine_kept, 3 * (l + 1))
                dve.wait_ge(freq_done, 5 * (l + 1))
                nc.vector.tensor_copy(f_out[:, :, HALF:HALF + 1], mid_out[:].unsqueeze(2))
                for cb in range(2):
                    nc.vector.tensor_tensor(f_out[:, cb, 0:HALF], cosine[:, cb, :], ps[:, 6 + cb, :], ALU.subtract)
                    ins = nc.vector.tensor_tensor(f_out[:, cb, SEQ - 1:HALF:-1], cosine[:, cb, 1:HALF], ps[:, 6 + cb, 1:HALF], ALU.add)
                ins.then_inc(f_made, 1)

                for tb in range(TB):
                    for part in range(3):
                        dve.wait_ge(turn_act, 3 * (TB * l + tb) + part + 1)
                        dst, src = turn_parts(tb, part)
                        nc.vector.tensor_tensor(dst[1], src, f32(dst[0]), ALU.subtract).then_inc(turn_dve, 1)

                def top_of(n):
                    dve.wait_ge(scored, N_ROWS * l + n + 1)
                    nc.vector.tensor_reduce(top[:, 0, n % 4:n % 4 + 1], ps[:, 2 * (n % 2):2 * (n % 2) + 2, :].rearrange("p a c -> p (a c)"),
                                            AX.X, ALU.max, negate=True).then_inc(topped, 1)

                def invert(n):
                    dve.wait_ge(exped, N_ROWS * l + n + 1)
                    nc.vector.reciprocal(top[:, 2, n % 4:n % 4 + 1], top[:, 1, n % 4:n % 4 + 1]).then_inc(inverted, 1)

                def add_low(tile):
                    odd = tile % 2
                    dve.wait_ge(v_low_set, N_TILES * l + tile + 1)
                    if tile >= 4:
                        dve.wait_ge(o_split, N_TILES // 2 * l + tile // 2 - 1)
                    nc.vector.tensor_tensor(o_sum[HD * odd:HD * odd + HD, tile // 2 % 2, :], ps[0:HD, 7, 0:QB],
                                            v_low[0:HD, tile % 2, :], ALU.add).then_inc(o_summed, 1)

                top_of(0)
                top_of(1)
                invert(0)
                for n in range(N_ROWS + 1):
                    if n + 2 < N_ROWS:
                        top_of(n + 2)
                    if n + 1 < N_ROWS:
                        invert(n + 1)
                    if n >= 1:
                        m = n - 1
                        tile, qb = m // 2, m % 2
                        for i in range(2):
                            k = 2 * m + i
                            dve.wait_ge(pt_hi_set, 2 * N_ROWS * l + k + 1)
                            sl = (slice(None), tile % 2, slice(4 * i, 4 * i + 4), slice(qb * P, (qb + 1) * P))
                            nc.vector.tensor_tensor(pt_lo[sl], ps[:, 4 + k % 3, :].rearrange("p (a c) -> p a c", a=4),
                                                    f32(pt_hi[sl]), ALU.subtract).then_inc(pt_lo_set, 1)
                        if n % 2 == 0 and n >= 4:
                            add_low(n // 2 - 2)
                add_low(N_TILES - 1)

                k0 = l * 4 * N_MERGE
                d0 = l * TILES_DOWN

                def merge_tiles(g):
                    def lo(i):
                        dve.wait_ge(u_hi_set, l * TILES_UP + 4 * g + i + 1)
                        sl = (slice(None), 2 * (g % 2) + i // 2, slice((i % 2) * NT, (i % 2 + 1) * NT))
                        nc.vector.tensor_tensor(u_lo[sl], gate_in[:, i, 0, :], f32(u_hi[sl]), ALU.subtract).then_inc(u_lo_set, 1)
                    for i in range(4):
                        k = k0 + 4 * g + i
                        dve.wait_ge(branch_done, k + 1)
                        dve.wait_ge(gate_loaded[i], 16 * (l * N_MERGE + g + 1))
                        nc.vector.tensor_tensor(gate_in[:, i, 0, :], ps[:, i % 2, :], gate_in[:, i, 0, :], ALU.mult)
                        ins = nc.vector.tensor_tensor(gate_in[:, i, 1, :], ps[:, 2 + i % 2, :], gate_in[:, i, 1, :], ALU.mult)
                        ins.then_inc(branch_used, 1)
                        dve.wait_ge(branch_used, k + 1)
                        nc.vector.tensor_tensor(gate_in[:, i, 0, :], gate_in[:, i, 0, :], gate_in[:, i, 1, :], ALU.add).then_inc(gated, 1)
                        if i:
                            lo(i - 1)
                    lo(3)

                merge_tiles(0)
                for g in range(1, N_MERGE):
                    merge_tiles(g)
                    for i in range(16):
                        add_tile(i, d0 + 16 * (g - 1) + i + 1, 16 * (l + 2) if g == 1 else None)

                def last_adds(base):
                    def adds(tb):
                        add_tile(2 * tb, base + 2 * tb + 1)
                        add_tile(2 * tb + 1, base + 2 * tb + 2)
                    return adds

                norm(2 * l + 1, last_adds(d0 + 16 * (N_MERGE - 1)))

                d0 += 16 * N_MERGE
                u0 = l * TILES_UP + 4 * N_MERGE
                r0 = l * 4 * N_MLP

                def square_tiles(par, r, u, fresh=False):
                    def lo(i):
                        dve.wait_ge(u_hi_set, u(i))
                        fb, th = (i % 2, i // 2) if fresh else (i // 2, i % 2)
                        sl = (slice(None), 2 * par + fb, slice(th * NT, (th + 1) * NT))
                        nc.vector.tensor_tensor(u_lo[sl], squares[:, i % 2, :], f32(u_hi[sl]), ALU.subtract).then_inc(u_lo_set, 1)
                    for i in range(4):
                        dve.wait_ge(relu_set, r(i))
                        dve.wait_ge(u_lo_set, u(i) - 2)
                        nc.vector.tensor_tensor(squares[:, i % 2, :], relu[:, i % 2, :], relu[:, i % 2, :], ALU.mult).then_inc(squared, 1)
                        if i:
                            lo(i - 1)
                    lo(3)

                square_tiles(0, lambda i: r0 + i + 1, lambda i: u0 + i + 1, True)
                with dve.Fori(0, N_MLP // 2 - 1) as it:
                    for j in range(2):
                        square_tiles((1 + j) % 2, lambda i: it * 8 + (r0 + 4 * (j + 1) + i + 1),
                                     lambda i: it * 8 + (u0 + 4 * (j + 1) + i + 1))
                        for i in range(16):
                            add_tile(i, it * 32 + (d0 + 16 * j + i + 1))
                g = N_MLP - 1
                square_tiles(1, lambda i: r0 + 4 * g + i + 1, lambda i: u0 + 4 * g + i + 1)
                for i in range(16):
                    add_tile(i, d0 + 16 * (g - 1) + i + 1)
                norm(2 * l + 2, last_adds(d0 + 16 * g))

        @block.gpsimd
        def _(pool):
            def split_lo(slot):
                nc.gpsimd.tensor_tensor(w_lo[:, slot, :], raw[:, slot, :], f32(w_hi[:, slot, :]),
                                        ALU.subtract).then_inc(lo_split, 1)

            chain_len = [0]

            def link(ins):
                chain_len[0] += 1
                ins.then_inc(newton_step, 1)
                pool.wait_ge(newton_step, chain_len[0])

            def newton(k, tb):
                r, t = rstd[:, 2, tb:tb + 1], rstd[:, 3, tb:tb + 1]
                pool.wait_ge(inv_ready, TB * k + tb + 1)
                link(nc.gpsimd.tensor_scalar(t, rstd[:, 0, tb:tb + 1], 1.0 / D, EPS, ALU.mult, ALU.add))
                link(nc.gpsimd.tensor_tensor(t, t, r, ALU.mult))
                link(nc.gpsimd.tensor_tensor(t, t, r, ALU.mult))
                link(nc.gpsimd.tensor_scalar(t, t, -0.5, 1.5, ALU.mult, ALU.add))
                nc.gpsimd.tensor_tensor(r, r, t, ALU.mult).then_inc(rstd_ready, 1)

            def newtons(k, unit=None):
                for tb in range(TB):
                    newton(k, tb)
                    if unit is not None and tb in (2, 3):
                        if tb == 2:
                            pool.wait_ge(hi_split, unit + 1)
                        part = slice((tb - 2) * UNIT // 2, (tb - 1) * UNIT // 2)
                        ins = nc.gpsimd.tensor_tensor(w_lo[:, unit % 2, part], raw[:, unit % 2, part],
                                                      f32(w_hi[:, unit % 2, part]), ALU.subtract)
                        if tb == 3:
                            ins.then_inc(lo_split, 1)

            def v_split(tb):
                src = vf[:, tb, 0:KVW].rearrange("p (k c) -> p k c", k=NKV)
                if tb == 0:
                    pool.wait_ge(*used(l * UNITS + U_MERGE - 1))
                nc.gpsimd.tensor_copy(v_hl[:, tb, :, 0:HD], src).then_inc(v_hi_set, 1)
                pool.wait_ge(v_hi_set, TB * l + tb + 1)
                nc.gpsimd.tensor_tensor(v_hl[:, tb, :, HD:P], src, f32(v_hl[:, tb, :, 0:HD]),
                                        ALU.subtract).then_inc(v_lo_set, 1)

            def split_one(n):
                pool.wait_ge(hi_split, n + 1)
                split_lo(n % 2)

            for l in range(DEPTH):
                n0 = l * UNITS
                if l == 0:
                    for tb in range(TB):
                        newton(0, tb)
                        if tb == 6:
                            pool.wait_ge(lo_split, 1)
                            split_one(1)
                with pool.Fori(1, U_MERGE // 2) as it:
                    for s in range(2):
                        pool.wait_ge(hi_split, it * 2 + (n0 + s + 1))
                        split_lo(s)

                for tb in range(TB):
                    pool.wait_ge(qk_ready, TB * l + tb + 1)
                    if tb == 0:
                        pool.wait_ge(rows_done, 5 * (l + 1))
                    elif tb >= 4:
                        pool.wait_ge(turned, 2 * (TB * l + tb - 4) + 1)
                    nc.gpsimd.tensor_copy(k_twice[:, tb % 4].rearrange("p k (d c) -> p k d c", d=2),
                                          qk[:, tb, QW:].rearrange("p (k c) -> p k c", k=NKV).unsqueeze(2).to_broadcast([P, NKV, 2, HD])).then_inc(k_doubled, 1)
                    if tb >= 4:
                        v_split(2 * tb - 8)
                        v_split(2 * tb - 7)

                def split_out(both):
                    pair, quarter = both // 4, both % 4
                    tok = slice(quarter * QB, (quarter + 1) * QB)
                    done = N_TILES // 2 * l + both + 1
                    pool.wait_ge(o_summed, 2 * done)
                    nc.gpsimd.tensor_copy(q_t[:, 2 * pair, tok], o_sum[:, both % 2, :]).then_inc(o_hi_set, 1)
                    pool.wait_ge(o_hi_set, done)
                    nc.gpsimd.tensor_tensor(q_t[:, 2 * pair + 1, tok], o_sum[:, both % 2, :],
                                            f32(q_t[:, 2 * pair, tok]), ALU.subtract).then_inc(o_split, 1)

                for n in range(N_ROWS):
                    pool.wait_ge(inverted, N_ROWS * l + n + 1)
                    nc.gpsimd.tensor_scalar(prob[:, n % 4, :], prob[:, n % 4, :], top[:, 2, n % 4:n % 4 + 1], 1.0,
                                            ALU.mult, ALU.mult).then_inc(normed, 1)
                    if n % 4 == 3 and n >= 7:
                        split_out(n // 4 - 1)
                    if n in FOUR_STEPS:
                        q = FOUR_STEPS.index(n)
                        cb, tok = q // 2, slice((q % 2) * NT, (q % 2 + 1) * NT)
                        nc.gpsimd.tensor_copy(four[:, 0, cb, tok], f_out[:, cb, tok]).then_inc(four_hi_set, 1)
                        pool.wait_ge(four_hi_set, 4 * l + q + 1)
                        nc.gpsimd.tensor_tensor(four[:, 1, cb, tok], f_out[:, cb, tok], f32(four[:, 0, cb, tok]),
                                                ALU.subtract).then_inc(four_set, 1)
                split_one(n0 + U_MERGE)
                split_out(N_TILES // 2 - 1)
                for u in range(1, 2 * N_MERGE):
                    split_one(n0 + U_MERGE + u)
                newtons(2 * l + 1, n0 + U_MLP)
                with pool.Fori(0, N_MLP - 1) as it:
                    for s in (1, 0):
                        pool.wait_ge(hi_split, it * 2 + (n0 + U_MLP + (2 if s else 3)))
                        split_lo(s)
                split_one(n0 + UNITS - 1)
                newtons(2 * l + 2, n0 + UNITS if l + 1 < DEPTH else None)
                if l + 1 < DEPTH:
                    split_one(n0 + UNITS + 1)


def tables():
    pairs = HD // 4
    inv = np.float32(10000.0) ** (-np.arange(pairs, dtype=np.float32) / np.float32(pairs))
    pos = np.arange(SEQ)
    ang = np.concatenate([(pos // 64).astype(np.float32)[:, None] * inv, (pos % 64).astype(np.float32)[:, None] * inv], -1)
    rope = np.stack([np.cos(ang), np.sin(ang)], 1).astype(np.float32)
    scale = 1.0 / np.sqrt(SEQ * 64.0)
    sk = np.outer(np.arange(HALF), np.arange(HALF)) % SEQ * (2 * np.pi / SEQ)
    cc = np.outer(np.arange(64), np.arange(64)) % 64 * (2 * np.pi / 64)
    two = np.eye(2)
    return {
        "c_ident": np.eye(P, dtype=np.float32),
        "c_rope": rope,
        "c_cos": (np.cos(sk) * scale).astype(np.float32),
        "c_sin": (np.sin(sk) * scale).astype(np.float32),
        "c_dft64": np.concatenate([np.kron(two, np.cos(cc)), np.kron(two, np.sin(cc))], 1).astype(np.float32),
        "c_alt": (scale * (1.0 - 2.0 * (np.arange(NT) % 2)))[None].astype(np.float32),
        "c_altcol": (scale * (1.0 - 2.0 * (np.arange(P) % 2)))[:, None].repeat(2, 1).astype(np.float32),
    }


def kernel(**inputs):
    import concourse.bacc as bacc
    from concourse.bass_utils import run_bass_kernel_spmd

    nc = bacc.Bacc("TRN2", target_bir_lowering=False, num_devices=1)
    arrays, args = {}, {}
    for name, a in {**inputs, **tables()}.items():
        a = np.ascontiguousarray(a)
        arrays[f"in_{name}"] = a
        args[name] = nc.dram_tensor(f"in_{name}", a.shape, mybir.dt.from_np(a.dtype), kind="ExternalInput").ap()
    out = nc.dram_tensor("out_0", (1, SEQ, D), F32, kind="ExternalOutput").ap()
    build(nc, args, out)
    r = run_bass_kernel_spmd(nc, [arrays], core_ids=[0])
    return r.results[0]["out_0"]
```

```python
from contextlib import ExitStack

import numpy as np

import concourse.bass as bass
from concourse import mybir

F32 = mybir.dt.float32
F32R = mybir.dt.float32r
ACT = mybir.ActivationFunctionType
ALU = mybir.AluOpType
AX = mybir.AxisListType

P = 128
D, SEQ, DEPTH = 1024, 1024, 2
HD, NH, NKV = 64, 12, 4
GROUP = NH // NKV
QW, KVW = NH * HD, NKV * HD
FW = 256
DFF = 4 * D
EPS = 1e-6
KB = D // P
TB = SEQ // P
NT = 512
UNIT = 2048
CHUNK = UNIT // KB
N_PROJ, N_GATE = 6, 2 * D // CHUNK
N_MERGE, N_MLP = D // CHUNK, DFF // CHUNK
U_GATE = N_PROJ
U_DFT = U_GATE + N_GATE // 2
U_MERGE = U_GATE + N_GATE + 2
U_MLP = U_MERGE + 2 * N_MERGE
UNITS = U_MLP + 2 * N_MLP
HALF = SEQ // 2
QB = 256
N_TILES = NH * SEQ // QB
N_ROWS = 2 * N_TILES
FOUR_STEPS = (9, 13, 17, 21)
MERGE_STEPS = (56, 62, 67)


def gate_unit(j):
    return U_GATE + j + (2 if j >= N_GATE // 2 else 0)


def up_unit(g):
    return 2 * g - 1 if g else 0


def down_unit(g, n):
    return 2 * g + 2 if g < n - 1 else 2 * n - 1


def build(nc, t, out):
    ctx = ExitStack()
    with ctx:
        def sem(name):
            return ctx.enter_context(nc.semaphore(name))

        base = (nc.sbuf_base + 31) // 32 * 32
        plan = {}
        off = base
        for name, size in (("x", 32768), ("raw", 16384), ("w", 32768), ("a", 65536), ("b", 32768),
                           ("vf", 16384), ("tmp", 8192), ("rope", 2048), ("dft64", 2048),
                           ("ident", 512), ("gain", 1024), ("bgate", 128), ("small", 1024), ("last", 1024)):
            plan[name] = off
            off += size

        def at(name, shape, dt, region, byte=0):
            return nc.alloc_sbuf_tensor_at(name, [P] + shape, dt, offset=plan[region] + byte)

        x = at("x", [TB, D], F32, "x")
        raw = at("raw", [2, UNIT], F32, "raw")
        w_hi = at("w_hi", [2, UNIT], F32R, "w")
        w_lo = at("w_lo", [2, UNIT], F32R, "w", 16384)
        ht_hi = at("ht_hi", [KB, SEQ], F32R, "a")
        ht_lo = at("ht_lo", [KB, SEQ], F32R, "a", 32768)
        q_t = at("q_t", [2, KB, SEQ], F32R, "a")
        four = at("four", [2, KB, SEQ], F32R, "a")[:, :, NH // 2:, :]
        v_hl = at("v_hl", [TB, NKV, P], F32R, "vf")
        v_rows = at("v_rows", [TB, NKV, 2, HD], F32, "vf")[:, :, :, 1, :]
        k_hi = at("k_hi", [NKV, SEQ], F32R, "w")
        k_lo = at("k_lo", [NKV, SEQ], F32R, "w", 16384)
        prob = at("prob", [4, SEQ], F32, "x", 16384)
        k_twice = [at(f"k_twice{i}", [TB // 2, NKV, P], F32, "x", (8192, 24576)[i]) for i in range(2)]
        qk = at("qk", [TB, D], F32, "b")
        pt_hi = at("pt_hi", [2, KB, QB], F32R, "b")
        pt_lo = at("pt_lo", [2, KB, QB], F32R, "b", 16384)
        u_hi = at("u_hi", [4, SEQ], F32R, "b")
        u_lo = at("u_lo", [4, SEQ], F32R, "b", 16384)
        h_row = at("h_row", [2, D], F32, "b")
        g_row = at("g_row", [D], F32, "b", 16384)
        junk = at("junk", [D], F32, "b", 20480)
        f_rows = at("f_rows", [TB, FW], F32, "x", 24576)
        f_t = at("f_t", [2, SEQ], F32, "x")
        fold = at("fold", [2, 2, HALF], F32, "x", 8192)
        fold_hi = at("fold_hi", [2, 2, HALF], F32R, "x", 16384)
        fold_lo = at("fold_lo", [2, 2, HALF], F32R, "x", 24576)
        gh_hi = at("gh_hi", [4, 2, 2, P], F32R, "x")
        gh_lo = at("gh_lo", [4, 2, 2, P], F32R, "x", 8192)
        cosine = at("cosine", [2, NT], F32, "x", 16384)
        f_out = at("f_out", [2, SEQ], F32, "x")
        dft64 = at("dft64", [2, P], F32, "b", 24576)
        dft64_hi = at("dft64_hi", [2, P], F32R, "dft64")
        dft64_lo = at("dft64_lo", [2, P], F32R, "dft64", 1024)
        alt_row = at("alt_row", [2, FW], F32, "x", 20480)[0:1]
        last_row = at("last_row", [FW], F32, "last")[0:1]
        gate_in = at("gate_in", [4, 2, NT], F32, "vf")
        gate_out = at("gate_out", [4, NT], F32, "tmp")
        relu = at("relu", [2, NT], F32, "tmp")
        rope_tmp = at("rope_tmp", [2, NT], F32, "tmp", 4096)
        squares = at("squares", [2, NT], F32, "tmp", 4096)
        qk_stat = at("qk_stat", [3, TB * 16], F32, "tmp", 6144)
        v_low = at("v_low", [2, QB], F32, "tmp", 4096)
        o_sum = at("o_sum", [2, QB], F32, "tmp", 6144)
        rope = at("rope", [TB, 2, 32], F32, "rope")
        ident = at("ident", [P], F32, "ident")
        qk_gain = at("qk_gain", [DEPTH, 2, HD], F32, "gain")
        b_gate = at("b_gate", [DEPTH, 16], F32, "bgate")
        rstd = at("rstd", [4, TB], F32, "small")
        qk_rstd = at("qk_rstd", [TB, 16], F32, "small", 128)
        top = at("top", [3, 4], F32, "small", 640)
        eps = at("eps", [1], F32, "small", 704)
        alt_col = at("alt_col", [2], F32, "small", 736)
        alt_col_r = at("alt_col_r", [2], F32R, "small", 768)
        mid = at("mid", [2], F32, "small", 800)
        mid_out = at("mid_out", [2], F32, "small", 832)

        ps = ctx.enter_context(nc.psum_tensor("ps", [P, 8, NT], F32))
        x_park = nc.dram_tensor("x_park", [SEQ, D], F32, kind="Internal").ap()
        gates = nc.dram_tensor("gates", [2, KB, P, SEQ], F32, kind="Internal").ap()

        x_loaded = [sem(f"x_loaded{i}") for i in range(TB)]
        x_parked = sem("x_parked")
        ident_loaded = sem("ident_loaded")
        consts_loaded = sem("consts_loaded")
        raw_loaded = [sem("raw_loaded0"), sem("raw_loaded1")]
        g_loaded = sem("g_loaded")
        dft_loaded = sem("dft_loaded")
        gate_loaded = [sem(f"gate_loaded{i}") for i in range(4)]
        gate_stored = [sem("gate_stored0"), sem("gate_stored1")]
        y_stored = [sem("y_stored0"), sem("y_stored1")]
        eps_set = sem("eps_set")
        hi_split = sem("hi_split")
        lo_split = sem("lo_split")
        first_half = sem("first_half")
        sq_summed = sem("sq_summed")
        sd_ready = sem("sd_ready")
        inv_ready = sem("inv_ready")
        newton_step = sem("newton_step")
        rstd_ready = sem("rstd_ready")
        chain = sem("chain")
        h_ready = sem("h_ready")
        h_turned = sem("h_turned")
        ht_hi_set = sem("ht_hi_set")
        ht_lo_set = sem("ht_lo_set")
        proj_done = sem("proj_done")
        proj_kept = sem("proj_kept")
        qk_summed = sem("qk_summed")
        qk_sd = sem("qk_sd")
        qk_ready = sem("qk_ready")
        gate_done = sem("gate_done")
        gate_made = sem("gate_made")
        k_doubled = sem("k_doubled")
        turned = sem("turned")
        turn_act = sem("turn_act")
        turn_dve = sem("turn_dve")
        v_hi_set = sem("v_hi_set")
        v_lo_set = sem("v_lo_set")
        scored = sem("scored")
        topped = sem("topped")
        exped = sem("exped")
        inverted = sem("inverted")
        normed = sem("normed")
        p_turned = sem("p_turned")
        pt_hi_set = sem("pt_hi_set")
        pt_lo_set = sem("pt_lo_set")
        valued = sem("valued")
        v_low_set = sem("v_low_set")
        o_summed = sem("o_summed")
        o_hi_set = sem("o_hi_set")
        o_split = sem("o_split")
        f_turned = sem("f_turned")
        f_kept = sem("f_kept")
        dft_hi = sem("dft_hi")
        dft_lo = sem("dft_lo")
        folded = sem("folded")
        fold_hi_set = sem("fold_hi_set")
        fold_lo_set = sem("fold_lo_set")
        rows_done = sem("rows_done")
        gh_hi_set = sem("gh_hi_set")
        gh_lo_set = sem("gh_lo_set")
        freq_done = sem("freq_done")
        cosine_kept = sem("cosine_kept")
        f_made = sem("f_made")
        four_hi_set = sem("four_hi_set")
        four_set = sem("four_set")
        branch_done = sem("branch_done")
        branch_used = sem("branch_used")
        gated = sem("gated")
        up_done = sem("up_done")
        relu_set = sem("relu_set")
        squared = sem("squared")
        u_hi_set = sem("u_hi_set")
        u_lo_set = sem("u_lo_set")
        down_done = sem("down_done")
        added = sem("added")

        block = ctx.enter_context(nc.Block())

        def f32(ap):
            return ap.bitcast(F32)

        N_STEPS = NKV + NH // 2
        TURN_PARTS = NKV + NH

        def turn_step(t):
            return ("k", t) if t < 2 else ("q", t - 2) if t < N_STEPS - 2 else ("k", t - NH // 2)

        def parts_after(t):
            return sum(1 if turn_step(u)[0] == "k" else 2 for u in range(t + 1))

        def turn_parts(t):
            kind, i = turn_step(t)
            b = 4 + 2 * (t % 2)
            if kind == "k":
                return [(k_hi[:, i, :], k_lo[:, i, :], ps[:, b:b + 2, :].rearrange("p a c -> p (a c)"))]
            halves = (slice(0, HD), slice(HD, P))
            return [(q_t[halves[odd], odd, i, :], q_t[halves[1 - odd], odd, i, :],
                     ps[halves[odd], b:b + 2, :].rearrange("p a c -> p (a c)")) for odd in range(2)]

        TILES_UP = 4 * (N_MERGE + N_MLP)
        TILES_DOWN = 16 * (N_MERGE + N_MLP)

        def used(n):
            l, u = divmod(n, UNITS)
            if u < U_GATE:
                return (proj_done, TB * (3 * l + u // 2 + 1)) if u % 2 else (first_half, 3 * l + u // 2 + 1)
            if u in (U_DFT, U_DFT + 1):
                return freq_done, 5 * l + (3, 5)[u - U_DFT]
            if u < U_MERGE:
                return gate_done, 4 * (N_GATE * l + u - U_GATE + 1 - (2 if u > U_DFT else 0))
            merge = u < U_MLP
            n_steps, first = (N_MERGE, U_MERGE) if merge else (N_MLP, U_MLP)
            for g in range(n_steps):
                if u - first == up_unit(g):
                    return (branch_done, 4 * (N_MERGE * l + g + 1)) if merge else (up_done, 4 * (N_MLP * l + g + 1))
                if u - first == down_unit(g, n_steps):
                    return down_done, l * TILES_DOWN + 16 * ((0 if merge else N_MERGE) + g + 1)

        @block.sync
        def _(sp):
            def load(src, slot):
                sp.dma_start(raw[:, slot, :].rearrange("p (a c) -> p a c", a=src.shape[1]), src).then_inc(raw_loaded[slot], 16)

            def w_proj(l, u):
                c, half = u // 2, u % 2
                col = (QW + KVW, 0, NT)[c]
                return t["w_in"][l].rearrange("(k p) n -> p k n", p=P)[:, half * 4:half * 4 + 4, col:col + NT]

            for tb in range(TB):
                sp.dma_start(x[:, tb, :], t["x"][0, tb * P:(tb + 1) * P, :]).then_inc(x_loaded[tb], 16)
                if tb == 0:
                    sp.dma_start(g_row[:], t["norm_mix"][0:1, :].to_broadcast([P, D])).then_inc(g_loaded, 16)
                    sp.dma_start(ident[:], t["c_ident"]).then_inc(ident_loaded, 16)
                if tb in (1, 5):
                    load(w_proj(0, tb // 4), tb // 4)
            sp.dma_start(dft64[:], t["c_dft64"].rearrange("p (a c) -> p a c", a=2)).then_inc(dft_loaded, 16)
            sp.dma_start(alt_col[:], t["c_altcol"]).then_inc(dft_loaded, 16)
            sp.dma_start(rope[:], t["c_rope"].rearrange("(b p) c f -> p b c f", p=P)).then_inc(consts_loaded, 16)
            for i, name in enumerate(("q_gain", "k_gain")):
                for l in range(DEPTH):
                    sp.dma_start(qk_gain[:, l, i, :], t[name][l:l + 1, :].to_broadcast([P, HD])).then_inc(consts_loaded, 16)
            for l in range(DEPTH):
                with nc.allow_non_contiguous_dma(reason="small"):
                    sp.dma_start(b_gate[:, l, :], t["b_gate"][l].rearrange("(f p) -> p f", p=P)).then_inc(consts_loaded, 16)

            for l in range(DEPTH):
                n0 = l * UNITS
                w_in = t["w_in"][l].rearrange("(k p) n -> p k n", p=P)
                for u in range(N_PROJ):
                    n = n0 + u
                    if u == 2 and l:
                        for tb in range(TB):
                            sp.wait_ge(added, l * TILES_DOWN - 14 + 2 * tb)
                            sp.dma_start(x_park[tb * P:(tb + 1) * P, :], x[:, tb, :]).then_inc(x_parked, 16)
                    if n >= 2:
                        sp.wait_ge(lo_split, n - 1)
                        load(w_proj(l, u), u % 2)
                for half in range(2):
                    with sp.Fori(0, N_GATE // 4) as i:
                        for s in range(2):
                            sp.wait_ge(lo_split, i * 2 + (n0 + gate_unit(half * (N_GATE // 2)) + s - 1))
                            load(w_in[:, :, bass.ds(i * (2 * CHUNK) + (QW + 2 * KVW + FW + (half * (N_GATE // 2) + s) * CHUNK), CHUNK)], s)
                    if half == 0:
                        for s, name in enumerate(("c_cos", "c_sin")):
                            sp.wait_ge(lo_split, n0 + U_DFT + s - 1)
                            load(t[name].rearrange("(k p) n -> p k n", p=P), s)
                        sp.wait_ge(rows_done, 5 * (l + 1))
                        sp.dma_start(alt_row, t["c_alt"].rearrange("a (b c) -> a b c", b=2)).then_inc(dft_loaded, 16)

                w_br = [t["w_attn_branch"][l].rearrange("(k p) n -> p k n", p=P),
                        t["w_fourier_branch"][l].rearrange("(k p) n -> p k n", p=P)]
                w_out = t["w_out"][l].rearrange("(k p) n -> p k n", p=P)
                gates_in = gates.rearrange("a f p n -> p a f n")
                order = [("up", 0)]
                for g in range(1, N_MERGE):
                    order += [("up", g), ("down", g - 1)]
                order += [("down", N_MERGE - 1)]
                for u, (kind, g) in enumerate(order):
                    n = n0 + U_MERGE + u
                    sp.wait_ge(lo_split, n - 1)
                    s = u % 2
                    if kind == "up":
                        sp.dma_start(raw[:, s, 0:6 * CHUNK].rearrange("p (a c) -> p a c", a=6),
                                     w_br[0][:, :, g * CHUNK:(g + 1) * CHUNK]).then_inc(raw_loaded[s], 16)
                        sp.dma_start(raw[:, s, 6 * CHUNK:].rearrange("p (a c) -> p a c", a=2),
                                     w_br[1][:, :, g * CHUNK:(g + 1) * CHUNK]).then_inc(raw_loaded[s], 16)
                        for gg in {0: (), 1: (0, 1)}.get(g, (g,)):
                            for i in range(4):
                                if gg == 0 and i == 0:
                                    sp.wait_ge(valued, N_TILES * (l + 1))
                                    for z in range(2):
                                        sp.wait_ge(gate_stored[z], 16 * 2 * N_GATE * (l + 1))
                                if gg:
                                    sp.wait_ge(u_lo_set, l * TILES_UP + 4 * (gg - 1) + i + 1)
                                sp.dma_start(gate_in[:, i, :, :],
                                             gates_in[:, :, 2 * gg + i // 2, (i % 2) * NT:(i % 2 + 1) * NT]).then_inc(gate_loaded[i], 16)
                    else:
                        load(w_out[:, 2 * g:2 * g + 2, :], s)
                    if u == 2:
                        sp.wait_ge(p_turned, 2 * N_ROWS * (l + 1))
                        sp.wait_ge(four_set, 4 * (l + 1))
                        for tb in range(TB):
                            src = t["x"][0, tb * P:(tb + 1) * P, :] if l == 0 else x_park[tb * P:(tb + 1) * P, :]
                            sp.dma_start(x[:, tb, :], src).then_inc(x_loaded[tb], 16)
                sp.wait_ge(*used(n0 + U_MLP - 2))
                sp.dma_start(g_row[:], t["norm_mlp"][l:l + 1, :].to_broadcast([P, D])).then_inc(g_loaded, 16)

                w_up = t["w_up"][l].rearrange("(k p) n -> p k n", p=P)
                w_down = t["w_down"][l].rearrange("(k p) n -> p k n", p=P)
                m0 = n0 + U_MLP
                sp.wait_ge(lo_split, m0 - 1)
                load(w_up[:, :, 0:CHUNK], 0)
                with sp.Fori(0, N_MLP // 2 - 1) as i:
                    for j, (kind, g) in enumerate((("up", 1), ("down", 0), ("up", 2), ("down", 1))):
                        sp.wait_ge(lo_split, i * 4 + (m0 + 1 + j - 1))
                        if kind == "up":
                            src = w_up[:, :, bass.ds(i * (2 * CHUNK) + g * CHUNK, CHUNK)]
                        else:
                            src = t["w_down"][l][bass.ds(i * (4 * P) + g * 2 * P, 2 * P), :].rearrange("(k p) n -> p k n", p=P)
                        load(src, (1 + j) % 2)
                g = N_MLP - 1
                for j, src in enumerate((w_up[:, :, g * CHUNK:(g + 1) * CHUNK], w_down[:, 2 * g - 2:2 * g, :],
                                         w_down[:, 2 * g:2 * g + 2, :])):
                    n = m0 + 2 * N_MLP - 3 + j
                    sp.wait_ge(lo_split, n - 1)
                    load(src, n % 2)
                sp.wait_ge(*used(n0 + UNITS - 2))
                last_gain = t["norm_mix"][l + 1:l + 2, :] if l + 1 < DEPTH else t["norm_final"].rearrange("(a d) -> a d", a=1)
                sp.dma_start(g_row[:], last_gain.to_broadcast([P, D])).then_inc(g_loaded, 16)
            for tb in range(TB):
                sp.wait_ge(h_ready, 2 * DEPTH * TB + tb + 1)
                sp.dma_start(out[0, tb * P:(tb + 1) * P, :], h_row[:, tb % 2, :]).then_inc(y_stored[tb % 2], 16)
            for z in range(2):
                sp.wait_ge(y_stored[z], 16 * TB // 2)
                sp.wait_ge(gate_stored[z], 16 * 2 * N_GATE * DEPTH)

        @block.tensor
        def _(pe):
            def three(o, stat, mov, start, stop):
                nc.tensor.matmul(o, stat[0], mov[0], start=start, stop=False)
                nc.tensor.matmul(o, stat[0], mov[1], start=False, stop=False)
                return nc.tensor.matmul(o, stat[1], mov[0], start=False, stop=stop)

            def turn_h(k, tb):
                pe.wait_ge(h_ready, TB * k + tb + 1)
                if k == 0 and tb == 0:
                    pe.wait_ge(ident_loaded, 16)
                for i in range(2):
                    if tb >= 2:
                        pe.wait_ge(ht_lo_set, 2 * (TB * k + tb - 2) + i + 1)
                    for j in range(4):
                        b = 4 * i + j
                        mm = nc.tensor.transpose(ps[:, 2 * (tb % 2) + i, j * P:(j + 1) * P],
                                                 h_row[:, tb % 2, b * P:(b + 1) * P], ident[:])
                    mm.then_inc(h_turned, 1)

            def project_tile(l, c, half, tb):
                bank = (tb + 4) % TB
                if half == 0 and c == 0:
                    if l and tb < 4:
                        pe.wait_ge(added, l * TILES_DOWN - 3 + tb)
                    pe.wait_ge(ht_lo_set, 2 * (2 * TB * l + tb + 1))
                    if tb >= 4:
                        pe.wait_ge(ht_lo_set, 2 * TB * (2 * l + 1) - (2 if tb < 6 else 0))
                elif half == 0:
                    pe.wait_ge(proj_kept, TB * (3 * l + c - 1) + tb + 1)
                for i in range(4):
                    kb = 4 * half + i
                    tok = slice(tb * P, (tb + 1) * P)
                    mm = three(ps[:, bank, :], (ht_hi[:, kb, tok], ht_lo[:, kb, tok]),
                               (w_hi[:, half, i * NT:(i + 1) * NT], w_lo[:, half, i * NT:(i + 1) * NT]),
                               kb == 0, kb == KB - 1)
                if half == 1:
                    mm.then_inc(proj_done, 1)
                elif tb == TB - 1:
                    mm.then_inc(first_half, 1)

            def project(l):
                for c in range(3):
                    for half in range(2):
                        if (c, half) != (0, 0):
                            pe.wait_ge(lo_split, l * UNITS + 2 * c + half + 1)
                        for tb in range(0 if (c, half) != (0, 0) else 4, TB):
                            project_tile(l, c, half, tb)

            def gate_unit_tiles(l, j):
                slot = j % 2
                pe.wait_ge(lo_split, l * UNITS + gate_unit(j) + 1)
                for i in range(4):
                    fb, th = i // 2, i % 2
                    if j == 0:
                        pe.wait_ge(proj_kept, TB * (3 * l + 2) + 4 + i + 1)
                    else:
                        pe.wait_ge(gate_made, 4 * (N_GATE * l + j - 1) + i + 1)
                    for kb in range(KB):
                        w = slice(kb * CHUNK + fb * P, kb * CHUNK + (fb + 1) * P)
                        tok = slice(th * NT, (th + 1) * NT)
                        mm = three(ps[:, i, :], (w_hi[:, slot, w], w_lo[:, slot, w]),
                                   (ht_hi[:, kb, tok], ht_lo[:, kb, tok]), kb == 0, kb == KB - 1)
                    mm.then_inc(gate_done, 1)

            def gate_stage(l):
                fourier_turn(l)
                gate_unit_tiles(l, 0)
                gate_unit_tiles(l, 1)
                fourier_rows(l)
                gate_unit_tiles(l, 2)
                gate_unit_tiles(l, 3)
                fourier_freq(l)
                for j in range(4, N_GATE - 1):
                    gate_unit_tiles(l, j)
                last_gate(l)

            def turn(l, t):
                if t == 0:
                    pe.wait_ge(k_doubled, TB * (l + 1))
                    pe.wait_ge(f_made, l + 1)
                if t >= 2:
                    pe.wait_ge(turn_dve, TURN_PARTS * l + parts_after(t - 2))
                kind, h = turn_step(t)
                for tb in range(TB):
                    src = k_twice[tb // 4][:, tb % 4, h, :] if kind == "k" else qk[:, tb, h * P:(h + 1) * P]
                    mm = nc.tensor.transpose(ps[:, 4 + 2 * (t % 2) + tb // 4, tb % 4 * P:(tb % 4 + 1) * P], src, ident[:])
                mm.then_inc(turned, 1)

            def last_gate(l):
                slot = (N_GATE - 1) % 2
                g0 = 4 * (N_GATE * (l + 1) - 1)
                turn(l, 0)
                turn(l, 1)
                pe.wait_ge(lo_split, l * UNITS + gate_unit(N_GATE - 1) + 1)

                def block_of(i, kb):
                    fb, th = i // 2, i % 2
                    w = slice(kb * CHUNK + fb * P, kb * CHUNK + (fb + 1) * P)
                    tok = slice(th * NT, (th + 1) * NT)
                    return three(ps[:, i, :], (w_hi[:, slot, w], w_lo[:, slot, w]),
                                 (ht_hi[:, kb, tok], ht_lo[:, kb, tok]), kb == 0, kb == KB - 1)

                for kb in range(NH // 2):
                    for i in range(4):
                        if kb == 0:
                            pe.wait_ge(gate_made, g0 - 4 + i + 1)
                        block_of(i, kb)
                    turn(l, 2 + kb)
                for i in range(4):
                    for kb in range(NH // 2, KB):
                        mm = block_of(i, kb)
                    mm.then_inc(gate_done, 1)

            def score(l, n):
                tile, qb = n // 2, n % 2
                pair, quarter, odd = tile // 8, tile // 2 % 4, tile % 2
                head = 2 * pair + odd
                tok = quarter * QB + qb * P
                if n >= 2:
                    pe.wait_ge(exped, N_ROWS * l + n - 1)
                for kh in range(2):
                    o = ps[:, 2 * (n % 2) + kh, :]
                    keys = slice(kh * NT, (kh + 1) * NT)
                    nc.tensor.matmul(o, q_t[:, odd, pair, tok:tok + P], k_hi[:, head // GROUP, keys], start=True, stop=False)
                    mm = nc.tensor.matmul(o, q_t[:, odd, pair, tok:tok + P], k_lo[:, head // GROUP, keys], start=False, stop=True)
                mm.then_inc(scored, 1)

            def turn_probs(l, n):
                pe.wait_ge(normed, N_ROWS * l + n + 1)
                for i in range(2):
                    k = 2 * n + i
                    if k >= 3:
                        pe.wait_ge(pt_lo_set, 2 * N_ROWS * l + k - 2)
                    for j in range(4):
                        kb = 4 * i + j
                        mm = nc.tensor.transpose(ps[:, 4 + k % 3, j * P:(j + 1) * P],
                                                 prob[:, n % 4, kb * P:(kb + 1) * P], ident[:])
                    mm.then_inc(p_turned, 1)

            def value(l, tile):
                head = 2 * (tile // 8) + tile % 2
                pe.wait_ge(pt_lo_set, 2 * N_ROWS * l + 4 * (tile + 1))
                if tile == 0:
                    pe.wait_ge(v_lo_set, TB * (l + 1))
                else:
                    pe.wait_ge(o_summed, N_TILES * l + tile)
                for kb in range(KB):
                    v = v_hl[:, kb, head // GROUP, :]
                    nc.tensor.matmul(ps[:, 7, 0:QB], v, pt_hi[:, tile % 2, kb, :], start=(kb == 0), stop=False)
                    mm = nc.tensor.matmul(ps[:, 7, 0:QB], v, pt_lo[:, tile % 2, kb, :], start=False, stop=(kb == KB - 1))
                mm.then_inc(valued, 1)

            def attend(l):
                pe.wait_ge(turn_dve, TURN_PARTS * l + parts_after(N_STEPS - 3))
                pe.wait_ge(gate_made, 4 * N_GATE * (l + 1) - 2)
                score(l, 0)
                pe.wait_ge(gate_made, 4 * N_GATE * (l + 1))
                score(l, 1)
                turn(l, N_STEPS - 2)
                turn(l, N_STEPS - 1)
                for n in range(N_ROWS + 1):
                    if n + 2 < N_ROWS:
                        score(l, n + 2)
                    if n in (1, 2):
                        pe.wait_ge(turn_dve, TURN_PARTS * (l + 1) + n - 2)
                    if n >= 1:
                        turn_probs(l, n - 1)
                        if n == N_ROWS:
                            pe.wait_ge(lo_split, l * UNITS + U_MERGE + 1)
                            pe.wait_ge(four_set, 4 * (l + 1))
                            pe.wait_ge(exped, N_ROWS * (l + 1))
                            branch_blocks(l, 0, 0, FOUR_BLOCKS)
                        if n % 2 == 0 and n >= 4:
                            value(l, n // 2 - 2)
                pe.wait_ge(o_split, N_TILES // 2 * (l + 1) - 4)
                branch_blocks(l, 0, 0, ATTN_BLOCKS[:-1])
                value(l, N_TILES - 1)
                branch_blocks(l, 0, 1, FOUR_BLOCKS + ATTN_BLOCKS[:-1])

            def fourier_turn(l):
                pe.wait_ge(proj_kept, TB * (3 * l + 2) + 4)
                for cb in range(2):
                    for i in range(2):
                        for j in range(4):
                            tb = 4 * i + j
                            mm = nc.tensor.transpose(ps[:, 4 + 2 * cb + i, j * P:(j + 1) * P],
                                                     f_rows[:, tb, cb * P:(cb + 1) * P], ident[:])
                        mm.then_inc(f_turned, 1)

            def fourier_rows(l):
                pe.wait_ge(dft_lo, 1)
                pe.wait_ge(fold_lo_set, l + 1)
                for cb in range(2):
                    o = ps[0:1, 7, cb * P:(cb + 1) * P]
                    nc.tensor.matmul(o, mid[:, cb:cb + 1], f32(dft64_hi[:, 0, :]), start=True, stop=False)
                    mm = nc.tensor.matmul(o, mid[:, cb:cb + 1], f32(dft64_lo[:, 0, :]), start=False, stop=True)
                mm.then_inc(rows_done, 1)
                for sb in range(4):
                    if sb == 3:
                        pe.wait_ge(gh_hi_set, 5 * l + 1)
                    for cs in range(2):
                        for cb in range(2):
                            pos = slice(sb * P, (sb + 1) * P)
                            c0 = (2 * cs + cb) * P
                            mm = three(ps[:, 4 + sb, c0:c0 + P], (fold_hi[:, cs, cb, pos], fold_lo[:, cs, cb, pos]),
                                       (dft64_hi[:, cs, :], dft64_lo[:, cs, :]), True, True)
                    mm.then_inc(rows_done, 1)

            def fourier_freq(l):
                n0 = l * UNITS + U_DFT
                pe.wait_ge(gh_lo_set, 4 * (l + 1))
                pe.wait_ge(dft_loaded, 32 + 16 * (l + 1))
                for cb in range(2):
                    o = ps[:, 6, 2 * cb:2 * cb + 2]
                    for sb in range(4):
                        nc.tensor.matmul(o, gh_hi[:, sb, 0, cb, :], alt_col_r[:], start=(sb == 0), stop=False)
                        nc.tensor.matmul(o, gh_lo[:, sb, 0, cb, :], alt_col_r[:], start=False, stop=False)
                    mm = nc.tensor.matmul(o, last_row[:, cb * P:(cb + 1) * P], alt_col[0:1, :], start=False, stop=True)
                mm.then_inc(freq_done, 1)
                for cs in range(2):
                    pe.wait_ge(lo_split, n0 + cs + 1)
                    if cs == 1:
                        pe.wait_ge(cosine_kept, 3 * l + 1)
                    for cb in range(2):
                        o = ps[:, 4 + 2 * cs + cb, :]
                        for sb in range(4):
                            tab = slice(sb * NT, (sb + 1) * NT)
                            mm = three(o, (gh_hi[:, sb, cs, cb, :], gh_lo[:, sb, cs, cb, :]),
                                       (w_hi[:, cs, tab], w_lo[:, cs, tab]), sb == 0, cs == 1 and sb == 3)
                        if cs == 0:
                            mm = nc.tensor.matmul(o.rearrange("p (b c) -> p b c", b=2), last_row[:, cb * P:(cb + 1) * P],
                                                  alt_row, start=False, stop=True)
                        mm.then_inc(freq_done, 1)

            ATTN_BLOCKS, FOUR_BLOCKS = list(range(NH // 2)), [6, 7]

            def branch_blocks(l, g, i, blocks):
                s = (l * UNITS + U_MERGE + up_unit(g)) % 2
                fb, th = i // 2, i % 2
                tok = slice(th * NT, (th + 1) * NT)
                for kb in blocks:
                    w = slice(kb * CHUNK + fb * P, kb * CHUNK + (fb + 1) * P)
                    if kb < 6:
                        mov = (q_t[:, 0, kb, tok], q_t[:, 1, kb, tok])
                    else:
                        mov = (four[:, 0, kb - 6, tok], four[:, 1, kb - 6, tok])
                    mm = three(ps[:, i % 2 + 2 * (kb >= 6), :], (w_hi[:, s, w], w_lo[:, s, w]), mov,
                               kb in (0, 6), kb in (5, 7))
                return mm

            def branch(l, g):
                pe.wait_ge(lo_split, l * UNITS + U_MERGE + up_unit(g) + 1)
                for i in range(4):
                    if g or i >= 2:
                        pe.wait_ge(branch_used, l * 4 * N_MERGE + 4 * g + i - 1)
                    if g == 0 and i < 2:
                        pe.wait_ge(o_split, N_TILES // 2 * (l + 1))
                        mm = branch_blocks(l, g, i, ATTN_BLOCKS[-1:])
                    else:
                        mm = branch_blocks(l, g, i, FOUR_BLOCKS + ATTN_BLOCKS)
                    mm.then_inc(branch_done, 1)

            def up(slot, read):
                for i in range(4):
                    fb, th = i // 2, i % 2
                    pe.wait_ge(relu_set, read(i))
                    for kb in range(KB):
                        w = slice(kb * CHUNK + fb * P, kb * CHUNK + (fb + 1) * P)
                        tok = slice(th * NT, (th + 1) * NT)
                        mm = three(ps[:, i, :], (w_hi[:, slot, w], w_lo[:, slot, w]),
                                   (ht_hi[:, kb, tok], ht_lo[:, kb, tok]), kb == 0, kb == KB - 1)
                    mm.then_inc(up_done, 1)

            def down(slot, par, read, after=None):
                for tb in range(TB):
                    for nh in range(2):
                        i = 2 * tb + nh
                        if read(i) is not None:
                            pe.wait_ge(added, read(i))
                        for j in range(2):
                            tok = slice(tb * P, (tb + 1) * P)
                            w = slice(j * D + nh * NT, j * D + (nh + 1) * NT)
                            mm = three(ps[:, 4 + i % 4, :], (u_hi[:, 2 * par + j, tok], u_lo[:, 2 * par + j, tok]),
                                       (w_hi[:, slot, w], w_lo[:, slot, w]), j == 0, j == 1)
                        mm.then_inc(down_done, 1)
                    if after:
                        after(tb)

            def norm_turns(k):
                def after(tb):
                    if tb >= 3:
                        turn_h(k, tb - 3)
                return after

            for l in range(DEPTH):
                if l == 0:
                    turn_h(0, 0)
                    turn_h(0, 1)
                for tb in range(4):
                    for block in ((2,), (3,), (4,), (5, 6))[tb] if l == 0 else ((), (5,), (6,), (7,))[tb]:
                        turn_h(2 * l, block)
                    if tb == 0:
                        pe.wait_ge(lo_split, l * UNITS + 1)
                    project_tile(l, 0, 0, tb)
                if l == 0:
                    turn_h(0, 7)
                project(l)
                gate_stage(l)
                attend(l)
                n0 = l * UNITS + U_MERGE
                d0 = l * TILES_DOWN
                u0 = l * TILES_UP

                def merge_down(g, after=None):
                    n = n0 + down_unit(g, N_MERGE)
                    pe.wait_ge(lo_split, n + 1)
                    pe.wait_ge(u_lo_set, u0 + 4 * (g + 1))
                    down(n % 2, g % 2,
                         lambda i: d0 + 16 * g + i - 3 if g or i >= 4 else None, after)

                pe.wait_ge(pt_lo_set, 2 * N_ROWS * (l + 1))
                branch(l, 0)
                for g in range(1, N_MERGE):
                    branch(l, g)
                    merge_down(g - 1)
                merge_down(N_MERGE - 1, norm_turns(2 * l + 1))
                n0 = l * UNITS + U_MLP
                d0 += 16 * N_MERGE
                u0 += 4 * N_MERGE
                r0 = l * 4 * N_MLP

                def mlp_down(g, after=None):
                    n = n0 + down_unit(g, N_MLP)
                    pe.wait_ge(lo_split, n + 1)
                    pe.wait_ge(u_lo_set, u0 + 4 * (g + 1))
                    down(n % 2, g % 2, lambda i: d0 + 16 * g + i - 3, after)

                pe.wait_ge(lo_split, n0 + 1)
                for i in range(4):
                    th, fb = i // 2, i % 2
                    if i == 1:
                        turn_h(2 * l + 1, 6)
                        turn_h(2 * l + 1, 7)
                    if i == 0:
                        pe.wait_ge(ht_lo_set, 2 * TB * (2 * l + 1) + 8)
                    if i == 2:
                        pe.wait_ge(ht_lo_set, 2 * TB * (2 * l + 2))
                    pe.wait_ge(added, d0 - 4 + i + 1)
                    for kb in range(KB):
                        if i == 0 and kb == KB // 2:
                            turn_h(2 * l + 1, 5)
                        w = slice(kb * CHUNK + fb * P, kb * CHUNK + (fb + 1) * P)
                        tok = slice(th * NT, (th + 1) * NT)
                        mm = three(ps[:, 4 + i, :], (w_hi[:, 0, w], w_lo[:, 0, w]),
                                   (ht_hi[:, kb, tok], ht_lo[:, kb, tok]), kb == 0, kb == KB - 1)
                    mm.then_inc(up_done, 1)
                with pe.Fori(0, N_MLP // 2 - 1) as it:
                    for j in range(2):
                        pe.wait_ge(lo_split, it * 4 + (n0 + 2 * j + 2))
                        up(1, lambda i: it * 8 + (r0 + 4 * j + i + 1))
                        pe.wait_ge(lo_split, it * 4 + (n0 + 2 * j + 3))
                        pe.wait_ge(u_lo_set, it * 8 + (u0 + 4 * j + 4))
                        down(0, j, lambda i: it * 32 + (d0 + 16 * j + i - 3))
                n = n0 + up_unit(N_MLP - 1)
                pe.wait_ge(lo_split, n + 1)
                up(n % 2, lambda i: r0 + 4 * (N_MLP - 2) + i + 1)
                mlp_down(N_MLP - 2)
                mlp_down(N_MLP - 1, norm_turns(2 * l + 2) if l + 1 < DEPTH else None)

        @block.scalar
        def _(act):
            merge_loads = [l * UNITS + U_MERGE + up_unit(g) for l in range(DEPTH) for g in range(N_MERGE)]

            def loads_to(n):
                return n // 2 + 1 + sum(1 for m in merge_loads if m <= n and (m - n) % 2 == 0)

            def split_hi(slot):
                nc.scalar.activation(w_hi[:, slot, :], raw[:, slot, :], ACT.Copy).then_inc(hi_split, 1)

            def split(n):
                act.wait_ge(raw_loaded[n % 2], 16 * loads_to(n))
                if n % UNITS == U_MERGE:
                    act.wait_ge(scored, N_ROWS * (n // UNITS) + N_ROWS // 2)
                elif n % UNITS == U_MERGE + 1:
                    act.wait_ge(scored, N_ROWS * (n // UNITS + 1))
                elif n >= 2:
                    act.wait_ge(*used(n - 2))
                split_hi(n % 2)

            def norm_sums(k, tb):
                if k == 0:
                    act.wait_ge(x_loaded[tb], 16)
                else:
                    act.wait_ge(added, (k - 1) // 2 * TILES_DOWN + 16 * (N_MERGE if k % 2 else N_MERGE + N_MLP) - 14 + 2 * tb)
                if tb == 0:
                    act.wait_ge(g_loaded, 16 * (k + 1))
                if k >= 1:
                    act.wait_ge(h_ready, TB * (k - 1) + tb + 1)
                nc.scalar.activation(junk[:], x[:, tb, :], ACT.Square,
                                     accum_out=rstd[:, 0, tb:tb + 1]).then_inc(sq_summed, 1)
                act.wait_ge(sq_summed, TB * k + tb + 1)
                nc.scalar.activation(rstd[:, 1, tb:tb + 1], rstd[:, 0, tb:tb + 1], ACT.Sqrt,
                                     bias=eps[:], scale=1.0 / D).then_inc(sd_ready, 1)

            def keep_hi(k, tb):
                for i in range(2):
                    act.wait_ge(h_turned, 2 * (TB * k + tb) + i + 1)
                    nc.scalar.activation(ht_hi[:, 4 * i:4 * i + 4, tb * P:(tb + 1) * P],
                                         ps[:, 2 * (tb % 2) + i, :].rearrange("p (a c) -> p a c", a=4),
                                         ACT.Copy).then_inc(ht_hi_set, 1)

            def norm(k, units):
                lag = 4 if k else 2
                for s in range(TB + 4):
                    if k and lag <= s < TB + lag and k < 2 * DEPTH:
                        keep_hi(k, s - lag)
                    if s < TB:
                        norm_sums(k, s)
                    if not k and lag <= s < TB + lag:
                        keep_hi(k, s - lag)
                    if s in units:
                        split(units[s])

            act.wait_ge(eps_set, 1)
            norm(0, {2: 0, 5: 1})
            for l in range(DEPTH):
                n0 = l * UNITS
                for c in range(3):
                    split(n0 + 2 * c + 2)
                    if c == 1 and l == 0:
                        act.wait_ge(dft_loaded, 32)
                        nc.scalar.activation(dft64_hi[:], dft64[:], ACT.Copy).then_inc(dft_hi, 1)
                        nc.scalar.activation(alt_col_r[:], alt_col[:], ACT.Copy).then_inc(dft_hi, 1)
                        act.wait_ge(dft_lo, 1)
                        act.wait_ge(consts_loaded, 16 * 7)
                    for tb in range(TB):
                        act.wait_ge(proj_done, TB * (3 * l + c) + tb + 1)
                        if c == 0:
                            if l and tb == 0:
                                act.wait_ge(x_parked, 16 * TB * l)
                            nc.scalar.activation(v_rows[:, tb], ps[:, (tb + 4) % TB, 0:KVW].rearrange("p (k c) -> p k c", k=NKV),
                                                 ACT.Copy)
                            dst, src = f_rows[:, tb, :], ps[:, (tb + 4) % TB, KVW:]
                        else:
                            dst, src = qk[:, tb, (c - 1) * NT:c * NT], ps[:, (tb + 4) % TB, :]
                        nc.scalar.activation(dst, src, ACT.Copy).then_inc(proj_kept, 1)
                    split(n0 + 2 * c + 3)
                act.wait_ge(qk_summed, 2 * TB * (l + 1))
                nc.scalar.activation(qk_stat[:, 1, :], qk_stat[:, 0, :], ACT.Sqrt, bias=eps[:],
                                     scale=1.0 / HD).then_inc(qk_sd, 1)

                for i in range(4):
                    act.wait_ge(f_turned, 4 * l + i + 1)
                    nc.scalar.activation(f_t[:, i // 2, (i % 2) * NT:(i % 2 + 1) * NT], ps[:, 4 + i, :],
                                         ACT.Copy).then_inc(f_kept, 1)
                act.wait_ge(folded, l + 1)
                nc.scalar.activation(fold_hi[:], fold[:], ACT.Copy).then_inc(fold_hi_set, 1)

                gates_out = gates.rearrange("a f p n -> p (a f) n")
                def turn_hi(t):
                    act.wait_ge(turned, N_STEPS * l + t + 1)
                    for hi, lo, src in turn_parts(t):
                        nc.scalar.activation(hi, src, ACT.Copy).then_inc(turn_act, 1)

                for j in range(N_GATE):
                    if j == N_GATE - 1:
                        for step in range(N_STEPS - 2):
                            turn_hi(step)
                    for i in range(4):
                        k = 4 * (N_GATE * l + j) + i
                        fb = 2 * j + i // 2
                        act.wait_ge(gate_done, k + 1)
                        slot = i if j == N_GATE - 1 else i % 2
                        if k >= 2 and slot < 2:
                            act.wait_ge(gate_stored[i % 2], 16 * (k // 2))
                        nc.scalar.activation(gate_out[:, slot, :], ps[:, i, :], ACT.Sigmoid,
                                             bias=b_gate[:, l, fb:fb + 1]).then_inc(gate_made, 1)
                        act.wait_ge(gate_made, k + 1)
                        act.dma_start(gates_out[:, fb:fb + 1, (i % 2) * NT:(i % 2 + 1) * NT],
                                      gate_out[:, slot:slot + 1, :]).then_inc(gate_stored[i % 2], 16)
                    if j < N_GATE - 2:
                        split(n0 + gate_unit(j) + 2)
                    if j == 1:
                        act.wait_ge(rows_done, 5 * l + 1)
                        nc.scalar.activation(last_row, ps[0:1, 7, 0:2 * P], ACT.Copy).then_inc(gh_hi_set, 1)
                        for sb in range(4):
                            act.wait_ge(rows_done, 5 * l + sb + 2)
                            nc.scalar.activation(gh_hi[:, sb].rearrange("p a b c -> p (a b c)"), ps[:, 4 + sb, :],
                                                 ACT.Copy).then_inc(gh_hi_set, 1)
                    if j == 3:
                        act.wait_ge(freq_done, 5 * l + 1)
                        nc.scalar.activation(mid_out[:], ps[:, 6, 0:4:2], ACT.Copy).then_inc(cosine_kept, 1)
                        split(n0 + U_DFT + 2)
                        for cb in range(2):
                            act.wait_ge(freq_done, 5 * l + cb + 2)
                            nc.scalar.activation(cosine[:, cb, :], ps[:, 4 + cb, :], ACT.Copy).then_inc(cosine_kept, 1)
                        split(n0 + U_DFT + 3)

                def exp(n):
                    act.wait_ge(topped, N_ROWS * l + n + 1)
                    if n >= 4:
                        act.wait_ge(p_turned, 2 * (N_ROWS * l + n - 3))
                    nc.scalar.activation(prob[:, n % 4, :], ps[:, 2 * (n % 2):2 * (n % 2) + 2, :].rearrange("p a c -> p (a c)"),
                                         ACT.Exp, bias=top[:, 0, n % 4:n % 4 + 1],
                                         accum_out=top[:, 1, n % 4:n % 4 + 1]).then_inc(exped, 1)

                exp(0)
                exp(1)
                turn_hi(N_STEPS - 2)
                exp(2)
                turn_hi(N_STEPS - 1)
                for n in range(N_ROWS + 1):
                    if 3 <= n + 1 < N_ROWS:
                        exp(n + 1)
                    if n == MERGE_STEPS[0]:
                        split(n0 + U_MERGE)
                    if n >= 1:
                        m = n - 1
                        tile, qb = m // 2, m % 2
                        if tile >= 2 and qb == 0:
                            act.wait_ge(valued, N_TILES * l + tile - 1)
                        for i in range(2):
                            k = 2 * m + i
                            act.wait_ge(p_turned, 2 * N_ROWS * l + k + 1)
                            nc.scalar.activation(pt_hi[:, tile % 2, 4 * i:4 * i + 4, qb * P:(qb + 1) * P],
                                                 ps[:, 4 + k % 3, :].rearrange("p (a c) -> p a c", a=4),
                                                 ACT.Copy).then_inc(pt_hi_set, 1)
                        if n % 2 == 0 and n >= 4:
                            tile = n // 2 - 2
                            act.wait_ge(valued, N_TILES * l + tile + 1)
                            if tile == 0:
                                for z in range(2):
                                    act.wait_ge(gate_stored[z], 16 * 2 * N_GATE * (l + 1))
                            if tile >= 2:
                                act.wait_ge(o_summed, N_TILES * l + tile - 1)
                            nc.scalar.activation(v_low[0:HD, tile % 2, :], ps[HD:P, 7, 0:QB], ACT.Copy).then_inc(v_low_set, 1)
                tile = N_TILES - 1
                act.wait_ge(valued, N_TILES * l + tile + 1)
                act.wait_ge(o_summed, N_TILES * l + tile - 1)
                nc.scalar.activation(v_low[0:HD, tile % 2, :], ps[HD:P, 7, 0:QB], ACT.Copy).then_inc(v_low_set, 1)

                split(n0 + U_MERGE + 1)

                u0 = l * TILES_UP

                def merge_hi(g):
                    for i in range(4):
                        k = l * 4 * N_MERGE + 4 * g + i
                        act.wait_ge(gated, k + 1)
                        if g >= 2 and i == 0:
                            act.wait_ge(*used(n0 + U_MERGE + down_unit(g - 2, N_MERGE)))
                        nc.scalar.activation(u_hi[:, 2 * (g % 2) + i // 2, (i % 2) * NT:(i % 2 + 1) * NT],
                                             gate_in[:, i, 0, :], ACT.Copy).then_inc(u_hi_set, 1)

                merge_hi(0)
                split(n0 + U_MERGE + 2)
                for g in range(1, N_MERGE):
                    merge_hi(g)
                    split(n0 + U_MERGE + up_unit(g) + 2)
                    if g < N_MERGE - 1:
                        split(n0 + U_MERGE + up_unit(g) + 3)
                norm(2 * l + 1, {2: n0 + U_MLP})
                split(n0 + U_MLP + 1)

                m0 = n0 + U_MLP
                r0 = l * 4 * N_MLP
                d0 = l * TILES_DOWN + 16 * N_MERGE

                def relu_tiles(par, val, fresh, used):
                    def hi(i):
                        act.wait_ge(squared, val(i))
                        if i == 0:
                            used()
                        fb, th = (i % 2, i // 2) if fresh else (i // 2, i % 2)
                        nc.scalar.activation(u_hi[:, 2 * par + fb, th * NT:(th + 1) * NT],
                                             squares[:, i % 2, :], ACT.Copy).then_inc(u_hi_set, 1)
                    for i in range(4):
                        act.wait_ge(up_done, val(i))
                        if not fresh or i >= 2:
                            act.wait_ge(squared, val(i - 2))
                        nc.scalar.activation(relu[:, i % 2, :], ps[:, 4 * fresh + i, :], ACT.Relu).then_inc(relu_set, 1)
                        if i:
                            hi(i - 1)
                    hi(3)

                relu_tiles(0, lambda i: r0 + i + 1, True, lambda: None)
                split(m0 + 2)
                with act.Fori(0, N_MLP // 2 - 1) as it:
                    for j in range(2):
                        relu_tiles((1 + j) % 2, lambda i: it * 8 + (r0 + 4 * (j + 1) + i + 1), False,
                                   lambda: act.wait_ge(down_done, it * 32 + (d0 + 16 * j)))
                        for s in (1, 0):
                            q = 2 * j + (3 if s else 4)
                            act.wait_ge(raw_loaded[s], it * 32 + 16 * loads_to(m0 + q))
                            if s:
                                act.wait_ge(up_done, it * 8 + (r0 + 4 * j + 8))
                            else:
                                act.wait_ge(down_done, it * 32 + (d0 + 16 * j + 16))
                            split_hi(s)
                g = N_MLP - 1
                relu_tiles(1, lambda i: r0 + 4 * g + i + 1, False,
                           lambda: act.wait_ge(*used(m0 + down_unit(g - 2, N_MLP))))
                split(m0 + 2 * N_MLP - 1)
                norm(2 * l + 2, {2: n0 + UNITS} if l + 1 < DEPTH else {})
                if l + 1 < DEPTH:
                    split(m0 + 2 * N_MLP + 1)

        @block.vector
        def _(dve):
            step = [0]

            def link(ins):
                step[0] += 1
                ins.then_inc(chain, 1)
                dve.wait_ge(chain, step[0])

            def newton(r, sd, sq, scale, tmp):
                link(nc.vector.tensor_scalar(tmp, sq, scale, EPS, ALU.mult, ALU.add))
                link(nc.vector.reciprocal(r, sd))
                link(nc.vector.tensor_tensor(tmp, tmp, r, ALU.mult))
                link(nc.vector.tensor_tensor(tmp, tmp, r, ALU.mult))
                link(nc.vector.tensor_scalar(tmp, tmp, -0.5, 1.5, ALU.mult, ALU.add))
                link(nc.vector.tensor_tensor(r, r, tmp, ALU.mult))

            def norm_inv(k, tb):
                dve.wait_ge(sd_ready, TB * k + tb + 1)
                nc.vector.reciprocal(rstd[:, 2, tb:tb + 1], rstd[:, 1, tb:tb + 1]).then_inc(inv_ready, 1)

            def norm_row(k, tb):
                dve.wait_ge(rstd_ready, TB * k + tb + 1)
                if tb == 0:
                    dve.wait_ge(g_loaded, 16 * (k + 1))
                if tb >= 2:
                    if k < 2 * DEPTH:
                        dve.wait_ge(h_turned, 2 * (TB * k + tb - 1))
                    else:
                        dve.wait_ge(y_stored[tb % 2], 16 * (tb // 2))
                nc.vector.scalar_tensor_tensor(out=h_row[:, tb % 2, :], in0=x[:, tb, :], scalar=rstd[:, 2, tb:tb + 1],
                                               in1=g_row[:], op0=ALU.mult, op1=ALU.mult).then_inc(h_ready, 1)

            def keep_lo(k, tb):
                for i in range(2):
                    dve.wait_ge(ht_hi_set, 2 * (TB * k + tb) + i + 1)
                    hi = ht_hi[:, 4 * i:4 * i + 4, tb * P:(tb + 1) * P]
                    nc.vector.tensor_tensor(ht_lo[:, 4 * i:4 * i + 4, tb * P:(tb + 1) * P],
                                            ps[:, 2 * (tb % 2) + i, :].rearrange("p (a c) -> p a c", a=4),
                                            f32(hi), ALU.subtract).then_inc(ht_lo_set, 1)

            def norm(k, adds):
                for s in range(TB + 4):
                    if s == 7 and k < 2 * DEPTH:
                        keep_lo(k, 3)
                    if s < TB:
                        adds(s)
                    if 1 <= s <= TB:
                        norm_inv(k, s - 1)
                    if 2 <= s < TB + 2:
                        norm_row(k, s - 2)
                    if 4 <= s and s != 7 and k < 2 * DEPTH:
                        keep_lo(k, s - 4)

            def first_norm():
                norm_inv(0, 0)
                norm_row(0, 0)
                norm_inv(0, 1)
                norm_inv(0, 2)
                norm_row(0, 1)
                keep_lo(0, 0)
                norm_row(0, 2)
                dve.wait_ge(hi_split, 1)
                nc.vector.tensor_tensor(w_lo[:, 0, :], raw[:, 0, :], f32(w_hi[:, 0, :]), ALU.subtract).then_inc(lo_split, 1)
                for s in range(3, TB + 2):
                    if s < TB:
                        norm_inv(0, s)
                    keep_lo(0, s - 2)
                    if s < TB:
                        norm_row(0, s)

            def add_tile(i, val, back=None):
                dve.wait_ge(down_done, val)
                if back:
                    dve.wait_ge(x_loaded[i // 2], back)
                xt = x[:, i // 2, (i % 2) * NT:(i % 2 + 1) * NT]
                nc.vector.tensor_tensor(xt, ps[:, 4 + i % 4, :], xt, ALU.add).then_inc(added, 1)

            nc.vector.memset(eps[:], EPS).then_inc(eps_set, 1)
            first_norm()
            dve.wait_ge(dft_hi, 1)
            nc.vector.tensor_tensor(dft64_lo[:], dft64[:], f32(dft64_hi[:]), ALU.subtract).then_inc(dft_lo, 1)
            dve.wait_ge(consts_loaded, 16 * 7)
            for l in range(DEPTH):
                link(nc.vector.tensor_scalar(qk_gain[:, l, 0, :], qk_gain[:, l, 0, :], HD ** -0.5, None, ALU.mult))
            for l in range(DEPTH):
                n0 = l * UNITS
                for c in (1, 2):
                    for tb in range(TB):
                        dve.wait_ge(proj_kept, TB * (3 * l + c) + tb + 1)
                        src = qk[:, tb, (c - 1) * NT:c * NT]
                        done = TB * (2 * l + c - 1) + tb
                        sq = rope_tmp[:, 0, :]
                        if done:
                            dve.wait_ge(qk_summed, done)
                        link(nc.vector.tensor_tensor(sq, src, src, ALU.mult))
                        nc.vector.tensor_reduce(qk_stat[:, 0, tb * 16 + 8 * (c - 1):tb * 16 + 8 * c],
                                                sq.rearrange("p (h c) -> p h c", h=8), AX.X,
                                                ALU.add).then_inc(qk_summed, 1)
                dve.wait_ge(f_kept, 4 * (l + 1))
                fwd, rev = f_t[:, :, 1:HALF], f_t[:, :, SEQ - 1:HALF:-1]
                nc.vector.tensor_tensor(fold[:, 0, :, 1:], fwd, rev, ALU.add)
                nc.vector.tensor_tensor(fold[:, 1, :, 1:], fwd, rev, ALU.subtract)
                nc.vector.tensor_copy(fold[:, 0, :, 0:1], f_t[:, :, 0:1])
                nc.vector.tensor_copy(mid[:].unsqueeze(2), f_t[:, :, HALF:HALF + 1])
                nc.vector.memset(fold[:, 1, :, 0:1], 0.0).then_inc(folded, 1)
                dve.wait_ge(fold_hi_set, l + 1)
                nc.vector.tensor_tensor(fold_lo[:], fold[:], f32(fold_hi[:]), ALU.subtract).then_inc(fold_lo_set, 1)

                dve.wait_ge(qk_sd, l + 1)
                r_all = qk_rstd[:].rearrange("p b h -> p (b h)")
                newton(r_all, qk_stat[:, 1, :], qk_stat[:, 0, :], 1.0 / HD, qk_stat[:, 2, :])
                t0, t1 = (rope_tmp[:, i, :].rearrange("p (h c) -> p h c", h=16) for i in range(2))
                for tb in range(TB):
                    row = qk[:, tb, :].rearrange("p (h c) -> p h c", h=16)
                    link(nc.vector.tensor_tensor(row, row, qk_rstd[:, tb, :].unsqueeze(2).to_broadcast([P, 16, HD]), ALU.mult))
                    for i, hs in enumerate((slice(0, NH), slice(NH, 16))):
                        g = qk_gain[:, l, i, :].unsqueeze(1).to_broadcast([P, hs.stop - hs.start, HD])
                        link(nc.vector.tensor_tensor(row[:, hs, :], row[:, hs, :], g, ALU.mult))
                    if tb:
                        dve.wait_ge(qk_ready, TB * l + tb)
                    x0, x1 = row[:, :, 0:HD:2], row[:, :, 1:HD:2]
                    c, s = (rope[:, tb, i, :].unsqueeze(1).to_broadcast([P, 16, 32]) for i in range(2))
                    nc.vector.tensor_tensor(t0, x0, s, ALU.mult)
                    link(nc.vector.tensor_tensor(t1, x1, s, ALU.mult))
                    link(nc.vector.tensor_tensor(x0, x0, c, ALU.mult))
                    link(nc.vector.tensor_tensor(x1, x1, c, ALU.mult))
                    nc.vector.tensor_tensor(x0, x0, t1, ALU.subtract)
                    nc.vector.tensor_tensor(x1, x1, t0, ALU.add).then_inc(qk_ready, 1)
                    if tb == 5:
                        for sb in range(4):
                            dve.wait_ge(gh_hi_set, 5 * l + sb + 2)
                            nc.vector.tensor_tensor(gh_lo[:, sb].rearrange("p a b c -> p (a b c)"), ps[:, 4 + sb, :],
                                                    f32(gh_hi[:, sb].rearrange("p a b c -> p (a b c)")),
                                                    ALU.subtract).then_inc(gh_lo_set, 1)
                dve.wait_ge(cosine_kept, 3 * (l + 1))
                dve.wait_ge(freq_done, 5 * (l + 1))
                nc.vector.tensor_copy(f_out[:, :, HALF:HALF + 1], mid_out[:].unsqueeze(2))
                for cb in range(2):
                    nc.vector.tensor_tensor(f_out[:, cb, 0:HALF], cosine[:, cb, :], ps[:, 6 + cb, :], ALU.subtract)
                    ins = nc.vector.tensor_tensor(f_out[:, cb, SEQ - 1:HALF:-1], cosine[:, cb, 1:HALF], ps[:, 6 + cb, 1:HALF], ALU.add)
                ins.then_inc(f_made, 1)

                def turn_lo(t):
                    for part, (hi, lo, src) in enumerate(turn_parts(t)):
                        dve.wait_ge(turn_act, TURN_PARTS * l + (parts_after(t - 1) if t else 0) + part + 1)
                        nc.vector.tensor_tensor(lo, src, f32(hi), ALU.subtract).then_inc(turn_dve, 1)

                for t in range(N_STEPS - 2):
                    turn_lo(t)

                def top_of(n):
                    dve.wait_ge(scored, N_ROWS * l + n + 1)
                    nc.vector.tensor_reduce(top[:, 0, n % 4:n % 4 + 1], ps[:, 2 * (n % 2):2 * (n % 2) + 2, :].rearrange("p a c -> p (a c)"),
                                            AX.X, ALU.max, negate=True).then_inc(topped, 1)

                def invert(n):
                    dve.wait_ge(exped, N_ROWS * l + n + 1)
                    nc.vector.reciprocal(top[:, 2, n % 4:n % 4 + 1], top[:, 1, n % 4:n % 4 + 1]).then_inc(inverted, 1)

                def add_low(tile):
                    odd = tile % 2
                    dve.wait_ge(v_low_set, N_TILES * l + tile + 1)
                    if tile >= 4:
                        dve.wait_ge(o_split, N_TILES // 2 * l + tile // 2 - 1)
                    nc.vector.tensor_tensor(o_sum[HD * odd:HD * odd + HD, tile // 2 % 2, :], ps[0:HD, 7, 0:QB],
                                            v_low[0:HD, tile % 2, :], ALU.add).then_inc(o_summed, 1)

                top_of(0)
                top_of(1)
                invert(0)
                top_of(2)
                invert(1)
                turn_lo(N_STEPS - 2)
                top_of(3)
                invert(2)
                turn_lo(N_STEPS - 1)
                for n in range(N_ROWS + 1):
                    if 4 <= n + 2 < N_ROWS:
                        top_of(n + 2)
                    if 3 <= n + 1 < N_ROWS:
                        invert(n + 1)
                    if n >= 1:
                        m = n - 1
                        tile, qb = m // 2, m % 2
                        for i in range(2):
                            k = 2 * m + i
                            dve.wait_ge(pt_hi_set, 2 * N_ROWS * l + k + 1)
                            sl = (slice(None), tile % 2, slice(4 * i, 4 * i + 4), slice(qb * P, (qb + 1) * P))
                            nc.vector.tensor_tensor(pt_lo[sl], ps[:, 4 + k % 3, :].rearrange("p (a c) -> p a c", a=4),
                                                    f32(pt_hi[sl]), ALU.subtract).then_inc(pt_lo_set, 1)
                        if n % 2 == 0 and n >= 4:
                            add_low(n // 2 - 2)
                add_low(N_TILES - 1)

                k0 = l * 4 * N_MERGE
                d0 = l * TILES_DOWN

                def merge_tiles(g):
                    def lo(i):
                        dve.wait_ge(u_hi_set, l * TILES_UP + 4 * g + i + 1)
                        sl = (slice(None), 2 * (g % 2) + i // 2, slice((i % 2) * NT, (i % 2 + 1) * NT))
                        nc.vector.tensor_tensor(u_lo[sl], gate_in[:, i, 0, :], f32(u_hi[sl]), ALU.subtract).then_inc(u_lo_set, 1)
                    for i in range(4):
                        k = k0 + 4 * g + i
                        dve.wait_ge(branch_done, k + 1)
                        dve.wait_ge(gate_loaded[i], 16 * (l * N_MERGE + g + 1))
                        nc.vector.tensor_tensor(gate_in[:, i, 0, :], ps[:, i % 2, :], gate_in[:, i, 0, :], ALU.mult)
                        ins = nc.vector.tensor_tensor(gate_in[:, i, 1, :], ps[:, 2 + i % 2, :], gate_in[:, i, 1, :], ALU.mult)
                        ins.then_inc(branch_used, 1)
                        dve.wait_ge(branch_used, k + 1)
                        nc.vector.tensor_tensor(gate_in[:, i, 0, :], gate_in[:, i, 0, :], gate_in[:, i, 1, :], ALU.add).then_inc(gated, 1)
                        if i:
                            lo(i - 1)
                    lo(3)

                merge_tiles(0)
                for g in range(1, N_MERGE):
                    merge_tiles(g)
                    for i in range(16):
                        add_tile(i, d0 + 16 * (g - 1) + i + 1, 16 * (l + 2) if g == 1 else None)

                def last_adds(base):
                    def adds(tb):
                        add_tile(2 * tb, base + 2 * tb + 1)
                        add_tile(2 * tb + 1, base + 2 * tb + 2)
                    return adds

                norm(2 * l + 1, last_adds(d0 + 16 * (N_MERGE - 1)))

                d0 += 16 * N_MERGE
                u0 = l * TILES_UP + 4 * N_MERGE
                r0 = l * 4 * N_MLP

                def square_tiles(par, r, u, fresh=False):
                    def lo(i):
                        dve.wait_ge(u_hi_set, u(i))
                        fb, th = (i % 2, i // 2) if fresh else (i // 2, i % 2)
                        sl = (slice(None), 2 * par + fb, slice(th * NT, (th + 1) * NT))
                        nc.vector.tensor_tensor(u_lo[sl], squares[:, i % 2, :], f32(u_hi[sl]), ALU.subtract).then_inc(u_lo_set, 1)
                    for i in range(4):
                        dve.wait_ge(relu_set, r(i))
                        dve.wait_ge(u_lo_set, u(i) - 2)
                        nc.vector.tensor_tensor(squares[:, i % 2, :], relu[:, i % 2, :], relu[:, i % 2, :], ALU.mult).then_inc(squared, 1)
                        if i:
                            lo(i - 1)
                    lo(3)

                square_tiles(0, lambda i: r0 + i + 1, lambda i: u0 + i + 1, True)
                with dve.Fori(0, N_MLP // 2 - 1) as it:
                    for j in range(2):
                        square_tiles((1 + j) % 2, lambda i: it * 8 + (r0 + 4 * (j + 1) + i + 1),
                                     lambda i: it * 8 + (u0 + 4 * (j + 1) + i + 1))
                        for i in range(16):
                            add_tile(i, it * 32 + (d0 + 16 * j + i + 1))
                g = N_MLP - 1
                square_tiles(1, lambda i: r0 + 4 * g + i + 1, lambda i: u0 + 4 * g + i + 1)
                for i in range(16):
                    add_tile(i, d0 + 16 * (g - 1) + i + 1)
                norm(2 * l + 2, last_adds(d0 + 16 * g))

        @block.gpsimd
        def _(pool):
            def split_lo(slot):
                nc.gpsimd.tensor_tensor(w_lo[:, slot, :], raw[:, slot, :], f32(w_hi[:, slot, :]),
                                        ALU.subtract).then_inc(lo_split, 1)

            chain_len = [0]

            def link(ins):
                chain_len[0] += 1
                ins.then_inc(newton_step, 1)
                pool.wait_ge(newton_step, chain_len[0])

            def newton(k, tb):
                r, t = rstd[:, 2, tb:tb + 1], rstd[:, 3, tb:tb + 1]
                pool.wait_ge(inv_ready, TB * k + tb + 1)
                link(nc.gpsimd.tensor_scalar(t, rstd[:, 0, tb:tb + 1], 1.0 / D, EPS, ALU.mult, ALU.add))
                link(nc.gpsimd.tensor_tensor(t, t, r, ALU.mult))
                link(nc.gpsimd.tensor_tensor(t, t, r, ALU.mult))
                link(nc.gpsimd.tensor_scalar(t, t, -0.5, 1.5, ALU.mult, ALU.add))
                nc.gpsimd.tensor_tensor(r, r, t, ALU.mult).then_inc(rstd_ready, 1)

            def split_half(n, half):
                if half == 0:
                    pool.wait_ge(hi_split, n + 1)
                part = slice(half * UNIT // 2, (half + 1) * UNIT // 2)
                ins = nc.gpsimd.tensor_tensor(w_lo[:, n % 2, part], raw[:, n % 2, part], f32(w_hi[:, n % 2, part]),
                                              ALU.subtract)
                if half == 1:
                    ins.then_inc(lo_split, 1)

            def newtons(k, unit=None):
                for tb in range(TB):
                    newton(k, tb)
                    if unit is not None and tb in (2, 3):
                        split_half(unit, tb - 2)

            def v_split(tb):
                pool.wait_ge(proj_kept, TB * 3 * l + tb + 1)
                hi, lo = v_hl[:, tb, :, 0:HD], v_hl[:, tb, :, HD:P]
                nc.gpsimd.tensor_copy(hi, v_rows[:, tb]).then_inc(v_hi_set, 1)
                pool.wait_ge(v_hi_set, TB * l + tb + 1)
                nc.gpsimd.tensor_tensor(lo, v_rows[:, tb], f32(hi), ALU.subtract).then_inc(v_lo_set, 1)

            def split_one(n):
                pool.wait_ge(hi_split, n + 1)
                split_lo(n % 2)

            for l in range(DEPTH):
                n0 = l * UNITS
                if l == 0:
                    for tb in range(TB):
                        newton(0, tb)
                    pool.wait_ge(lo_split, 1)
                    split_one(1)
                with pool.Fori(1, U_MERGE // 2 - 1) as it:
                    for s in range(2):
                        pool.wait_ge(hi_split, it * 2 + (n0 + s + 1))
                        split_lo(s)

                pool.wait_ge(freq_done, 5 * (l + 1))
                for tb in range(TB):
                    pool.wait_ge(qk_ready, TB * l + tb + 1)
                    nc.gpsimd.tensor_copy(k_twice[tb // 4][:, tb % 4].rearrange("p k (d c) -> p k d c", d=2),
                                          qk[:, tb, QW:].rearrange("p (k c) -> p k c", k=NKV).unsqueeze(2).to_broadcast([P, NKV, 2, HD])).then_inc(k_doubled, 1)
                    if tb % 4 == 3:
                        split_one(n0 + U_MERGE - 2 + tb // 4)
                for tb in range(TB):
                    v_split(tb)

                def split_out(both):
                    pair, quarter = both // 4, both % 4
                    tok = slice(quarter * QB, (quarter + 1) * QB)
                    done = N_TILES // 2 * l + both + 1
                    pool.wait_ge(o_summed, 2 * done)
                    nc.gpsimd.tensor_copy(q_t[:, 0, pair, tok], o_sum[:, both % 2, :]).then_inc(o_hi_set, 1)
                    pool.wait_ge(o_hi_set, done)
                    nc.gpsimd.tensor_tensor(q_t[:, 1, pair, tok], o_sum[:, both % 2, :],
                                            f32(q_t[:, 0, pair, tok]), ALU.subtract).then_inc(o_split, 1)

                for n in range(N_ROWS):
                    pool.wait_ge(inverted, N_ROWS * l + n + 1)
                    nc.gpsimd.tensor_scalar(prob[:, n % 4, :], prob[:, n % 4, :], top[:, 2, n % 4:n % 4 + 1], 1.0,
                                            ALU.mult, ALU.mult).then_inc(normed, 1)
                    if n % 4 == 3 and n >= 7:
                        split_out(n // 4 - 1)
                    if n in MERGE_STEPS[1:]:
                        split_half(n0 + U_MERGE, MERGE_STEPS.index(n) - 1)
                    if n in FOUR_STEPS:
                        q = FOUR_STEPS.index(n)
                        cb, tok = q // 2, slice((q % 2) * NT, (q % 2 + 1) * NT)
                        nc.gpsimd.tensor_copy(four[:, 0, cb, tok], f_out[:, cb, tok]).then_inc(four_hi_set, 1)
                        pool.wait_ge(four_hi_set, 4 * l + q + 1)
                        nc.gpsimd.tensor_tensor(four[:, 1, cb, tok], f_out[:, cb, tok], f32(four[:, 0, cb, tok]),
                                                ALU.subtract).then_inc(four_set, 1)
                split_out(N_TILES // 2 - 1)
                for u in range(1, 2 * N_MERGE):
                    split_one(n0 + U_MERGE + u)
                newtons(2 * l + 1, n0 + U_MLP)
                with pool.Fori(0, N_MLP - 1) as it:
                    for s in (1, 0):
                        pool.wait_ge(hi_split, it * 2 + (n0 + U_MLP + (2 if s else 3)))
                        split_lo(s)
                split_one(n0 + UNITS - 1)
                newtons(2 * l + 2, n0 + UNITS if l + 1 < DEPTH else None)
                if l + 1 < DEPTH:
                    split_one(n0 + UNITS + 1)


def tables():
    pairs = HD // 4
    inv = np.float32(10000.0) ** (-np.arange(pairs, dtype=np.float32) / np.float32(pairs))
    pos = np.arange(SEQ)
    ang = np.concatenate([(pos // 64).astype(np.float32)[:, None] * inv, (pos % 64).astype(np.float32)[:, None] * inv], -1)
    rope = np.stack([np.cos(ang), np.sin(ang)], 1).astype(np.float32)
    scale = 1.0 / np.sqrt(SEQ * 64.0)
    sk = np.outer(np.arange(HALF), np.arange(HALF)) % SEQ * (2 * np.pi / SEQ)
    cc = np.outer(np.arange(64), np.arange(64)) % 64 * (2 * np.pi / 64)
    two = np.eye(2)
    return {
        "c_ident": np.eye(P, dtype=np.float32),
        "c_rope": rope,
        "c_cos": (np.cos(sk) * scale).astype(np.float32),
        "c_sin": (np.sin(sk) * scale).astype(np.float32),
        "c_dft64": np.concatenate([np.kron(two, np.cos(cc)), np.kron(two, np.sin(cc))], 1).astype(np.float32),
        "c_alt": (scale * (1.0 - 2.0 * (np.arange(NT) % 2)))[None].astype(np.float32),
        "c_altcol": (scale * (1.0 - 2.0 * (np.arange(P) % 2)))[:, None].repeat(2, 1).astype(np.float32),
    }


def kernel(**inputs):
    import concourse.bacc as bacc
    from concourse.bass_utils import run_bass_kernel_spmd

    nc = bacc.Bacc("TRN2", target_bir_lowering=False, num_devices=1)
    arrays, args = {}, {}
    for name, a in {**inputs, **tables()}.items():
        a = np.ascontiguousarray(a)
        arrays[f"in_{name}"] = a
        args[name] = nc.dram_tensor(f"in_{name}", a.shape, mybir.dt.from_np(a.dtype), kind="ExternalInput").ap()
    out = nc.dram_tensor("out_0", (1, SEQ, D), F32, kind="ExternalOutput").ap()
    build(nc, args, out)
    r = run_bass_kernel_spmd(nc, [arrays], core_ids=[0])
    return r.results[0]["out_0"]
```
